# Optimizing a Trainium2 kernel written in Bass

```python
import jax, jax.numpy as jnp
from jax import lax
import numpy as np

D_MODEL = 1024
BATCH = 1
SEQ = 512
DEPTH = 1

N_Q_HEADS = 16
N_KV_HEADS = 4
HEAD_DIM = 64
WINDOW = 128
ATTN_BLOCK = WINDOW
SSD_EXPAND = 2
D_INNER = SSD_EXPAND * D_MODEL
SSD_HEAD_DIM = 64
N_SSD_HEADS = D_INNER // SSD_HEAD_DIM
N_SSD_GROUPS = 4
D_STATE = 128
SSD_CONV = 4
CHUNK = 128
D_FF = 2816
FFN_CONV = 3
EPS = 1e-5
NEG = -1e30

Q_DIM = N_Q_HEADS * HEAD_DIM
KV_DIM = N_KV_HEADS * HEAD_DIM
BC_DIM = N_SSD_GROUPS * D_STATE
XBC_DIM = D_INNER + 2 * BC_DIM
IN_SPLITS = (Q_DIM, KV_DIM, KV_DIM, D_INNER, XBC_DIM, N_SSD_HEADS, D_MODEL, D_MODEL)
IN_DIM = sum(IN_SPLITS)

kernel_name = "hybrid_swa_sink_ssd_convffn"

def _split(t, sizes):
    idx = np.cumsum(np.array(sizes))[:-1].tolist()
    return jnp.split(t, idx, axis=-1)

def rmsnorm(x, w):
    xf = x.astype(jnp.float32)
    y = xf * lax.rsqrt(jnp.mean(xf * xf, axis=-1, keepdims=True) + EPS)
    return (y * w.astype(jnp.float32)).astype(x.dtype)

def causal_dwconv(x, w, b):
    K = w.shape[0]
    S = x.shape[1]
    xp = jnp.pad(x, ((0, 0), (K - 1, 0), (0, 0)))
    y = xp[:, 0:S] * w[0]
    for k in range(1, K):
        y = y + xp[:, k:k + S] * w[k]
    return y + b

def banded_sink_attention(q, k, v, sinks):
    Bsz, S, _ = q.shape
    W = ATTN_BLOCK
    nb = S // W
    G = N_Q_HEADS // N_KV_HEADS
    qb = q.reshape(Bsz, nb, W, N_KV_HEADS, G, HEAD_DIM)

    def band(t):
        t = t.reshape(Bsz, S, N_KV_HEADS, HEAD_DIM)
        tp = jnp.pad(t, ((0, 0), (W, 0), (0, 0), (0, 0)))
        prev = tp[:, :S].reshape(Bsz, nb, W, N_KV_HEADS, HEAD_DIM)
        cur = t.reshape(Bsz, nb, W, N_KV_HEADS, HEAD_DIM)
        return jnp.concatenate([prev, cur], axis=2)

    kb, vb = band(k), band(v)
    scores = jnp.einsum('bnqhgd,bnshd->bnhgqs', qb, kb).astype(jnp.float32) * (HEAD_DIM ** -0.5)
    qi = jnp.arange(W)[:, None]
    si = jnp.arange(2 * W)[None, :]
    dist = W + qi - si
    kpos = jnp.arange(nb)[:, None, None] * W - W + si[None]
    valid = (dist >= 0)[None] & (dist < WINDOW)[None] & (kpos >= 0)
    valid = valid[None, :, None, None]
    scores = jnp.where(valid, scores, NEG)
    sink = sinks.astype(jnp.float32).reshape(N_KV_HEADS, G)[None, None, :, :, None]
    m = jnp.maximum(scores.max(axis=-1), sink)
    p = jnp.where(valid, jnp.exp(scores - m[..., None]), 0.0)
    denom = p.sum(axis=-1) + jnp.exp(sink - m)
    probs = (p / denom[..., None]).astype(v.dtype)
    out = jnp.einsum('bnhgqs,bnshd->bnqhgd', probs, vb)
    return out.reshape(Bsz, S, Q_DIM)

def ssd_chunked(xs, dt, a_log, bmat, cmat, d_skip):
    Bsz, S, H, P = xs.shape
    G, N = bmat.shape[2], bmat.shape[3]
    J = H // G
    L = CHUNK
    nc = S // L
    A = -jnp.exp(a_log.astype(jnp.float32))
    dA = (dt * A).reshape(Bsz, nc, L, G, J)
    xf = xs.astype(jnp.float32)
    xc = (xf * dt[..., None]).reshape(Bsz, nc, L, G, J, P)
    bc = bmat.astype(jnp.float32).reshape(Bsz, nc, L, G, N)
    cc = cmat.astype(jnp.float32).reshape(Bsz, nc, L, G, N)
    a_cs = jnp.cumsum(dA, axis=2)
    seg = a_cs[:, :, :, None] - a_cs[:, :, None, :]
    causal = jnp.tril(jnp.ones((L, L), dtype=bool))[:, :, None, None]
    decay = jnp.where(causal, jnp.exp(jnp.where(causal, seg, 0.0)), 0.0)
    cb = jnp.einsum('bclgn,bcsgn->bclsg', cc, bc)
    y_diag = jnp.einsum('bclsgj,bcsgjp->bclgjp', cb[..., None] * decay, xc)
    decay_states = jnp.exp(a_cs[:, :, -1:] - a_cs)
    states = jnp.einsum('bclgn,bclgjp->bcgjpn', bc, xc * decay_states[..., None])
    chunk_decay = jnp.exp(a_cs[:, :, -1])

    def step(h, inp):
        st, dec = inp
        h_new = h * dec[..., None, None] + st
        return h_new, h

    h0 = jnp.zeros((Bsz, G, J, P, N), jnp.float32)
    _, prev = lax.scan(step, h0, (jnp.swapaxes(states, 0, 1), jnp.swapaxes(chunk_decay, 0, 1)))
    prev = jnp.swapaxes(prev, 0, 1)
    y_off = jnp.einsum('bclgn,bcgjpn->bclgjp', cc, prev) * jnp.exp(a_cs)[..., None]
    y = (y_diag + y_off).reshape(Bsz, S, H, P)
    return y + xf * d_skip.astype(jnp.float32)[:, None]

def setup_inputs(seed: int = 0) -> dict:
    key = jax.random.key(seed)
    ks = jax.random.split(key, 24)
    f32 = jnp.float32
    nrm = lambda k, shape, scale: jax.random.normal(k, shape, f32) * scale
    dt0 = jnp.exp(jax.random.uniform(ks[9], (DEPTH, N_SSD_HEADS), f32,
                                     jnp.log(0.001), jnp.log(0.1)))
    return {
        "x": nrm(ks[0], (BATCH, SEQ, D_MODEL), 1.0),
        "norm1_w": 1.0 + nrm(ks[1], (DEPTH, D_MODEL), 0.02),
        "w_in": nrm(ks[2], (DEPTH, D_MODEL, IN_DIM), D_MODEL ** -0.5),
        "b_gate": nrm(ks[3], (DEPTH, 2 * D_MODEL), 0.02),
        "attn_sinks": nrm(ks[4], (DEPTH, N_Q_HEADS), 0.5),
        "w_attn_o": nrm(ks[5], (DEPTH, Q_DIM, D_MODEL), Q_DIM ** -0.5),
        "ssd_conv_w": nrm(ks[6], (DEPTH, SSD_CONV, XBC_DIM), SSD_CONV ** -0.5),
        "ssd_conv_b": nrm(ks[7], (DEPTH, XBC_DIM), 0.02),
        "dt_bias": dt0 + jnp.log(-jnp.expm1(-dt0)),
        "a_log": jnp.log(jax.random.uniform(ks[10], (DEPTH, N_SSD_HEADS), f32, 1.0, 16.0)),
        "d_skip": 1.0 + nrm(ks[11], (DEPTH, N_SSD_HEADS), 0.02),
        "ssd_norm_w": 1.0 + nrm(ks[12], (DEPTH, D_INNER), 0.02),
        "w_ssd_o": nrm(ks[13], (DEPTH, D_INNER, D_MODEL), D_INNER ** -0.5),
        "w_out": nrm(ks[14], (DEPTH, D_MODEL, D_MODEL), D_MODEL ** -0.5),
        "norm2_w": 1.0 + nrm(ks[15], (DEPTH, D_MODEL), 0.02),
        "w_up": nrm(ks[16], (DEPTH, D_MODEL, 2 * D_FF), D_MODEL ** -0.5),
        "ffn_conv_w": nrm(ks[17], (DEPTH, FFN_CONV, 2 * D_FF), FFN_CONV ** -0.5),
        "ffn_conv_b": nrm(ks[18], (DEPTH, 2 * D_FF), 0.02),
        "w_down": nrm(ks[19], (DEPTH, D_FF, D_MODEL), D_FF ** -0.5),
        "final_norm_w": 1.0 + nrm(ks[20], (D_MODEL,), 0.02),
    }

def reference(x, norm1_w, w_in, b_gate, attn_sinks, w_attn_o, ssd_conv_w, ssd_conv_b, dt_bias,
              a_log, d_skip, ssd_norm_w, w_ssd_o, w_out, norm2_w, w_up, ffn_conv_w, ffn_conv_b,
              w_down, final_norm_w):
    Bsz, S, _ = x.shape
    h = x
    for layer in range(DEPTH):
        xn = rmsnorm(h, norm1_w[layer])
        proj = xn @ w_in[layer]
        q, k, v, z, xbc, dt_raw, ga_raw, gs_raw = _split(proj, IN_SPLITS)
        ba, bs = _split(b_gate[layer], (D_MODEL, D_MODEL))
        gate_a = jax.nn.sigmoid(ga_raw + ba)
        gate_s = jax.nn.sigmoid(gs_raw + bs)
        attn = banded_sink_attention(q, k, v, attn_sinks[layer]) @ w_attn_o[layer]
        xbc = jax.nn.silu(causal_dwconv(xbc, ssd_conv_w[layer], ssd_conv_b[layer]))
        xs, bm, cm = _split(xbc, (D_INNER, BC_DIM, BC_DIM))
        dt = jax.nn.softplus(dt_raw.astype(jnp.float32) + dt_bias[layer].astype(jnp.float32))
        y = ssd_chunked(xs.reshape(Bsz, S, N_SSD_HEADS, SSD_HEAD_DIM), dt, a_log[layer],
                        bm.reshape(Bsz, S, N_SSD_GROUPS, D_STATE),
                        cm.reshape(Bsz, S, N_SSD_GROUPS, D_STATE), d_skip[layer])
        y = y.reshape(Bsz, S, D_INNER) * jax.nn.silu(z.astype(jnp.float32))
        yg = y.reshape(Bsz, S, N_SSD_GROUPS, D_INNER // N_SSD_GROUPS)
        yg = yg * lax.rsqrt(jnp.mean(yg * yg, axis=-1, keepdims=True) + EPS)
        y = (yg.reshape(Bsz, S, D_INNER) * ssd_norm_w[layer].astype(jnp.float32)).astype(x.dtype)
        ssd_out = y @ w_ssd_o[layer]
        mix = (gate_a * attn + gate_s * ssd_out) @ w_out[layer]
        h = h + mix.astype(h.dtype)
        hn = rmsnorm(h, norm2_w[layer])
        u = causal_dwconv(hn @ w_up[layer], ffn_conv_w[layer], ffn_conv_b[layer])
        val, gt = _split(u, (D_FF, D_FF))
        h = h + ((jax.nn.silu(gt) * val) @ w_down[layer]).astype(h.dtype)
    return rmsnorm(h, final_norm_w)


_drawn_inputs = setup_inputs


def setup_inputs(seed=0):
    import zlib

    import numpy as np

    out = dict(_drawn_inputs(seed))
    spreads = {}
    factors = {'norm1_w': 3.161,
     'b_gate': 8.0,
     'attn_sinks': 28.496,
     'ssd_conv_b': 3.838,
     'd_skip': 62.704,
     'ssd_norm_w': 5.556,
     'norm2_w': 4.27,
     'ffn_conv_b': 4.311,
     'final_norm_w': 8.709}
    for name, (base, spread) in spreads.items():
        noise = np.random.default_rng([zlib.crc32(name.encode()), seed]).standard_normal(out[name].shape)
        drawn = base * np.exp(spread * noise) if base else spread * noise
        out[name] = __import__('jax').numpy.asarray(drawn.astype(out[name].dtype))
    for name, factor in factors.items():
        out[name] = (out[name] * factor).astype(out[name].dtype)
    return out
```

```python
import concourse.bass as bass
from concourse import mybir
from contextlib import ExitStack

F32 = mybir.dt.float32
F32R = mybir.dt.float32r
I32 = mybir.dt.int32
ALU = mybir.AluOpType
ACT = mybir.ActivationFunctionType
AX = mybir.AxisListType

P = 128
SEQ, D = 512, 1024
NT = SEQ // P
KT = D // P
HQ, HKV, HD = 16, 4, 64
GQ = HQ // HKV
DI = 2 * D
NH, NG, NS = 32, 4, 128
HG = NH // NG
TG = DI // NG // P
XBC = DI + 2 * NG * NS
FF = 2816
FT = FF // P
EPS = 1e-5
NEG = -1e30
Q0 = 0
K0 = Q0 + HQ * HD
V0 = K0 + HKV * HD
Z0 = V0 + HKV * HD
X0 = Z0 + DI
B0 = X0 + DI
DT0 = X0 + XBC
GA0 = DT0 + NH
GS0 = GA0 + D
CH = 2048
VW = HKV * HD + NH

CHUNKS = [("k", 0), ("vd", 0), ("vd", 1)] + [("q", i) for i in range(4)]
CHUNKS += [("bc", i) for i in range(4)]
CHUNKS += [("xs", 0), ("xs", 1), ("z", 0), ("z", 1), ("xs", 2), ("xs", 3), ("z", 2), ("z", 3)]
for _i in range(4):
    CHUNKS += [("ga", _i), ("ao", _i)]
CHUNKS += [("xs", 4), ("xs", 5), ("z", 4), ("z", 5), ("xs", 6), ("xs", 7), ("z", 6), ("z", 7)]
CHUNKS += [("gs", i) for i in range(4)]
for _i in range(2):
    CHUNKS += [("so", (2 * _i, 0)), ("so", (2 * _i + 1, 0)), ("so", (2 * _i, 1)), ("so", (2 * _i + 1, 1))]
CHUNKS += [("out", i) for i in range(4)]
CHUNKS += [("up", i) for i in range(22)]
CHUNKS += [("down", i) for i in range(12)]
AT = {ch: n for n, ch in enumerate(CHUNKS)}

FORM_B = ("vd", "out", "down")
DONE = {}
_n = 0
for _c, (_kind, _i) in enumerate(CHUNKS):
    for _p in range(4 if _kind in FORM_B else 2):
        _n += 1
        DONE[_c, _p] = _n
    DONE[_c] = _n

N_ATT = NT * HKV
N_SSD = NG * NT
RIDES = {}
RIDES[AT[("q", 1)], 1] = [("acs", 0)]
RIDES[AT[("q", 2)], 1] = [("acs", 1)]
_first = AT[("bc", 0)]
for _n in range(N_ATT + 2):
    _u = _n + _n // 3 + 1
    RIDES.setdefault((_first + _u // 2, _u % 2), []).append(("att", _n))
_u = 2 * AT[("xs", 4)]
for _n in range(N_SSD + 2):
    _at = _u + (2 * _n + 1 if _n < 8 else 16 + (_n - 8))
    RIDES.setdefault((_at // 2, _at % 2), []).append(("ssd", _n))


def hybrid_layer(nc, x, norm1_w, w_in, b_gate, attn_sinks, w_attn_o, ssd_conv_w, ssd_conv_b, dt_bias,
                 a_log, d_skip, ssd_norm_w, w_ssd_o, w_out, norm2_w, w_up, ffn_conv_w, ffn_conv_b,
                 w_down, final_norm_w, out):
    ctx = ExitStack()
    with ctx:
        base = 16512

        def sb(name, shape, kb, dt=F32):
            return nc.alloc_sbuf_tensor_at(name, shape, dt, offset=base + int(kb * 1024))

        xn_hi = sb("xn_hi", [P, KT, SEQ], 0, F32R)
        xn_lo = sb("xn_lo", [P, KT, SEQ], 16, F32R)
        raw = sb("w_raw", [P, 2, CH], 32)
        whi = sb("w_hi", [P, 2, CH], 48, F32R)
        wlo = sb("w_lo", [P, 2, CH], 64, F32R)
        xs = sb("xs", [P, 16, SEQ], 80)
        y_hi = sb("y_hi", [P, 16, SEQ], 80, F32R)
        sz = sb("sz", [P, 16, SEQ], 112)
        y_lo = sb("y_lo", [P, 16, SEQ], 112, F32R)
        bc = sb("bc", [P, 2 * NG, SEQ], 144)
        qT = sb("qT", [P, 8, SEQ], 160)
        a_hi = sb("a_hi", [P, 8, SEQ], 160, F32R)
        a_lo = sb("a_lo", [P, 8, SEQ], 96, F32R)
        kT = sb("kT", [P, 2, SEQ], 176)
        v = sb("v", [P, NT, HKV * HD], 180)
        cacc = sb("conv_acc", [P, 2, SEQ], 184)
        cth = sb("conv_tanh", [P, 2, SEQ], 188)
        xnat = sb("x_nat", [P, NT, D], 112)
        xsc = sb("x_scaled", [P, D], 128)
        xt = sb("x_t", [P, D], 132)
        junk = sb("junk", [P, D], 136)
        stage = sb("param_rows", [P, 3, P], 140)
        dskb = sb("d_skip_rows", [P, NH], 141.5)
        sp = [sb(f"softplus{i}", [P, NT * NH], 112 + 0.5 * i) for i in range(6)]
        acsT = sb("acs_t", [NH, SEQ], 116)
        S = sb("scores", [P, GQ, P], 128)
        Pr = sb("probs", [P, GQ, P], 130)
        pt = sb("probs_t", [P, GQ, P], 132)
        ptc = sb("probs_t_cur", [P, GQ, P], 134)
        ptp = sb("probs_t_prev", [P, GQ, P], 136)
        ag = sb("decay", [P, 2, HG, P], 160)
        e2 = sb("decay_off", [P, 2, TG, P], 168)
        xc = sb("xdt", [P, SEQ], 172)
        xcd = sb("xdt_decayed", [P, SEQ], 174)
        st = sb("state", [P, SEQ], 176)
        yo = sb("y_off", [P, SEQ], 178)
        bncb = sb("b_nat_cb", [P, 2 * P], 180)
        sq = sb("y_squared", [P, SEQ], 181)
        gsd = sb("group_rms", [P, SEQ], 203.5)
        sq1 = sb("y_sq_pair", [P, 2 * P], 205.5)
        sq2 = sb("y_sq_sum", [P, P], 206.5)
        mix_hi = sb("mix_hi", [P, KT, SEQ], 144, F32R)
        mix_lo = sb("mix_lo", [P, KT, SEQ], 160, F32R)
        h = sb("h", [P, NT, D], 0)
        hn_hi = sb("hn_hi", [P, KT, SEQ], 16, F32R)
        hn_lo = sb("hn_lo", [P, KT, SEQ], 80, F32R)
        hsc = sb("h_scaled", [P, D], 176)
        ht = sb("h_t", [P, D], 180)
        hjunk = sb("h_junk", [P, D], 96)
        act_hi = sb("act_hi", [P, FT, SEQ], 96, F32R)
        act_lo = sb("act_lo", [P, FT, SEQ], 140, F32R)
        ga2 = sb("gated", [P, 2, SEQ], 203.5)
        fnw = sb("final_norm_row", [P, D], 16)
        fo = sb("final_out", [P, 2, D], 20)
        fjunk = sb("f_junk", [P, D], 28)
        ident = sb("ident", [P, P], 192)
        ones = sb("ones", [P, P], 192.5)
        tri = sb("tri", [P, P], 193)
        negm = sb("neg_mask", [P, P], 193.5)
        mprevT = sb("mask_prev_t", [P, P], 194)
        mprev = sb("mask_prev", [P, P], 194.5, I32)
        negt = sb("neg_tile", [P, P], 195)
        pcol = sb("param_cols", [P, 3, P], 195.5)
        small = sb("small", [P, 512], 197)
        dt = sb("dt", [P, NT, NH], 199)
        nacs = sb("neg_acs", [P, NT, NH], 199.5)
        ddt = sb("dt_decay", [P, 2, HG], 200)
        cdec = sb("chunk_decay", [P, 2, HG], 200.125)
        dsk = sb("d_cols", [P, 16], 200.25)
        dtr = sb("dt_raw", [P, NT, NH], 200.5)
        nA = sb("neg_a", [P, NH], 201)
        dtb = sb("dt_bias", [P, NH], 201.25)
        cwh = sb("half_conv", [P, P], 201.5)
        fwh = sb("half_ffn", [P, 4, FT], 202)
        bgh = sb("half_gate_bias", [P, 16], 202.5)
        PS = ctx.enter_context(nc.psum_tensor("banks", [P, 8, 512], F32))

        NX = XBC // P
        CW = lambda k, t: cwh[:, k * NX + t:k * NX + t + 1]
        CB = lambda t: cwh[:, 4 * NX + t:4 * NX + t + 1]
        n1w = pcol[:, 0, 5 * NX:5 * NX + KT]
        n2w = pcol[:, 1, 4 * FT:4 * FT + KT]
        bg0 = 4 * FT + KT
        snw = pcol[:, 1, bg0 + 16:bg0 + 32]

        def FW(k, t):
            if t >= FT:
                return fwh[:, k, t - FT:t - FT + 1]
            if k < 2:
                return pcol[:, 1, k * 2 * FT + t:k * 2 * FT + t + 1]
            o = (k - 2) * 2 * FT + t
            return pcol[:, 2, o:o + 1]

        ss, sd, rs = small[:, 0:8], small[:, 8:16], small[:, 16:24]
        mx, m_, nm = small[:, 24:28], small[:, 28:32], small[:, 32:36]
        rsum, es, den, rden = small[:, 36:40], small[:, 40:44], small[:, 44:48], small[:, 48:52]
        snk = small[:, 52:68]
        epsc = small[:, 68:69]
        dd8 = small[:, 72:80]
        fss, fsd, frs = small[:, 80:84], small[:, 84:88], small[:, 88:92]
        hss, hsd, hrs = small[:, 92:96], small[:, 96:100], small[:, 100:104]

        acs_d = nc.dram_tensor("acs_scratch", [NH, SEQ], F32, kind="Internal").ap()
        mixa_d = nc.dram_tensor("mixa_scratch", [KT, P, SEQ], F32, kind="Internal").ap()
        gs_d = nc.dram_tensor("gs_scratch", [KT, P, SEQ], F32, kind="Internal").ap()

        def sem(name):
            return ctx.enter_context(nc.semaphore(name))

        x_in = [sem(f"x_in{t}") for t in range(NT)]
        params_in = sem("params_in")
        w_in_slot = [sem(f"w_loaded{i}") for i in range(2)]
        w_rounded, w_split = sem("w_rounded"), sem("w_split")
        consts = sem("consts")
        pcols_t, pcols = sem("param_transposed"), sem("params_ready")
        gemm_done = sem("gemm_done")
        n_sq, n_sd, n_rs, n_sc, n_tp, n_tw, n_hi, n_lo = [sem("n_" + s) for s in (
            "squared", "root", "rstd", "scaled", "transposed", "weighted", "hi", "lo")]
        qk_ready = sem("qk_ready")
        vd_done, v_ready = sem("vd_done"), sem("v_ready")
        spc, spa, spd, da_ready = sem("softplus_abs"), sem("softplus_exp"), sem("softplus_steps"), sem("da_ready")
        acs_mm, acs_ev, acs_out, acs_tp, acs_nat = [sem("acs_" + s) for s in ("mm", "copied", "stored", "t", "nat")]
        c_acc, c_tap, c_tanh, c_out = [sem("conv_" + s) for s in ("bias", "tap", "tanh", "out")]
        z_tanh, z_out = sem("z_tanh"), sem("z_out")
        g_tanh, ao_out, gs_tanh = sem("ga_tanh"), sem("ao_gated"), sem("gs_tanh")
        ao_sp = [sem(f"ao_spilled{j}") for j in range(2)]
        gs_sp = [sem(f"gs_spilled{j}") for j in range(2)]
        a_sc, a_cur, a_sel, a_max, a_m, a_nm, a_exp, a_es, a_den, a_rd, a_pr = [sem("att_" + s) for s in (
            "scores", "cur", "selected", "max", "m", "negm", "exp", "sink", "den", "rden", "probs")]
        a_df = sem("att_sinkdiff")
        a_tp, a_pt, a_ptc, a_ptp, a_pv, a_oh, a_ol = [sem("att_" + s) for s in (
            "transposed", "pt", "ptc", "ptp", "pv", "hi", "lo")]
        d_ab = [sem(f"ssd_acs_in{i}") for i in range(2)]
        d_e2 = [sem(f"ssd_acs2_in{i}") for i in range(2)]
        (d_x, d_bc, d_bcs, d_gm, d_exp, d_m, d_e2x, d_dd, d_de, d_cd, d_ddt, d_xc, d_xcd, d_dxs, d_stt, d_stm,
         d_mm, d_yo, d_yd, d_yx, d_y, d_sq, d_s1, d_s2, d_sum, d_stp) = [sem("ssd_" + s) for s in (
             "xs_t", "b_cb", "b_cb_copied", "masked", "exp", "m", "e2", "dd", "dexp", "cdec", "ddt", "xc", "xcd",
             "dxs", "st_mm", "st_scaled", "diag", "yoff", "yadd", "yskip", "y", "sq", "sq1", "sq2", "sum", "state")]
        g_sd, g_rs, g_w, g_hi, g_lo = [sem("gnorm_" + s) for s in ("root", "rstd", "weighted", "hi", "lo")]
        so_in = [sem(f"so_in{j}") for j in range(2)]
        so_g, so_a, so_hi, so_lo = [sem("so_" + s) for s in ("gated", "added", "hi", "lo")]
        h_in = sem("h_x_in")
        out_done, h_add = sem("out_done"), sem("h_added")
        u_acc, u_tap, u_tanh, u_silu, u_mul, u_hi, u_lo = [sem("up_" + s) for s in (
            "bias", "tap", "tanh", "silu", "mul", "hi", "lo")]
        dn_done, dn_add = sem("down_done"), sem("down_added")
        f_sq, f_sd, f_rs, f_out, fnw_in = [sem("final_" + s) for s in ("squared", "root", "rstd", "weighted", "row_in")]
        f_st = [sem(f"final_stored{i}") for i in range(2)]

        win = w_in[0]

        def chunk_dmas(c):
            kind, i = CHUNKS[c]
            slot = raw[:, c % 2, :]

            def cols(w, k0, nk, c0, nc_):
                return w[k0 * P:(k0 + nk) * P, c0:c0 + nc_].rearrange("(t p) n -> p t n", p=P)

            a = slot.rearrange("p (t n) -> p t n", t=KT)
            b = slot.rearrange("p (t n) -> p t n", t=4)
            if kind == "k":
                return [(a, cols(win, 0, KT, K0, 256))]
            if kind == "q":
                res = []
                for u in range(2):
                    t = 2 * i + u
                    G, j = t // GQ, t % GQ
                    for hh in range(2):
                        c0 = Q0 + ((2 * G + hh) * GQ + j) * HD
                        res.append((a[:, :, u * P + hh * HD:u * P + (hh + 1) * HD], cols(win, 0, KT, c0, HD)))
                return res
            if kind == "vd":
                s = slot[:, 0:4 * VW].rearrange("p (t n) -> p t n", t=4)
                return [(s[:, :, 0:HKV * HD], cols(win, 4 * i, 4, V0, HKV * HD)),
                        (s[:, :, HKV * HD:VW], cols(win, 4 * i, 4, DT0, NH))]
            c0 = {"bc": B0, "xs": X0, "z": Z0, "ga": GA0, "gs": GS0}.get(kind)
            if c0 is not None:
                return [(a, cols(win, 0, KT, c0 + 256 * i, 256))]
            if kind == "ao":
                res = []
                for G in range(2):
                    for hh in range(2):
                        r0 = (2 * G + hh) * GQ * HD
                        src = w_attn_o[0][r0:r0 + GQ * HD, 256 * i:256 * i + 256].rearrange("(j d) n -> d j n", d=HD)
                        res.append((a[hh * HD:(hh + 1) * HD, G * GQ:(G + 1) * GQ, :], src))
                return res
            if kind == "so":
                f, kh = i
                return [(a, cols(w_ssd_o[0], KT * kh, KT, 256 * f, 256))]
            if kind == "out":
                return [(b, cols(w_out[0], 4 * (i % 2), 4, 512 * (i // 2), 512))]
            if kind == "up":
                return [(a, cols(w_up[0], 0, KT, (i % 2) * FF + 256 * (i // 2), 256))]
            if kind == "down":
                nh, kc = i // 6, i % 6
                nk = min(4, FT - 4 * kc)
                return [(b[:, 0:nk, :], cols(w_down[0], 4 * kc, nk, 512 * nh, 512))]

        def chunk_len(c):
            kind, i = CHUNKS[c]
            if kind == "vd":
                return 4 * VW
            if kind == "down" and i % 6 == 5:
                return (FT - 20) * 512
            return CH

        loads_before = []
        _cnt = [0, 0]
        for c in range(len(CHUNKS)):
            _cnt[c % 2] += 16 * len(chunk_dmas(c))
            loads_before.append(_cnt[c % 2])

        f32 = lambda t: t.bitcast(F32)
        block = ctx.enter_context(nc.Block())

        @block.sync
        def _(eng):
            for t in range(NT):
                eng.dma_start(xnat[:, t, :], x[0, t * P:(t + 1) * P, :]).then_inc(x_in[t], 16)
            for c in range(len(CHUNKS)):
                if c >= 2:
                    eng.wait_ge(w_split, c - 1)
                for dst, src in chunk_dmas(c):
                    eng.dma_start(dst, src).then_inc(w_in_slot[c % 2], 16)
                if c == AT[("so", (2, 1))]:
                    eng.wait_ge(gemm_done, DONE[AT[("gs", 3)]])
                    eng.dma_start(h[:, :, :], x[0].rearrange("(t p) n -> p t n", p=P)).then_inc(h_in, 16)
                if c == AT[("down", 3)]:
                    eng.wait_ge(gemm_done, DONE[AT[("up", 21)]])
                    eng.dma_start(fnw[:, :], final_norm_w.unsqueeze(0).broadcast_to([P, D])).then_inc(fnw_in, 16)
            for t in range(NT):
                eng.wait_ge(f_out, t + 1)
                eng.dma_start(out[0, t * P:(t + 1) * P, :], fo[:, t % 2, :]).then_inc(f_st[t % 2], 16)
            for i in range(2):
                eng.wait_ge(f_st[i], 16 * (NT // 2))

        @block.gpsimd
        def _(eng):
            n = [0]

            def made(ins):
                n[0] += 1
                ins.then_inc(consts, 1)

            for t_, val in ((ident, 0.0), (ones, 1.0), (tri, 1.0), (negm, 0.0), (mprevT, 1.0), (negt, NEG)):
                made(eng.memset(t_[:, :], val))
            made(eng.memset(epsc, EPS))
            made(eng.memset(f32(mprev[:, :]), 1.0))
            eng.wait_ge(consts, 8)
            made(eng.affine_select(out=ident[:, :], in_=ident[:, :], compare_op=ALU.not_equal, fill=1.0, base=0,
                                   pattern=[[-1, P]], channel_multiplier=1))
            made(eng.affine_select(out=tri[:, :], in_=tri[:, :], compare_op=ALU.is_ge, fill=0.0, base=0,
                                   pattern=[[1, P]], channel_multiplier=-1))
            made(eng.affine_select(out=negm[:, :], in_=negm[:, :], compare_op=ALU.is_ge, fill=NEG, base=0,
                                   pattern=[[1, P]], channel_multiplier=-1))
            made(eng.affine_select(out=mprevT[:, :], in_=mprevT[:, :], compare_op=ALU.is_gt, fill=0.0, base=0,
                                   pattern=[[-1, P]], channel_multiplier=1))
            made(eng.affine_select(out=f32(mprev[:, :]), in_=f32(mprev[:, :]), compare_op=ALU.is_gt, fill=0.0,
                                   base=0, pattern=[[1, P]], channel_multiplier=-1))

            eng.wait_ge(acs_ev, 1)
            eng.dma_start(acs_d, acsT[:, :]).then_inc(acs_out, 16)

            def acs_load(n):
                g, c = n // NT, n % NT
                if n >= 2:
                    eng.wait_ge(d_mm, n - 1)
                    eng.wait_ge(d_y, n - 1)
                if n == 0:
                    eng.wait_ge(acs_out, 16)
                    eng.wait_ge(gemm_done, DONE[AT[("ao", 3)]])
                rows = acs_d[HG * g:HG * g + HG, c * P:(c + 1) * P]
                eng.dma_start(ag[:, n % 2, :, :], rows.unsqueeze(0).broadcast_to([P, HG, P])).then_inc(d_ab[n % 2], 16)
                for hh in range(2):
                    src = rows.rearrange("(i two) l -> two i l", two=2)[hh]
                    eng.dma_start(e2[hh * HD:(hh + 1) * HD, n % 2, :, :],
                                  src.unsqueeze(0).broadcast_to([HD, TG, P])).then_inc(d_e2[n % 2], 16)

            for c, (kind, i) in enumerate(CHUNKS):
                if kind == "so" and i[1] == 1:
                    if i[0] == 0:
                        eng.wait_ge(c_out, 24)
                    for j in range(2):
                        f = 2 * i[0] + j
                        if i[0] == 0:
                            eng.wait_ge(ao_sp[j], 16 * 4)
                            eng.wait_ge(gs_sp[j], 16 * 4)
                        else:
                            eng.wait_ge(so_lo, 2 * (i[0] - 1) + j + 1)
                        eng.dma_start(cacc[:, j, :], mixa_d[f]).then_inc(so_in[j], 16)
                        eng.dma_start(cth[:, j, :], gs_d[f]).then_inc(so_in[j], 16)
                for u in range(2):
                    if kind == "ao":
                        eng.wait_ge(ao_out, 2 * i + u + 1)
                        eng.dma_start(mixa_d[2 * i + u], cacc[:, u, :]).then_inc(ao_sp[u], 16)
                    if kind == "gs":
                        eng.wait_ge(gs_tanh, 2 * i + u + 1)
                        eng.dma_start(gs_d[2 * i + u], cth[:, u, :]).then_inc(gs_sp[u], 16)
                    for what, n in RIDES.get((c, u), []):
                        if what == "att":
                            if 1 <= n <= N_ATT:
                                k = n - 1
                                eng.wait_ge(a_pt, k + 1)
                                if k:
                                    eng.wait_ge(a_pv, k)
                                eng.tensor_tensor(ptp[:, :, :], pt[:, :, :],
                                                  mprevT[:, :].unsqueeze(1).broadcast_to([P, GQ, P]),
                                                  ALU.mult).then_inc(a_ptp, 1)
                        elif what == "ssd":
                            if n == 0:
                                acs_load(0)
                            if n + 1 < N_SSD:
                                acs_load(n + 1)
                            if n < N_SSD:
                                eng.wait_ge(d_ab[n % 2], 16 * (n // 2 + 1))
                                eng.wait_ge(d_dd, n + 1)
                                eng.wait_ge(d_cd, n + 1)
                                eng.tensor_tensor(ag[:, n % 2, :, :], ag[:, n % 2, :, :],
                                                  negm[:, :].unsqueeze(1).broadcast_to([P, HG, P]),
                                                  ALU.add).then_inc(d_gm, 1)
                                g, cc = n // NT, n % NT
                                eng.wait_ge(d_x, n + 1)
                                eng.wait_ge(pcols, 11)
                                v_ = xs[:, TG * g:TG * g + TG, cc * P:(cc + 1) * P]
                                eng.tensor_tensor(v_, v_, dsk[:, TG * g:TG * g + TG].unsqueeze(2)
                                                  .broadcast_to([P, TG, P]), ALU.mult).then_inc(d_dxs, 1)
                            if 1 <= n <= N_SSD:
                                k = n - 1
                                eng.wait_ge(d_sq, k + 1)
                                if k:
                                    eng.wait_ge(d_s2, k)
                                eng.tensor_tensor(sq1[:, :], sq[:, 0:2 * P], sq[:, 2 * P:4 * P],
                                                  ALU.add).then_inc(d_s1, 1)
                                eng.wait_ge(d_s1, k + 1)
                                if k:
                                    eng.wait_ge(d_sum, k)
                                eng.tensor_tensor(sq2[:, :], sq1[:, 0:P], sq1[:, P:2 * P],
                                                  ALU.add).then_inc(d_s2, 1)

        @block.scalar
        def _(eng):
            A = nc.scalar
            rows = [
                (stage[0:96, 0, :], ssd_conv_w[0].rearrange("k (t p) -> (k t) p", p=P)),
                (stage[96:120, 0, :], ssd_conv_b[0].rearrange("(t p) -> t p", p=P)),
                (stage[120:128, 0, :], norm1_w[0].rearrange("(t p) -> t p", p=P)),
                (stage[0:88, 1, :], ffn_conv_w[0, 0:2].rearrange("k (t p) -> (k t) p", p=P)),
                (stage[88:96, 1, :], norm2_w[0].rearrange("(t p) -> t p", p=P)),
                (stage[96:112, 1, :], b_gate[0].rearrange("(t p) -> t p", p=P)),
                (stage[112:128, 1, :], ssd_norm_w[0].rearrange("(t p) -> t p", p=P)),
                (stage[0:44, 2, :], ffn_conv_w[0, 2].rearrange("(t p) -> t p", p=P)),
                (stage[44:88, 2, :], ffn_conv_b[0].rearrange("(t p) -> t p", p=P)),
                (dtb[:, :], dt_bias[0].unsqueeze(0).broadcast_to([P, NH])),
                (nA[:, :], a_log[0].unsqueeze(0).broadcast_to([P, NH])),
                (dskb[:, :], d_skip[0].unsqueeze(0).broadcast_to([P, NH])),
                (snk, attn_sinks[0].unsqueeze(0).broadcast_to([P, HQ])),
            ]
            for dst, src in rows:
                eng.dma_start(dst, src).then_inc(params_in, 16)

            def split(c):
                eng.wait_ge(w_in_slot[c % 2], loads_before[c])
                if c >= 2:
                    eng.wait_ge(gemm_done, DONE[c - 2])
                n = chunk_len(c)
                A.activation(whi[:, c % 2, 0:n], raw[:, c % 2, 0:n], ACT.Copy).then_inc(w_rounded, 1)

            def norm_hi(t):
                eng.wait_ge(n_tw, NT + t + 1)
                A.activation(hn_hi[:, :, t * P:(t + 1) * P], ht[:, :].rearrange("p (k l) -> p k l", k=KT),
                             ACT.Copy).then_inc(n_hi, 1)

            for t in range(NT):
                eng.wait_ge(x_in[t], 16)
                if t == 0:
                    eng.wait_ge(consts, 13)
                else:
                    eng.wait_ge(n_sq, t)
                A.activation(junk[:, :], xnat[:, t, :], ACT.Square, accum_out=ss[:, t:t + 1]).then_inc(n_sq, 1)
                eng.wait_ge(n_sq, t + 1)
                A.activation(sd[:, t:t + 1], ss[:, t:t + 1], ACT.Sqrt, bias=epsc, scale=1.0 / D).then_inc(n_sd, 1)
            for t in range(NT):
                eng.wait_ge(n_tw, t + 1)
                A.activation(xn_hi[:, :, t * P:(t + 1) * P], xt[:, :].rearrange("p (k l) -> p k l", k=KT),
                             ACT.Copy).then_inc(n_hi, 1)
            eng.wait_ge(params_in, 16 * 13)
            A.activation(nA[:, :], nA[:, :], ACT.Exp).then_inc(spa, 1)
            split(0)
            k_conv = k_z = k_gs = 0
            for c, (kind, i) in enumerate(CHUNKS):
                if c + 1 < len(CHUNKS):
                    split(c + 1)
                for u in range(2):
                    if kind in ("k", "q"):
                        eng.wait_ge(gemm_done, DONE[c, u])
                        if kind == "k":
                            A.activation(kT[:, u, :], PS[:, u, :], ACT.Copy).then_inc(qk_ready, 1)
                        else:
                            A.activation(qT[:, 2 * i + u, :], PS[:, u, :], ACT.Copy,
                                         scale=HD ** -0.5).then_inc(qk_ready, 1)
                    elif kind in ("bc", "xs"):
                        t = 2 * i + u + (16 if kind == "bc" else 0)
                        eng.wait_ge(gemm_done, DONE[c, u])
                        if k_conv == 0:
                            eng.wait_ge(pcols, 11)
                        if kind == "xs" and i == 4:
                            eng.wait_ge(ao_sp[u], 16 * 4)
                        if k_conv >= 2:
                            eng.wait_ge(c_out, k_conv - 1)
                        A.activation(cacc[:, u, :], PS[:, u, :], ACT.Identity, bias=CB(t),
                                     scale=CW(3, t)).then_inc(c_acc, 1)
                        eng.wait_ge(c_tap, 3 * k_conv + 3)
                        A.activation(cth[:, u, :], cacc[:, u, :], ACT.Tanh).then_inc(c_tanh, 1)
                        k_conv += 1
                    elif kind == "z":
                        eng.wait_ge(gemm_done, DONE[c, u])
                        eng.wait_ge(c_out, k_conv)
                        if k_z >= 2:
                            eng.wait_ge(z_out, k_z - 1)
                        A.activation(cth[:, u, :], PS[:, u, :], ACT.Tanh, scale=0.5).then_inc(z_tanh, 1)
                        k_z += 1
                    elif kind == "ga":
                        eng.wait_ge(gemm_done, DONE[c, u])
                        eng.wait_ge(z_out, k_z)
                        if i:
                            eng.wait_ge(ao_out, 2 * (i - 1) + u + 1)
                        A.activation(cth[:, u, :], PS[:, u, :], ACT.Tanh, scale=0.5,
                                     bias=bgh[:, 2 * i + u:2 * i + u + 1]).then_inc(g_tanh, 1)
                    elif kind == "gs":
                        eng.wait_ge(gemm_done, DONE[c, u])
                        eng.wait_ge(z_out, k_z)
                        if i:
                            eng.wait_ge(gs_sp[u], 16 * i)
                        A.activation(cth[:, u, :], PS[:, u, :], ACT.Tanh, scale=0.5,
                                     bias=bgh[:, 8 + 2 * i + u:8 + 2 * i + u + 1]).then_inc(gs_tanh, 1)
                    elif kind == "so" and i[1] == 1:
                        f = 2 * i[0] + u
                        eng.wait_ge(so_a, f + 1)
                        A.activation(mix_hi[:, f, :], cacc[:, u, :], ACT.Copy, scale=0.5).then_inc(so_hi, 1)
                    elif kind == "up":
                        k = 2 * i + u
                        t = (i % 2) * FT + 2 * (i // 2) + u
                        b = 2 * (i % 2) + u
                        it = i // 2
                        dst = cacc[:, u, :] if i % 2 == 0 else ga2[:, u, :]
                        eng.wait_ge(gemm_done, DONE[c, u])
                        if it:
                            eng.wait_ge(u_lo if i % 2 else u_mul, 2 * (it - 1) + u + 1)
                        A.activation(dst, PS[:, b, :], ACT.Identity, bias=FW(3, t), scale=FW(2, t)).then_inc(u_acc, 1)
                        if i % 2:
                            eng.wait_ge(u_tap, 2 * k + 2)
                            A.activation(cth[:, u, :], ga2[:, u, :], ACT.Tanh).then_inc(u_tanh, 1)
                            f = 2 * it + u
                            eng.wait_ge(u_mul, f + 1)
                            A.activation(act_hi[:, f, :], ga2[:, u, :], ACT.Copy).then_inc(u_hi, 1)
                    if kind == "vd" and i == 1 and u == 1:
                        eng.wait_ge(spc, 1)
                        A.activation(sp[0][:, :], sp[0][:, :], ACT.Exp, scale=-1.0).then_inc(spa, 1)
                    for what, n in RIDES.get((c, u), []):
                        if what == "acs":
                            if n == 0:
                                eng.wait_ge(acs_mm, 1)
                                A.activation(acsT[:, :], PS[0:NH, 2, :], ACT.Copy).then_inc(acs_ev, 1)
                        elif what == "att":
                            if n < N_ATT:
                                eng.wait_ge(a_sc, n + 1)
                                if n:
                                    eng.wait_ge(a_exp, GQ * n)
                                sv = PS[:, 2 + 2 * (n % 2):4 + 2 * (n % 2), :].rearrange("p b (j s) -> p (b j) s", j=2)
                                A.activation(S[:, :, :], sv[:, :, P:2 * P], ACT.Copy).then_inc(a_cur, 1)
                            if 1 <= n <= N_ATT:
                                k = n - 1
                                eng.wait_ge(a_tp, k + 1)
                                if k:
                                    eng.wait_ge(a_ptc, k)
                                    eng.wait_ge(a_ptp, k)
                                A.activation(pt[:, :, :], PS[:, 6, :].rearrange("p (j q) -> p j q", j=GQ),
                                             ACT.Copy).then_inc(a_pt, 1)
                            if n >= 2:
                                k = n - 2
                                g, b = k % HKV, k // HKV
                                o = (g % 2) * HD
                                eng.wait_ge(a_pv, k + 1)
                                A.activation(a_hi[o:o + HD, (g // 2) * GQ:(g // 2) * GQ + GQ, b * P:(b + 1) * P],
                                             PS[o:o + HD, 7, :].rearrange("p (j q) -> p j q", j=GQ),
                                             ACT.Copy).then_inc(a_oh, 1)
                            if n < N_ATT:
                                eng.wait_ge(a_nm, n + 1)
                                if n:
                                    eng.wait_ge(a_tp, n)
                                for j in range(GQ):
                                    A.activation(Pr[:, j, :], S[:, j, :], ACT.Exp, bias=nm[:, j:j + 1],
                                                 accum_out=rsum[:, j:j + 1]).then_inc(a_exp, 1)
                                eng.wait_ge(a_df, n + 1)
                                A.activation(es, es, ACT.Exp).then_inc(a_es, 1)
                        else:
                            if n < N_SSD:
                                g, cc = n // NT, n % NT
                                eng.wait_ge(d_ab[n % 2], 16 * (n // 2 + 1))
                                if n >= 2:
                                    eng.wait_ge(d_y, n - 1)
                                A.activation(cdec[:, n % 2, :], ag[:, n % 2, :, P - 1], ACT.Exp).then_inc(d_cd, 1)
                                eng.wait_ge(d_dd, n + 1)
                                A.activation(dd8, dd8, ACT.Exp).then_inc(d_de, 1)
                                eng.wait_ge(d_bc, n + 1)
                                if n:
                                    eng.wait_ge(d_m, n)
                                    eng.wait_ge(d_mm, n)
                                A.activation(bncb[:, :], PS[:, 3, 0:2 * P], ACT.Copy).then_inc(d_bcs, 1)
                                eng.wait_ge(d_e2[n % 2], 32 * (n // 2 + 1))
                                A.activation(e2[:, n % 2, :, :], e2[:, n % 2, :, :], ACT.Exp).then_inc(d_e2x, 1)
                                eng.wait_ge(d_gm, n + 1)
                                for hd in range(HG):
                                    ins = A.activation(ag[:, n % 2, hd, :], ag[:, n % 2, hd, :], ACT.Exp,
                                                       bias=nacs[:, cc, HG * g + hd:HG * g + hd + 1])
                                ins.then_inc(d_exp, 1)
                            if 1 <= n <= N_SSD:
                                k = n - 1
                                g, cc = k // NT, k % NT
                                eng.wait_ge(d_y, k + 1)
                                if k:
                                    eng.wait_ge(d_s1, k)
                                A.activation(sq[:, :].rearrange("p (i l) -> p i l", i=TG),
                                             sz[:, TG * g:TG * g + TG, cc * P:(cc + 1) * P],
                                             ACT.Square).then_inc(d_sq, 1)
                            if n >= 2 and (n - 2) % NT == NT - 1:
                                g = (n - 2) // NT
                                eng.wait_ge(d_sum, n - 1)
                                if g:
                                    eng.wait_ge(g_w, TG * g)
                                A.activation(gsd[:, :], PS[:, 7, :], ACT.Sqrt, bias=epsc,
                                             scale=1.0 / (TG * P)).then_inc(g_sd, 1)
                                for t in range(TG):
                                    eng.wait_ge(g_w, TG * g + t + 1)
                                    A.activation(y_hi[:, TG * g + t, :], sz[:, TG * g + t, :],
                                                 ACT.Copy).then_inc(g_hi, 1)
                if kind == "out" and i == 3:
                    for t in range(NT):
                        eng.wait_ge(h_add, NT + t + 1)
                        A.activation(hjunk[:, :], h[:, t, :], ACT.Square, accum_out=hss[:, t:t + 1]).then_inc(n_sq, 1)
                        eng.wait_ge(n_sq, NT + t + 1)
                        A.activation(hsd[:, t:t + 1], hss[:, t:t + 1], ACT.Sqrt, bias=epsc, scale=1.0 / D).then_inc(n_sd, 1)
                        if t:
                            norm_hi(t - 1)
                    norm_hi(NT - 1)
            for t in range(NT):
                eng.wait_ge(dn_add, NT + t + 1)
                if t:
                    eng.wait_ge(f_sq, t)
                A.activation(fjunk[:, :], h[:, t, :], ACT.Square, accum_out=fss[:, t:t + 1]).then_inc(f_sq, 1)
                eng.wait_ge(f_sq, t + 1)
                A.activation(fsd[:, t:t + 1], fss[:, t:t + 1], ACT.Sqrt, bias=epsc, scale=1.0 / D).then_inc(f_sd, 1)

        @block.vector
        def _(eng):
            V = nc.vector

            def bcast(cols, n, width):
                return cols.unsqueeze(2).broadcast_to([P, n, width])

            def split(c):
                eng.wait_ge(w_rounded, c + 1)
                n = chunk_len(c)
                V.tensor_tensor(wlo[:, c % 2, 0:n], raw[:, c % 2, 0:n], f32(whi[:, c % 2, 0:n]),
                                ALU.subtract).then_inc(w_split, 1)

            def norm_scale(t, k, src, root, inv, dst):
                eng.wait_ge(n_sd, k + 1)
                V.reciprocal(inv[:, t:t + 1], root[:, t:t + 1]).then_inc(n_rs, 1)
                eng.wait_ge(n_rs, k + 1)
                if k:
                    eng.wait_ge(n_tp, k)
                V.tensor_scalar(dst, src, inv[:, t:t + 1], None, ALU.mult).then_inc(n_sc, 1)

            def norm_weight(t, k, dst, w):
                eng.wait_ge(n_tp, k + 1)
                if k:
                    eng.wait_ge(n_lo, k)
                b = 4 + 2 * (t % 2)
                V.tensor_tensor(dst.rearrange("p (k l) -> p k l", k=KT),
                                PS[:, b:b + 2, :].rearrange("p b (k l) -> p (b k) l", l=P),
                                bcast(w, KT, P), ALU.mult).then_inc(n_tw, 1)

            def norm_lo(t, k, src, hi, lo):
                eng.wait_ge(n_hi, k + 1)
                V.tensor_tensor(lo[:, :, t * P:(t + 1) * P], src.rearrange("p (k l) -> p k l", k=KT),
                                f32(hi[:, :, t * P:(t + 1) * P]), ALU.subtract).then_inc(n_lo, 1)

            eng.wait_ge(pcols_t, 3)
            for i, n in enumerate((P, P, 88)):
                V.tensor_copy(pcol[:, i, 0:n], PS[:, i, 0:n]).then_inc(pcols, 1)
            eng.wait_ge(pcols, 3)
            V.tensor_scalar(cwh[:, 0:5 * NX], pcol[:, 0, 0:5 * NX], 0.5, None, ALU.mult).then_inc(pcols, 1)
            V.tensor_scalar(bgh[:, :], pcol[:, 1, bg0:bg0 + 16], 0.5, None, ALU.mult).then_inc(pcols, 1)
            for k in range(4):
                o = (k % 2) * 2 * FT + FT
                V.tensor_scalar(fwh[:, k, :], pcol[:, 1 + k // 2, o:o + FT], 0.5, None, ALU.mult).then_inc(pcols, 1)
            for hh in range(2):
                V.tensor_copy(dsk[hh * HD:(hh + 1) * HD, :], dskb[hh * HD:(hh + 1) * HD, hh:NH:2]).then_inc(pcols, 1)
            for t in range(NT):
                norm_scale(t, t, xnat[:, t, :], sd, rs, xsc[:, :])
                if t:
                    norm_weight(t - 1, t - 1, xt[:, :], n1w)
                    norm_lo(t - 1, t - 1, xt[:, :], xn_hi, xn_lo)
            norm_weight(NT - 1, NT - 1, xt[:, :], n1w)
            norm_lo(NT - 1, NT - 1, xt[:, :], xn_hi, xn_lo)
            split(0)
            k_conv = k_z = n_sp = n_yo = n_yx = n_stm = 0
            for c, (kind, i) in enumerate(CHUNKS):
                if c + 1 < len(CHUNKS):
                    split(c + 1)
                if kind == "vd" and i == 1:
                    for t in range(NT):
                        eng.wait_ge(gemm_done, DONE[c, t])
                        V.tensor_copy(v[:, t, :], PS[:, 4 + t, 0:HKV * HD]).then_inc(v_ready, 1)
                        if t == 0:
                            eng.wait_ge(params_in, 16 * 13)
                        V.tensor_tensor(dtr[:, t, :], PS[:, 4 + t, HKV * HD:VW], dtb[:, :],
                                        ALU.add).then_inc(v_ready, 1)
                    X = dtr[:, :, :].rearrange("p t h -> p (t h)")
                    e, z, w, pl, r, q_ = (s_[:, :] for s_ in sp)
                    eng.wait_ge(v_ready, 2 * NT)
                    V.tensor_scalar(q_, X, -1.0, None, ALU.mult).then_inc(spd, 1)
                    eng.wait_ge(spd, 1)
                    V.tensor_tensor(e, X, q_, ALU.max).then_inc(spc, 1)
                    eng.wait_ge(spa, 2)

                    def chained(ins):
                        nonlocal n_sp
                        n_sp += 1
                        ins.then_inc(spd, 1)
                        eng.wait_ge(spd, n_sp + 1)

                    chained(V.tensor_scalar(r, e, 2.0, None, ALU.add))
                    chained(V.reciprocal(r, r))
                    chained(V.tensor_tensor(z, e, r, ALU.mult))
                    chained(V.tensor_tensor(w, z, z, ALU.mult))
                    chained(V.tensor_scalar(pl, w, 1.0 / 17, 1.0 / 15, ALU.mult, ALU.add))
                    for k in (13, 11, 9, 7, 5, 3, 1):
                        chained(V.tensor_tensor(pl, pl, w, ALU.mult))
                        chained(V.tensor_scalar(pl, pl, 1.0 / k, None, ALU.add))
                    chained(V.scalar_tensor_tensor(out=pl, in0=z, scalar=2.0, in1=pl, op0=ALU.mult, op1=ALU.mult))
                    chained(V.tensor_scalar(r, X, 0.0, None, ALU.max))
                    chained(V.tensor_tensor(dt[:, :, :].rearrange("p t h -> p (t h)"), r, pl, ALU.add))
                    V.scalar_tensor_tensor(out=q_.rearrange("p (t h) -> p t h", t=NT), in0=dt[:, :, :], scalar=-1.0,
                                           in1=nA[:, :].unsqueeze(1).broadcast_to([P, NT, NH]),
                                           op0=ALU.mult, op1=ALU.mult).then_inc(da_ready, 1)
                if kind in FORM_B and kind != "vd":
                    add, nh, last = (h_add, i // 2, i % 2 == 1) if kind == "out" else (dn_add, i // 6, i % 6 == 5)
                    if last:
                        for t in range(NT):
                            eng.wait_ge(gemm_done, DONE[c, t])
                            if kind == "out" and nh == 0 and t == 0:
                                eng.wait_ge(h_in, 16)
                            hv = h[:, t, nh * 512:nh * 512 + 512]
                            V.tensor_tensor(hv, hv, PS[:, (4, 0)[nh] + t, :], ALU.add).then_inc(add, 1)
                            if kind == "out" and nh == 1:
                                if t:
                                    norm_scale(t - 1, NT + t - 1, h[:, t - 1, :], hsd, hrs, hsc[:, :])
                                if t > 1:
                                    norm_weight(t - 2, NT + t - 2, ht[:, :], n2w)
                                    norm_lo(t - 2, NT + t - 2, ht[:, :], hn_hi, hn_lo)
                        if kind == "out" and nh == 1:
                            norm_scale(NT - 1, 2 * NT - 1, h[:, NT - 1, :], hsd, hrs, hsc[:, :])
                            for t in (NT - 2, NT - 1):
                                norm_weight(t, NT + t, ht[:, :], n2w)
                                norm_lo(t, NT + t, ht[:, :], hn_hi, hn_lo)
                    continue
                for u in range(2):
                    b = PS[:, u, :]
                    if kind in ("bc", "xs"):
                        t = 2 * i + u + (16 if kind == "bc" else 0)
                        acc = cacc[:, u, :]
                        eng.wait_ge(c_acc, k_conv + 1)
                        for back in (1, 2, 3):
                            if back > 1:
                                eng.wait_ge(c_tap, 3 * k_conv + back - 1)
                            V.scalar_tensor_tensor(out=acc[:, back:SEQ], in0=b[:, 0:SEQ - back], scalar=CW(3 - back, t),
                                                   in1=acc[:, back:SEQ], op0=ALU.mult, op1=ALU.add).then_inc(c_tap, 1)
                        eng.wait_ge(c_tanh, k_conv + 1)
                        dst = bc[:, t - 16, :] if kind == "bc" else xs[:, t, :]
                        V.scalar_tensor_tensor(out=dst, in0=cth[:, u, :], scalar=1.0, in1=acc,
                                               op0=ALU.add, op1=ALU.mult).then_inc(c_out, 1)
                        k_conv += 1
                    elif kind == "z":
                        eng.wait_ge(z_tanh, k_z + 1)
                        if k_z == 0:
                            eng.wait_ge(acs_out, 16)
                        V.scalar_tensor_tensor(out=sz[:, 2 * i + u, :], in0=cth[:, u, :], scalar=1.0, in1=b,
                                               op0=ALU.add, op1=ALU.mult).then_inc(z_out, 1)
                        k_z += 1
                    elif kind == "ao":
                        eng.wait_ge(gemm_done, DONE[c, u])
                        eng.wait_ge(g_tanh, 2 * i + u + 1)
                        if i:
                            eng.wait_ge(ao_sp[u], 16 * i)
                        V.scalar_tensor_tensor(out=cacc[:, u, :], in0=cth[:, u, :], scalar=1.0, in1=b,
                                               op0=ALU.add, op1=ALU.mult).then_inc(ao_out, 1)
                    elif kind == "so" and i[1] == 1:
                        f = 2 * i[0] + u
                        eng.wait_ge(gemm_done, DONE[c, u])
                        eng.wait_ge(so_in[u], 32 * (i[0] + 1))
                        V.scalar_tensor_tensor(out=cth[:, u, :], in0=cth[:, u, :], scalar=1.0,
                                               in1=PS[:, 2 * (i[0] % 2) + u, :], op0=ALU.add, op1=ALU.mult).then_inc(so_g, 1)
                        eng.wait_ge(so_g, f + 1)
                        V.tensor_tensor(cacc[:, u, :], cacc[:, u, :], cth[:, u, :], ALU.add).then_inc(so_a, 1)
                        eng.wait_ge(so_hi, f + 1)
                        V.scalar_tensor_tensor(out=mix_lo[:, f, :], in0=cacc[:, u, :], scalar=0.5, in1=f32(mix_hi[:, f, :]),
                                               op0=ALU.mult, op1=ALU.subtract).then_inc(so_lo, 1)
                    elif kind == "up":
                        k, it = 2 * i + u, i // 2
                        t = (i % 2) * FT + 2 * it + u
                        acc = ga2[:, u, :] if i % 2 else cacc[:, u, :]
                        eng.wait_ge(u_acc, k + 1)
                        for back in (1, 2):
                            if back > 1:
                                eng.wait_ge(u_tap, 2 * k + 1)
                            V.scalar_tensor_tensor(out=acc[:, back:SEQ], in0=PS[:, 2 * (i % 2) + u, 0:SEQ - back],
                                                   scalar=FW(2 - back, t), in1=acc[:, back:SEQ],
                                                   op0=ALU.mult, op1=ALU.add).then_inc(u_tap, 1)
                        if i % 2:
                            f = 2 * it + u
                            eng.wait_ge(u_tanh, f + 1)
                            V.scalar_tensor_tensor(out=acc, in0=cth[:, u, :], scalar=1.0, in1=acc,
                                                   op0=ALU.add, op1=ALU.mult).then_inc(u_silu, 1)
                            eng.wait_ge(u_silu, f + 1)
                            V.tensor_tensor(acc, acc, cacc[:, u, :], ALU.mult).then_inc(u_mul, 1)
                            eng.wait_ge(u_hi, f + 1)
                            V.tensor_tensor(act_lo[:, f, :], acc, f32(act_hi[:, f, :]), ALU.subtract).then_inc(u_lo, 1)
                    for what, n in RIDES.get((c, u), []):
                        if what == "acs" and n == 1:
                            eng.wait_ge(acs_tp, 1)
                            V.tensor_scalar(nacs[:, :, :].rearrange("p t h -> p (t h)"), PS[:, 3, 0:NT * NH],
                                            -1.0, None, ALU.mult).then_inc(acs_nat, 1)
                        if what == "att":
                            g, b_ = n % HKV, n // HKV
                            if n < N_ATT:
                                eng.wait_ge(a_cur, n + 1)
                                if b_:
                                    prev = PS[:, 2 + 2 * (n % 2):4 + 2 * (n % 2), :].rearrange(
                                        "p b (j s) -> p (b j) s", j=2)[:, :, 0:P]
                                else:
                                    prev = negt[:, :].unsqueeze(1).broadcast_to([P, GQ, P])
                                V.copy_predicated(S[:, :, :], mprev[:, :].unsqueeze(1).broadcast_to([P, GQ, P]),
                                                  prev).then_inc(a_sel, 1)
                                eng.wait_ge(a_sel, n + 1)
                                V.tensor_reduce(mx, S[:, :, :], AX.X, ALU.max).then_inc(a_max, 1)
                                eng.wait_ge(a_max, n + 1)
                                V.tensor_tensor(m_, mx, snk[:, GQ * g:GQ * g + GQ], ALU.max).then_inc(a_m, 1)
                                eng.wait_ge(a_m, n + 1)
                                V.tensor_scalar(nm, m_, -1.0, None, ALU.mult).then_inc(a_nm, 1)
                                V.tensor_tensor(es, snk[:, GQ * g:GQ * g + GQ], m_, ALU.subtract).then_inc(a_df, 1)
                            if 1 <= n <= N_ATT:
                                k = n - 1
                                eng.wait_ge(a_pt, k + 1)
                                if k:
                                    eng.wait_ge(a_pv, k)
                                V.tensor_tensor(ptc[:, :, :], pt[:, :, :], tri[:, :].unsqueeze(1).broadcast_to([P, GQ, P]),
                                                ALU.mult).then_inc(a_ptc, 1)
                            if n >= 2:
                                k = n - 2
                                g2, b2 = k % HKV, k // HKV
                                o = (g2 % 2) * HD
                                tl = slice((g2 // 2) * GQ, (g2 // 2) * GQ + GQ)
                                eng.wait_ge(a_oh, k + 1)
                                V.tensor_tensor(a_lo[o:o + HD, tl, b2 * P:(b2 + 1) * P],
                                                PS[o:o + HD, 7, :].rearrange("p (j q) -> p j q", j=GQ),
                                                f32(a_hi[o:o + HD, tl, b2 * P:(b2 + 1) * P]), ALU.subtract).then_inc(a_ol, 1)
                            if n < N_ATT:
                                eng.wait_ge(a_exp, GQ * (n + 1))
                                eng.wait_ge(a_es, n + 1)
                                V.tensor_tensor(den, rsum, es, ALU.add).then_inc(a_den, 1)
                                eng.wait_ge(a_den, n + 1)
                                V.reciprocal(rden, den).then_inc(a_rd, 1)
                                eng.wait_ge(a_rd, n + 1)
                                V.tensor_tensor(Pr[:, :, :], Pr[:, :, :], bcast(rden, GQ, P), ALU.mult).then_inc(a_pr, 1)
                        if what == "ssd":
                            g, cc = n // NT, n % NT
                            hs = slice(HG * g, HG * g + HG)
                            if n < N_SSD:
                                eng.wait_ge(d_ab[n % 2], 16 * (n // 2 + 1))
                                if n:
                                    eng.wait_ge(d_ddt, n)
                                V.tensor_tensor(dd8, ag[:, n % 2, :, P - 1], nacs[:, cc, hs], ALU.add).then_inc(d_dd, 1)
                            if 1 <= n <= N_SSD:
                                k = n - 1
                                gk, ck = k // NT, k % NT
                                eng.wait_ge(d_mm, k + 1)
                                sv = st[:, :].rearrange("p (h q) -> p h q", h=HG)
                                if ck == 0:
                                    V.tensor_copy(st[:, :], PS[:, 6, :]).then_inc(d_stp, 1)
                                elif ck < NT - 1:
                                    V.tensor_tensor(sv, sv, bcast(cdec[:, k % 2, :], HG, HD), ALU.mult).then_inc(d_stm, 1)
                                    n_stm += 1
                                    eng.wait_ge(d_stm, n_stm)
                                    V.tensor_tensor(st[:, :], st[:, :], PS[:, 6, :], ALU.add).then_inc(d_stp, 1)
                            if n < N_SSD:
                                eng.wait_ge(d_de, n + 1)
                                V.tensor_tensor(ddt[:, n % 2, :], dd8, dt[:, cc, hs], ALU.mult).then_inc(d_ddt, 1)
                                eng.wait_ge(d_x, n + 1)
                                xv = PS[:, 2, :].rearrange("p (h q) -> p h q", h=HG)
                                V.tensor_tensor(xc[:, :].rearrange("p (h q) -> p h q", h=HG), xv,
                                                bcast(dt[:, cc, hs], HG, HD), ALU.mult).then_inc(d_xc, 1)
                                eng.wait_ge(d_ddt, n + 1)
                                V.tensor_tensor(xcd[:, :].rearrange("p (h q) -> p h q", h=HG), xv,
                                                bcast(ddt[:, n % 2, :], HG, HD), ALU.mult).then_inc(d_xcd, 1)
                            if 1 <= n <= N_SSD:
                                yv = yo[:, :].rearrange("p (i l) -> p i l", i=TG)
                                dg = PS[:, 5, :].rearrange("p (i l) -> p i l", i=TG)
                                xsv = xs[:, TG * gk:TG * gk + TG, ck * P:(ck + 1) * P]
                                szv = sz[:, TG * gk:TG * gk + TG, ck * P:(ck + 1) * P]
                                eng.wait_ge(d_dxs, k + 1)
                                if ck:
                                    eng.wait_ge(d_e2x, k + 1)
                                    V.tensor_tensor(yv, PS[:, 4, :].rearrange("p (i l) -> p i l", i=TG),
                                                    e2[:, k % 2, :, :], ALU.mult).then_inc(d_yo, 1)
                                    n_yo += 1
                                    eng.wait_ge(d_yo, n_yo)
                                    V.tensor_tensor(yv, yv, xsv, ALU.add).then_inc(d_yx, 1)
                                    n_yx += 1
                                    eng.wait_ge(d_yx, n_yx)
                                    V.tensor_tensor(yv, yv, dg, ALU.add).then_inc(d_yd, 1)
                                else:
                                    V.tensor_tensor(yv, xsv, dg, ALU.add).then_inc(d_yd, 1)
                                eng.wait_ge(d_yd, k + 1)
                                V.scalar_tensor_tensor(out=szv, in0=yv, scalar=0.5, in1=szv,
                                                       op0=ALU.mult, op1=ALU.mult).then_inc(d_y, 1)
                            if n < N_SSD:
                                eng.wait_ge(d_exp, n + 1)
                                eng.wait_ge(d_bcs, n + 1)
                                V.tensor_tensor(ag[:, n % 2, :, :], ag[:, n % 2, :, :],
                                                bncb[:, P:2 * P].unsqueeze(1).broadcast_to([P, HG, P]),
                                                ALU.mult).then_inc(d_m, 1)
                            if n >= 2 and (n - 2) % NT == NT - 1:
                                gg = (n - 2) // NT
                                eng.wait_ge(g_sd, gg + 1)
                                V.reciprocal(gsd[:, :], gsd[:, :]).then_inc(g_rs, 1)
                                eng.wait_ge(g_rs, gg + 1)
                                for t in range(TG):
                                    f = TG * gg + t
                                    V.scalar_tensor_tensor(out=sz[:, f, :], in0=sz[:, f, :], scalar=snw[:, f:f + 1],
                                                           in1=gsd[:, :], op0=ALU.mult, op1=ALU.mult).then_inc(g_w, 1)
                                for t in range(TG):
                                    f = TG * gg + t
                                    eng.wait_ge(g_hi, f + 1)
                                    V.tensor_tensor(y_lo[:, f, :], sz[:, f, :], f32(y_hi[:, f, :]),
                                                    ALU.subtract).then_inc(g_lo, 1)
            eng.wait_ge(fnw_in, 16)
            for t in range(NT):
                eng.wait_ge(f_sd, t + 1)
                V.reciprocal(frs[:, t:t + 1], fsd[:, t:t + 1]).then_inc(f_rs, 1)
                eng.wait_ge(f_rs, t + 1)
                if t >= 2:
                    eng.wait_ge(f_st[t % 2], 16)
                V.scalar_tensor_tensor(out=fo[:, t % 2, :], in0=h[:, t, :], scalar=frs[:, t:t + 1], in1=fnw[:, :],
                                       op0=ALU.mult, op1=ALU.mult).then_inc(f_out, 1)

        @block.tensor
        def _(eng):
            T = nc.tensor
            freed_by = {}

            def take(b, sem_, value):
                if b in freed_by:
                    eng.wait_ge(*freed_by[b])
                freed_by[b] = (sem_, value)

            def three(out_, w, m, first, last):
                T.matmul(out_, w[0], m[0], start=first, stop=False)
                T.matmul(out_, w[0], m[1], start=False, stop=False)
                return T.matmul(out_, w[1], m[0], start=False, stop=last)

            eng.wait_ge(consts, 13)
            eng.wait_ge(params_in, 16 * 13)
            for i, n in enumerate((P, P, 88)):
                take(i, pcols, 3)
                T.transpose(PS[:, i, 0:n], stage[0:n, i, :], ident[0:n, 0:n]).then_inc(pcols_t, 1)

            def norm_transposes(t, k, src):
                b = 4 + 2 * (t % 2)
                eng.wait_ge(n_sc, k + 1)
                take(b, n_tw, k + 1)
                take(b + 1, n_tw, k + 1)
                for kt in range(KT):
                    ins = T.transpose(PS[:, b + kt // 4, (kt % 4) * P:(kt % 4 + 1) * P], src[:, kt * P:(kt + 1) * P], ident[:, :])
                ins.then_inc(n_tp, 1)

            for t in range(NT):
                norm_transposes(t, t, xsc)
            eng.wait_ge(n_lo, NT)
            k_conv = k_z = 0
            acc_open = {}
            for c, (kind, i) in enumerate(CHUNKS):
                s_ = c % 2
                wh, wl = whi[:, s_, :], wlo[:, s_, :]
                eng.wait_ge(w_split, c + 1)
                if kind in FORM_B:
                    if kind == "vd":
                        nk, width, k0, first, last = 4, VW, 4 * i, i == 0, i == 1
                        mh, ml, b0 = xn_hi, xn_lo, 4
                    elif kind == "out":
                        nk, width, k0, first, last = 4, 512, 4 * (i % 2), i % 2 == 0, i % 2 == 1
                        mh, ml, b0 = mix_hi, mix_lo, (4, 0)[i // 2]
                        eng.wait_ge(so_lo, k0 + 4)
                    else:
                        k0 = 4 * (i % 6)
                        nk, width, first, last = min(4, FT - k0), 512, i % 6 == 0, i % 6 == 5
                        mh, ml, b0 = act_hi, act_lo, (4, 0)[i // 6]
                        eng.wait_ge(u_lo, k0 + nk)
                    for t in range(NT):
                        if first:
                            if kind == "vd":
                                take(b0 + t, v_ready, 2 * t + 2)
                            else:
                                take(b0 + t, h_add if kind == "out" else dn_add, NT * (i // (2 if kind == "out" else 6)) + t + 1)
                        for kt in range(nk):
                            tok = slice(t * P, (t + 1) * P)
                            cols_ = slice(kt * width, (kt + 1) * width)
                            ins = three(PS[:, b0 + t, 0:width], (mh[:, k0 + kt, tok], ml[:, k0 + kt, tok]),
                                        (wh[:, cols_], wl[:, cols_]), first and kt == 0, last and kt == nk - 1)
                        ins.then_inc(gemm_done, 1)
                    if kind == "out" and i == 3:
                        for t in range(NT):
                            norm_transposes(t, NT + t, hsc)
                        eng.wait_ge(n_lo, 2 * NT)
                    continue
                for u in range(2):
                    b, k0, first, last = u, 0, True, True
                    mh, ml = xn_hi, xn_lo
                    if kind == "k":
                        take(b, qk_ready, u + 1)
                    elif kind == "q":
                        take(b, qk_ready, 2 + 2 * i + u + 1)
                    elif kind in ("bc", "xs"):
                        k_conv += 1
                        take(b, c_tap, 3 * k_conv)
                    elif kind == "z":
                        k_z += 1
                        take(b, z_out, k_z)
                    elif kind == "ga":
                        take(b, g_tanh, 2 * i + u + 1)
                    elif kind == "ao":
                        take(b, ao_out, 2 * i + u + 1)
                        mh, ml = a_hi, a_lo
                        if i == 0 and u == 0:
                            eng.wait_ge(a_ol, N_ATT)
                    elif kind == "gs":
                        take(b, gs_tanh, 2 * i + u + 1)
                    elif kind == "so":
                        b = 2 * (i[0] % 2) + u
                        mh, ml, k0 = y_hi, y_lo, KT * i[1]
                        first, last = i[1] == 0, i[1] == 1
                        if first:
                            take(b, so_g, 2 * i[0] + u + 1)
                    elif kind == "up":
                        b = 2 * (i % 2) + u
                        take(b, u_tap, 2 * (2 * i + u) + 2)
                        mh, ml = hn_hi, hn_lo
                    for kt in range(KT):
                        if kind == "so" and (k0 + kt) % TG == 0:
                            eng.wait_ge(g_lo, k0 + kt + TG)
                        w_ = slice(kt * 256 + u * P, kt * 256 + (u + 1) * P)
                        ins = three(PS[:, b, :], (wh[:, w_], wl[:, w_]), (mh[:, k0 + kt, :], ml[:, k0 + kt, :]),
                                    first and kt == 0, last and kt == KT - 1)
                    ins.then_inc(gemm_done, 1)
                    for what, n in RIDES.get((c, u), []):
                        if what == "acs" and n == 0:
                            eng.wait_ge(da_ready, 1)
                            take(2, acs_ev, 1)
                            for t in range(NT):
                                ins = T.matmul(PS[0:NH, 2, t * P:(t + 1) * P], sp[5][:, t * NH:(t + 1) * NH], tri[:, :],
                                               start=True, stop=True)
                            ins.then_inc(acs_mm, 1)
                        if what == "acs" and n == 1:
                            eng.wait_ge(acs_ev, 1)
                            take(3, acs_nat, 1)
                            for t in range(NT):
                                ins = T.transpose(PS[:, 3, t * NH:(t + 1) * NH], acsT[:, t * P:(t + 1) * P],
                                                  ident[0:NH, 0:NH])
                            ins.then_inc(acs_tp, 1)
                        if what == "att":
                            if n < N_ATT:
                                g, b_ = n % HKV, n // HKV
                                o = (g % 2) * HD
                                if n == 0:
                                    eng.wait_ge(qk_ready, 10)
                                for q_ in range(2):
                                    take(2 + 2 * (n % 2) + q_, a_sel, n + 1)
                                for j in range(GQ):
                                    bank = PS[:, 2 + 2 * (n % 2) + j // 2, :]
                                    c0 = (j % 2) * 2 * P + (0 if b_ else P)
                                    k0_ = max(b_ - 1, 0) * P
                                    ins = T.matmul(bank[:, c0:(j % 2 + 1) * 2 * P],
                                                   qT[o:o + HD, (g // 2) * GQ + j, b_ * P:(b_ + 1) * P],
                                                   kT[o:o + HD, g // 2, k0_:(b_ + 1) * P], start=True, stop=True)
                                ins.then_inc(a_sc, 1)
                            if 1 <= n <= N_ATT:
                                k = n - 1
                                eng.wait_ge(a_pr, k + 1)
                                take(6, a_pt, k + 1)
                                for j in range(GQ):
                                    ins = T.transpose(PS[:, 6, j * P:(j + 1) * P], Pr[:, j, :], ident[:, :])
                                ins.then_inc(a_tp, 1)
                            if n >= 2:
                                k = n - 2
                                g, b_ = k % HKV, k // HKV
                                o = (g % 2) * HD
                                eng.wait_ge(a_ptc, k + 1)
                                eng.wait_ge(a_ptp, k + 1)
                                take(7, a_ol, k + 1)
                                if b_:
                                    T.matmul(PS[o:o + HD, 7, :], v[:, b_ - 1, g * HD:(g + 1) * HD],
                                             ptp[:, :, :].rearrange("p j q -> p (j q)"), start=True, stop=False)
                                T.matmul(PS[o:o + HD, 7, :], v[:, b_, g * HD:(g + 1) * HD],
                                         ptc[:, :, :].rearrange("p j q -> p (j q)"), start=b_ == 0, stop=True).then_inc(a_pv, 1)
                        if what == "ssd":
                            if n < N_SSD:
                                g, cc = n // NT, n % NT
                                tok = slice(cc * P, (cc + 1) * P)
                                eng.wait_ge(c_out, 8 + 4 * (g + 1))
                                take(2, d_xcd, n + 1)
                                for t in range(TG):
                                    ins = T.transpose(PS[:, 2, t * P:(t + 1) * P], xs[:, TG * g + t, tok], ident[:, :])
                                ins.then_inc(d_x, 1)
                                take(3, d_bcs, n + 1)
                                T.transpose(PS[:, 3, 0:P], bc[:, g, tok], ident[:, :])
                                T.matmul(PS[:, 3, P:2 * P], bc[:, g, tok], bc[:, NG + g, tok], start=True,
                                         stop=True).then_inc(d_bc, 1)
                            if 1 <= n <= N_SSD:
                                k = n - 1
                                g, cc = k // NT, k % NT
                                tok = slice(cc * P, (cc + 1) * P)
                                if cc < NT - 1:
                                    eng.wait_ge(d_xcd, k + 1)
                                    eng.wait_ge(d_bcs, k + 1)
                                    take(6, d_stp, (NT - 1) * g + cc + 1)
                                    T.matmul(PS[:, 6, :], bncb[:, 0:P], xcd[:, :], start=True, stop=True)
                                if cc:
                                    eng.wait_ge(d_stp, (NT - 1) * g + cc)
                                    take(4, d_yd, k + 1)
                                    for t in range(TG):
                                        T.matmul(PS[:, 4, t * P:(t + 1) * P], st[:, t * P:(t + 1) * P],
                                                 bc[:, NG + g, tok], start=True, stop=True)
                                eng.wait_ge(d_m, k + 1)
                                eng.wait_ge(d_xc, k + 1)
                                take(5, d_yd, k + 1)
                                for hd in range(HG):
                                    o = (hd % 2) * HD
                                    ins = T.matmul(PS[o:o + HD, 5, (hd // 2) * P:(hd // 2 + 1) * P],
                                                   xc[:, hd * HD:(hd + 1) * HD], ag[:, k % 2, hd, :],
                                                   start=True, stop=True)
                                ins.then_inc(d_mm, 1)
                            if n >= 2:
                                k = n - 2
                                g, cc = k // NT, k % NT
                                eng.wait_ge(d_s2, k + 1)
                                if cc == 0:
                                    take(7, g_sd, g + 1)
                                T.matmul(PS[:, 7, cc * P:(cc + 1) * P], ones[:, :], sq2[:, :], start=True,
                                         stop=True).then_inc(d_sum, 1)


_INS = ["x", "norm1_w", "w_in", "b_gate", "attn_sinks", "w_attn_o", "ssd_conv_w", "ssd_conv_b", "dt_bias",
        "a_log", "d_skip", "ssd_norm_w", "w_ssd_o", "w_out", "norm2_w", "w_up", "ffn_conv_w", "ffn_conv_b",
        "w_down", "final_norm_w"]


def kernel(**inputs):
    import numpy as _np
    import concourse.bacc as _bacc
    from concourse import mybir as _mybir
    from concourse.bass_utils import run_bass_kernel_spmd as _run

    nc = _bacc.Bacc("TRN2", target_bir_lowering=False, num_devices=1)
    arrays, args = {}, []
    for name in _INS:
        a = _np.ascontiguousarray(inputs[name])
        arrays[f"in_{name}"] = a
        args.append(nc.dram_tensor(f"in_{name}", a.shape, _mybir.dt.from_np(a.dtype), kind="ExternalInput").ap())
    out = nc.dram_tensor("out_0", (1, SEQ, D), F32, kind="ExternalOutput").ap()
    hybrid_layer(nc, *args, out)
    r = _run(nc, [arrays], core_ids=[0])
    return r.results[0]["out_0"]
```

```python
import concourse.bass as bass
from concourse import mybir
from contextlib import ExitStack

F32 = mybir.dt.float32
F32R = mybir.dt.float32r
I32 = mybir.dt.int32
ALU = mybir.AluOpType
ACT = mybir.ActivationFunctionType
AX = mybir.AxisListType

P = 128
SEQ, D = 512, 1024
NT = SEQ // P
KT = D // P
HQ, HKV, HD = 16, 4, 64
GQ = HQ // HKV
DI = 2 * D
NH, NG, NS = 32, 4, 128
HG = NH // NG
TG = DI // NG // P
XBC = DI + 2 * NG * NS
FF = 2816
FT = FF // P
EPS = 1e-5
NEG = -1e30
Q0 = 0
K0 = Q0 + HQ * HD
V0 = K0 + HKV * HD
Z0 = V0 + HKV * HD
X0 = Z0 + DI
B0 = X0 + DI
DT0 = X0 + XBC
GA0 = DT0 + NH
GS0 = GA0 + D
CH = 2048
VW = HKV * HD + NH

CHUNKS = [("vd", 0), ("vd", 1), ("k", 0)] + [("q", i) for i in range(4)]
CHUNKS += [("bc", i) for i in range(4)]
CHUNKS += [("xs", 0), ("xs", 1), ("z", 0), ("z", 1), ("xs", 2), ("xs", 3), ("z", 2), ("z", 3)]
for _i in range(4):
    CHUNKS += [("ga", _i), ("ao", _i)]
CHUNKS += [("xs", 4), ("xs", 5), ("z", 4), ("z", 5), ("xs", 6), ("xs", 7), ("z", 6), ("z", 7)]
CHUNKS += [("gs", i) for i in range(4)]
for _i in range(2):
    CHUNKS += [("so", (2 * _i, 0)), ("so", (2 * _i + 1, 0)), ("so", (2 * _i, 1)), ("so", (2 * _i + 1, 1))]
CHUNKS += [("out", i) for i in range(4)]
CHUNKS += [("up", i) for i in range(22)]
CHUNKS += [("down", i) for i in range(12)]
AT = {ch: n for n, ch in enumerate(CHUNKS)}

FORM_B = ("vd", "out", "down")
DONE = {}
_n = 0
for _c, (_kind, _i) in enumerate(CHUNKS):
    for _p in range(4 if _kind in FORM_B else 2):
        _n += 1
        DONE[_c, _p] = _n
    DONE[_c] = _n

N_ATT = NT * HKV
N_SSD = NG * NT
RIDES = {}
RIDES[AT[("q", 1)], 1] = [("acs", 0)]
RIDES[AT[("q", 2)], 1] = [("acs", 1)]
_first = AT[("bc", 0)]
for _n in range(N_ATT + 2):
    _u = _n + _n // 3 + 1
    RIDES.setdefault((_first + _u // 2, _u % 2), []).append(("att", _n))


def ride(unit, what, n):
    RIDES.setdefault((unit // 2, unit % 2), []).append((what, n))


_w1, _w2 = 2 * AT[("ga", 0)], 2 * AT[("xs", 6)]
ride(_w1, "load", 0)
ride(_w1, "dec", 0)
for _n in range(N_SSD):
    _u = _w1 + 1 + 2 * _n if _n < 8 else _w2 + 2 * (_n - 8)
    if _n == 8:
        ride(_w2 - 2, "load", _n)
        ride(_w2 - 1, "dec", _n)
    ride(_u, "s1", _n)
    if _n and _n != 8:
        ride(_u, "sum", _n - 1)
        if _n % NT == 0:
            ride(_u, "gend", _n // NT - 1)
    if _n not in (7, 15):
        ride(_u, "load", _n + 1)
    ride(_u + 1, "s2", _n)
    if _n not in (7, 15):
        ride(_u + 1, "dec", _n + 1)
    if _n in (7, 15):
        ride(_u + 2, "sum", _n)
        ride(_u + 2, "gend", _n // NT)


def hybrid_layer(nc, x, norm1_w, w_in, b_gate, attn_sinks, w_attn_o, ssd_conv_w, ssd_conv_b, dt_bias,
                 a_log, d_skip, ssd_norm_w, w_ssd_o, w_out, norm2_w, w_up, ffn_conv_w, ffn_conv_b,
                 w_down, final_norm_w, out):
    ctx = ExitStack()
    with ctx:
        base = 16512

        def sb(name, shape, kb, dt=F32):
            return nc.alloc_sbuf_tensor_at(name, shape, dt, offset=base + int(kb * 1024))

        xn_hi = sb("xn_hi", [P, KT, SEQ], 0, F32R)
        xn_lo = sb("xn_lo", [P, KT, SEQ], 16, F32R)
        raw = sb("w_raw", [P, 2, CH], 32)
        whi = sb("w_hi", [P, 2, CH], 48, F32R)
        wlo = sb("w_lo", [P, 2, CH], 64, F32R)
        xs = sb("xs", [P, 16, SEQ], 80)
        y_hi = sb("y_hi", [P, 16, SEQ], 80, F32R)
        sz = sb("sz", [P, 16, SEQ], 112)
        y_lo = sb("y_lo", [P, 16, SEQ], 112, F32R)
        bc = sb("bc", [P, 2 * NG, SEQ], 144)
        qT = sb("qT", [P, 8, SEQ], 160)
        a_hi = sb("a_hi", [P, 8, SEQ], 160, F32R)
        a_lo = sb("a_lo", [P, 8, SEQ], 96, F32R)
        kT = sb("kT", [P, 2, SEQ], 176)
        v = sb("v", [P, NT, HKV * HD], 180)
        cacc = sb("conv_acc", [P, 2, SEQ], 184)
        cth = sb("conv_tanh", [P, 2, SEQ], 188)
        xnat = sb("x_nat", [P, NT, D], 112)
        xsc = sb("x_scaled", [P, D], 128)
        xt = sb("x_t", [P, D], 132)
        junk = sb("junk", [P, D], 136)
        stage = sb("param_rows", [P, 3, P], 140)
        dskb = sb("d_skip_rows", [P, NH], 141.5)
        sp = [sb(f"softplus{i}", [P, NT * NH], 112 + 0.5 * i) for i in range(6)]
        acsT = sb("acs_t", [NH, SEQ], 116)
        S = sb("scores", [P, GQ, P], 128)
        Pr = sb("probs", [P, GQ, P], 130)
        pt = sb("probs_t", [P, GQ, P], 132)
        ptc = sb("probs_t_cur", [P, GQ, P], 134)
        ptp = sb("probs_t_prev", [P, GQ, P], 136)
        ag_of = [sb(f"decay{i}", [P, 3, HG, P], o) for i, o in enumerate((128, 160))]
        xc_of = [sb(f"xdt{i}", [P, SEQ], o) for i, o in enumerate((140, 172))]
        xcd_of = [sb(f"xdt_decayed{i}", [P, SEQ], o) for i, o in enumerate((142, 174))]
        e2 = sb("decay_off", [P, TG, P], 176)
        st = sb("state", [P, SEQ], 178)
        yo = sb("y_off", [P, SEQ], 180)
        bncb = sb("b_nat_cb", [P, 2 * P], 182)
        cbm = sb("cb_masked", [P, P], 183)
        gsd = sb("group_rms", [P, SEQ], 203.5)
        sq1 = sb("y_sq_pair", [P, 2 * P], 205.5)
        sq2 = sb("y_sq_sum", [P, P], 206.5)
        mix_hi = sb("mix_hi", [P, KT, SEQ], 144, F32R)
        mix_lo = sb("mix_lo", [P, KT, SEQ], 160, F32R)
        h = sb("h", [P, NT, D], 0)
        hn_hi = sb("hn_hi", [P, KT, SEQ], 16, F32R)
        hn_lo = sb("hn_lo", [P, KT, SEQ], 80, F32R)
        hsc = sb("h_scaled", [P, D], 176)
        ht = sb("h_t", [P, D], 180)
        hjunk = sb("h_junk", [P, D], 96)
        act_hi = sb("act_hi", [P, FT, SEQ], 96, F32R)
        act_lo = sb("act_lo", [P, FT, SEQ], 140, F32R)
        ga2 = sb("gated", [P, 2, SEQ], 203.5)
        fnw = sb("final_norm_row", [P, D], 16)
        fo = sb("final_out", [P, 2, D], 20)
        fjunk = sb("f_junk", [P, D], 28)
        ident = sb("ident", [P, P], 192)
        ones = sb("ones", [P, P], 192.5)
        tri = sb("tri", [P, P], 193)
        mprevT = sb("mask_prev_t", [P, P], 194)
        mprev = sb("mask_prev", [P, P], 194.5, I32)
        negt = sb("neg_tile", [P, P], 195)
        pcol = sb("param_cols", [P, 3, P], 195.5)
        small = sb("small", [P, 512], 197)
        dt = sb("dt", [P, NT, NH], 199)
        nacs = sb("neg_acs", [P, NT, NH], 199.5)
        ddt = sb("dt_decay", [P, 2, HG], 200)
        cdec = sb("chunk_decay", [P, 2, HG], 200.125)
        dsk = sb("d_cols", [P, 16], 200.25)
        dtr = sb("dt_raw", [P, NT, NH], 200.5)
        nA = sb("neg_a", [P, NH], 201)
        dtb = sb("dt_bias", [P, NH], 201.25)
        cwh = sb("half_conv", [P, P], 201.5)
        fwh = sb("half_ffn", [P, 4, FT], 202)
        bgh = sb("half_gate_bias", [P, 16], 202.5)
        PS = ctx.enter_context(nc.psum_tensor("banks", [P, 8, 512], F32))

        NX = XBC // P
        CW = lambda k, t: cwh[:, k * NX + t:k * NX + t + 1]
        CB = lambda t: cwh[:, 4 * NX + t:4 * NX + t + 1]
        n1w = pcol[:, 0, 5 * NX:5 * NX + KT]
        n2w = pcol[:, 1, 4 * FT:4 * FT + KT]
        bg0 = 4 * FT + KT
        snw = pcol[:, 1, bg0 + 16:bg0 + 32]

        def FW(k, t):
            if t >= FT:
                return fwh[:, k, t - FT:t - FT + 1]
            if k < 2:
                return pcol[:, 1, k * 2 * FT + t:k * 2 * FT + t + 1]
            o = (k - 2) * 2 * FT + t
            return pcol[:, 2, o:o + 1]

        ss, sd, rs = small[:, 0:8], small[:, 8:16], small[:, 16:24]
        mx, m_, nm = small[:, 24:28], small[:, 28:32], small[:, 32:36]
        rsum, es, den, rden = small[:, 36:40], small[:, 40:44], small[:, 44:48], small[:, 48:52]
        snk = small[:, 52:68]
        epsc = small[:, 68:69]
        dd8 = small[:, 72:80]
        fss, fsd, frs = small[:, 80:84], small[:, 84:88], small[:, 88:92]
        hss, hsd, hrs = small[:, 92:96], small[:, 96:100], small[:, 100:104]

        acs_d = nc.dram_tensor("acs_scratch", [NH, SEQ], F32, kind="Internal").ap()
        mixa_d = nc.dram_tensor("mixa_scratch", [KT, P, SEQ], F32, kind="Internal").ap()
        gs_d = nc.dram_tensor("gs_scratch", [KT, P, SEQ], F32, kind="Internal").ap()

        def sem(name):
            return ctx.enter_context(nc.semaphore(name))

        x_in = [sem(f"x_in{t}") for t in range(NT)]
        params_in = sem("params_in")
        w_in_slot = [sem(f"w_loaded{i}") for i in range(2)]
        w_rounded, w_split = sem("w_rounded"), sem("w_split")
        consts = sem("consts")
        pcols_t, pcols = sem("param_transposed"), sem("params_ready")
        gemm_done = sem("gemm_done")
        n_sq, n_sd, n_rs, n_sc, n_tp, n_tw, n_hi, n_lo = [sem("n_" + s) for s in (
            "squared", "root", "rstd", "scaled", "transposed", "weighted", "hi", "lo")]
        qk_ready = sem("qk_ready")
        vd_done, v_ready = sem("vd_done"), sem("v_ready")
        spc, spa, spd, da_ready = sem("softplus_abs"), sem("softplus_exp"), sem("softplus_steps"), sem("da_ready")
        acs_mm, acs_ev, acs_out, acs_tp, acs_nat = [sem("acs_" + s) for s in ("mm", "copied", "stored", "t", "nat")]
        c_acc, c_tap, c_tanh, c_out = [sem("conv_" + s) for s in ("bias", "tap", "tanh", "out")]
        z_tanh, z_out = sem("z_tanh"), sem("z_out")
        g_tanh, ao_out, gs_tanh = sem("ga_tanh"), sem("ao_gated"), sem("gs_tanh")
        ao_sp = [sem(f"ao_spilled{j}") for j in range(2)]
        gs_sp = [sem(f"gs_spilled{j}") for j in range(2)]
        a_sc, a_cur, a_sel, a_max, a_m, a_nm, a_exp, a_es, a_den, a_rd, a_pr = [sem("att_" + s) for s in (
            "scores", "cur", "selected", "max", "m", "negm", "exp", "sink", "den", "rden", "probs")]
        a_df = sem("att_sinkdiff")
        a_tp, a_pt, a_ptc, a_ptp, a_pv, a_oh, a_ol = [sem("att_" + s) for s in (
            "transposed", "pt", "ptc", "ptp", "pv", "hi", "lo")]
        d_ab = [sem(f"ssd_acs_in{i}") for i in range(3)]
        d_e2 = sem("ssd_acs2_in")
        (d_x, d_bc, d_bcs, d_seg, d_cbm, d_exp, d_m, d_e2x, d_dd, d_de, d_cd, d_ddt, d_xc, d_xcd, d_dxs, d_stt, d_stm,
         d_mm, d_yo, d_yd, d_yx, d_y, d_sq, d_s1, d_s2, d_sum, d_stp) = [sem("ssd_" + s) for s in (
             "xs_t", "b_cb", "b_cb_copied", "seg", "cb_masked", "exp", "m", "e2", "dd", "dexp", "cdec", "ddt", "xc", "xcd",
             "dxs", "st_mm", "st_scaled", "diag", "yoff", "yadd", "yskip", "y", "sq", "sq1", "sq2", "sum", "state")]
        g_sd, g_rs, g_w, g_hi, g_lo = [sem("gnorm_" + s) for s in ("root", "rstd", "weighted", "hi", "lo")]
        so_in = [sem(f"so_in{j}") for j in range(2)]
        so_g, so_a, so_hi, so_lo = [sem("so_" + s) for s in ("gated", "added", "hi", "lo")]
        h_in = sem("h_x_in")
        out_done, h_add = sem("out_done"), sem("h_added")
        u_acc, u_tap, u_tanh, u_silu, u_mul, u_hi, u_lo = [sem("up_" + s) for s in (
            "bias", "tap", "tanh", "silu", "mul", "hi", "lo")]
        dn_done, dn_add = sem("down_done"), sem("down_added")
        f_sq, f_sd, f_rs, f_out, fnw_in = [sem("final_" + s) for s in ("squared", "root", "rstd", "weighted", "row_in")]
        f_st = [sem(f"final_stored{i}") for i in range(2)]

        win = w_in[0]

        def down_tiles(i):
            short = FT % 4
            kc = i % 6
            return (0, short) if kc == 0 else (short + 4 * (kc - 1), 4)

        def chunk_dmas(c):
            kind, i = CHUNKS[c]
            slot = raw[:, c % 2, :]

            def cols(w, k0, nk, c0, nc_):
                return w[k0 * P:(k0 + nk) * P, c0:c0 + nc_].rearrange("(t p) n -> p t n", p=P)

            a = slot.rearrange("p (t n) -> p t n", t=KT)
            b = slot.rearrange("p (t n) -> p t n", t=4)
            if kind == "k":
                return [(a, cols(win, 0, KT, K0, 256))]
            if kind == "q":
                res = []
                for u in range(2):
                    t = 2 * i + u
                    G, j = t // GQ, t % GQ
                    for hh in range(2):
                        c0 = Q0 + ((2 * G + hh) * GQ + j) * HD
                        res.append((a[:, :, u * P + hh * HD:u * P + (hh + 1) * HD], cols(win, 0, KT, c0, HD)))
                return res
            if kind == "vd":
                s = slot[:, 0:4 * VW].rearrange("p (t n) -> p t n", t=4)
                return [(s[:, :, 0:HKV * HD], cols(win, 4 * i, 4, V0, HKV * HD)),
                        (s[:, :, HKV * HD:VW], cols(win, 4 * i, 4, DT0, NH))]
            c0 = {"bc": B0, "xs": X0, "z": Z0, "ga": GA0, "gs": GS0}.get(kind)
            if c0 is not None:
                return [(a, cols(win, 0, KT, c0 + 256 * i, 256))]
            if kind == "ao":
                res = []
                for G in range(2):
                    for hh in range(2):
                        r0 = (2 * G + hh) * GQ * HD
                        src = w_attn_o[0][r0:r0 + GQ * HD, 256 * i:256 * i + 256].rearrange("(j d) n -> d j n", d=HD)
                        res.append((a[hh * HD:(hh + 1) * HD, G * GQ:(G + 1) * GQ, :], src))
                return res
            if kind == "so":
                f, kh = i
                return [(a, cols(w_ssd_o[0], KT * kh, KT, 256 * f, 256))]
            if kind == "out":
                return [(b, cols(w_out[0], 4 * (i % 2), 4, 512 * (i // 2), 512))]
            if kind == "up":
                return [(a, cols(w_up[0], 0, KT, (i % 2) * FF + 256 * (i // 2), 256))]
            if kind == "down":
                nh, (k0, nk) = i // 6, down_tiles(i)
                return [(b[:, 0:nk, :], cols(w_down[0], k0, nk, 512 * nh, 512))]

        def chunk_len(c):
            kind, i = CHUNKS[c]
            if kind == "vd":
                return 4 * VW
            if kind == "down":
                return down_tiles(i)[1] * 512
            return CH

        loads_before = []
        _cnt = [0, 0]
        for c in range(len(CHUNKS)):
            _cnt[c % 2] += 16 * len(chunk_dmas(c))
            loads_before.append(_cnt[c % 2])

        f32 = lambda t: t.bitcast(F32)
        block = ctx.enter_context(nc.Block())

        @block.sync
        def _(eng):
            for t in range(NT):
                eng.dma_start(xnat[:, t, :], x[0, t * P:(t + 1) * P, :]).then_inc(x_in[t], 16)
            for c in range(len(CHUNKS)):
                if c >= 2:
                    eng.wait_ge(w_split, c - 1)
                for dst, src in chunk_dmas(c):
                    eng.dma_start(dst, src).then_inc(w_in_slot[c % 2], 16)
                if c == AT[("so", (2, 1))]:
                    eng.wait_ge(gemm_done, DONE[AT[("gs", 3)]])
                    eng.dma_start(h[:, :, :], x[0].rearrange("(t p) n -> p t n", p=P)).then_inc(h_in, 16)
                if c == AT[("down", 3)]:
                    eng.wait_ge(gemm_done, DONE[AT[("up", 21)]])
                    eng.dma_start(fnw[:, :], final_norm_w.unsqueeze(0).broadcast_to([P, D])).then_inc(fnw_in, 16)
            for t in range(NT):
                eng.wait_ge(f_out, t + 1)
                eng.dma_start(out[0, t * P:(t + 1) * P, :], fo[:, t % 2, :]).then_inc(f_st[t % 2], 16)
            for i in range(2):
                eng.wait_ge(f_st[i], 16 * (NT // 2))

        @block.gpsimd
        def _(eng):
            n = [0]

            def made(ins):
                n[0] += 1
                ins.then_inc(consts, 1)

            for t_, val in ((ident, 0.0), (ones, 1.0), (tri, 1.0), (mprevT, 1.0), (negt, NEG)):
                made(eng.memset(t_[:, :], val))
            made(eng.memset(epsc, EPS))
            made(eng.memset(f32(mprev[:, :]), 1.0))
            eng.wait_ge(consts, 7)
            made(eng.affine_select(out=ident[:, :], in_=ident[:, :], compare_op=ALU.not_equal, fill=1.0, base=0,
                                   pattern=[[-1, P]], channel_multiplier=1))
            made(eng.affine_select(out=tri[:, :], in_=tri[:, :], compare_op=ALU.is_ge, fill=0.0, base=0,
                                   pattern=[[1, P]], channel_multiplier=-1))
            made(eng.affine_select(out=mprevT[:, :], in_=mprevT[:, :], compare_op=ALU.is_gt, fill=0.0, base=0,
                                   pattern=[[-1, P]], channel_multiplier=1))
            made(eng.affine_select(out=f32(mprev[:, :]), in_=f32(mprev[:, :]), compare_op=ALU.is_gt, fill=0.0,
                                   base=0, pattern=[[1, P]], channel_multiplier=-1))

            eng.wait_ge(acs_ev, 1)
            eng.dma_start(acs_d, acsT[:, :]).then_inc(acs_out, 16)

            for c, (kind, i) in enumerate(CHUNKS):
                if kind == "so" and i[1] == 1:
                    if i[0] == 0:
                        eng.wait_ge(c_out, 24)
                    for j in range(2):
                        f = 2 * i[0] + j
                        if i[0] == 0:
                            eng.wait_ge(ao_sp[j], 16 * 4)
                            eng.wait_ge(gs_sp[j], 16 * 4)
                        else:
                            eng.wait_ge(so_lo, 2 * (i[0] - 1) + j + 1)
                        eng.dma_start(cacc[:, j, :], mixa_d[f]).then_inc(so_in[j], 16)
                        eng.dma_start(cth[:, j, :], gs_d[f]).then_inc(so_in[j], 16)
                for u in range(2):
                    if kind == "ao":
                        eng.wait_ge(ao_out, 2 * i + u + 1)
                        eng.dma_start(mixa_d[2 * i + u], cacc[:, u, :]).then_inc(ao_sp[u], 16)
                    if kind == "gs":
                        eng.wait_ge(gs_tanh, 2 * i + u + 1)
                        eng.dma_start(gs_d[2 * i + u], cth[:, u, :]).then_inc(gs_sp[u], 16)
                    for what, n in RIDES.get((c, u), []):
                        if what == "att":
                            if 1 <= n <= N_ATT:
                                k = n - 1
                                eng.wait_ge(a_pt, k + 1)
                                if k:
                                    eng.wait_ge(a_pv, k)
                                eng.tensor_tensor(ptp[:, :, :], pt[:, :, :],
                                                  mprevT[:, :].unsqueeze(1).broadcast_to([P, GQ, P]),
                                                  ALU.mult).then_inc(a_ptp, 1)
                        elif what == "s1":
                            g, cc = n // NT, n % NT
                            eng.wait_ge(d_x, n + 1)
                            eng.wait_ge(pcols, 11)
                            v_ = xs[:, TG * g:TG * g + TG, cc * P:(cc + 1) * P]
                            eng.tensor_tensor(v_, v_, dsk[:, TG * g:TG * g + TG].unsqueeze(2)
                                              .broadcast_to([P, TG, P]), ALU.mult).then_inc(d_dxs, 1)
                        elif what == "s2":
                            eng.wait_ge(d_sq, n + 1)
                            if n:
                                eng.wait_ge(d_s2, n)
                            eng.tensor_tensor(sq1[:, :], yo[:, 0:2 * P], yo[:, 2 * P:4 * P], ALU.add).then_inc(d_s1, 1)
                            eng.wait_ge(d_s1, n + 1)
                            if n:
                                eng.wait_ge(d_sum, n)
                            eng.tensor_tensor(sq2[:, :], sq1[:, 0:P], sq1[:, P:2 * P], ALU.add).then_inc(d_s2, 1)

        @block.scalar
        def _(eng):
            A = nc.scalar
            rows = [
                (stage[0:96, 0, :], ssd_conv_w[0].rearrange("k (t p) -> (k t) p", p=P)),
                (stage[96:120, 0, :], ssd_conv_b[0].rearrange("(t p) -> t p", p=P)),
                (stage[120:128, 0, :], norm1_w[0].rearrange("(t p) -> t p", p=P)),
                (stage[0:88, 1, :], ffn_conv_w[0, 0:2].rearrange("k (t p) -> (k t) p", p=P)),
                (stage[88:96, 1, :], norm2_w[0].rearrange("(t p) -> t p", p=P)),
                (stage[96:112, 1, :], b_gate[0].rearrange("(t p) -> t p", p=P)),
                (stage[112:128, 1, :], ssd_norm_w[0].rearrange("(t p) -> t p", p=P)),
                (stage[0:44, 2, :], ffn_conv_w[0, 2].rearrange("(t p) -> t p", p=P)),
                (stage[44:88, 2, :], ffn_conv_b[0].rearrange("(t p) -> t p", p=P)),
                (dtb[:, :], dt_bias[0].unsqueeze(0).broadcast_to([P, NH])),
                (nA[:, :], a_log[0].unsqueeze(0).broadcast_to([P, NH])),
                (dskb[:, :], d_skip[0].unsqueeze(0).broadcast_to([P, NH])),
                (snk, attn_sinks[0].unsqueeze(0).broadcast_to([P, HQ])),
            ]
            for dst, src in rows:
                eng.dma_start(dst, src).then_inc(params_in, 16)

            def split(c):
                eng.wait_ge(w_in_slot[c % 2], loads_before[c])
                if c >= 2:
                    eng.wait_ge(gemm_done, DONE[c - 2])
                n = chunk_len(c)
                A.activation(whi[:, c % 2, 0:n], raw[:, c % 2, 0:n], ACT.Copy).then_inc(w_rounded, 1)

            def norm_hi(t):
                eng.wait_ge(n_tw, NT + t + 1)
                A.activation(hn_hi[:, :, t * P:(t + 1) * P], ht[:, :].rearrange("p (k l) -> p k l", k=KT),
                             ACT.Copy).then_inc(n_hi, 1)

            for t in range(NT):
                eng.wait_ge(x_in[t], 16)
                if t == 0:
                    eng.wait_ge(consts, 11)
                else:
                    eng.wait_ge(n_sq, t)
                A.activation(junk[:, :], xnat[:, t, :], ACT.Square, accum_out=ss[:, t:t + 1]).then_inc(n_sq, 1)
                eng.wait_ge(n_sq, t + 1)
                A.activation(sd[:, t:t + 1], ss[:, t:t + 1], ACT.Sqrt, bias=epsc, scale=1.0 / D).then_inc(n_sd, 1)
            for t in range(NT):
                eng.wait_ge(n_tw, t + 1)
                A.activation(xn_hi[:, :, t * P:(t + 1) * P], xt[:, :].rearrange("p (k l) -> p k l", k=KT),
                             ACT.Copy).then_inc(n_hi, 1)
            eng.wait_ge(params_in, 16 * 13)
            A.activation(nA[:, :], nA[:, :], ACT.Exp).then_inc(spa, 1)
            split(0)
            k_conv = k_z = k_gs = 0
            for c, (kind, i) in enumerate(CHUNKS):
                if c + 1 < len(CHUNKS):
                    split(c + 1)
                for u in range(2):
                    if kind in ("k", "q"):
                        eng.wait_ge(gemm_done, DONE[c, u])
                        if kind == "k":
                            A.activation(kT[:, u, :], PS[:, u, :], ACT.Copy).then_inc(qk_ready, 1)
                        else:
                            A.activation(qT[:, 2 * i + u, :], PS[:, u, :], ACT.Copy,
                                         scale=HD ** -0.5).then_inc(qk_ready, 1)
                    elif kind in ("bc", "xs"):
                        t = 2 * i + u + (16 if kind == "bc" else 0)
                        eng.wait_ge(gemm_done, DONE[c, u])
                        if k_conv == 0:
                            eng.wait_ge(pcols, 11)
                        if kind == "xs" and i == 4:
                            eng.wait_ge(ao_sp[u], 16 * 4)
                        if k_conv >= 2:
                            eng.wait_ge(c_out, k_conv - 1)
                        A.activation(cacc[:, u, :], PS[:, u, :], ACT.Identity, bias=CB(t),
                                     scale=CW(3, t)).then_inc(c_acc, 1)
                        eng.wait_ge(c_tap, 3 * k_conv + 3)
                        A.activation(cth[:, u, :], cacc[:, u, :], ACT.Tanh).then_inc(c_tanh, 1)
                        k_conv += 1
                    elif kind == "z":
                        eng.wait_ge(gemm_done, DONE[c, u])
                        eng.wait_ge(c_out, k_conv)
                        if k_z >= 2:
                            eng.wait_ge(z_out, k_z - 1)
                        A.activation(cth[:, u, :], PS[:, u, :], ACT.Tanh, scale=0.5).then_inc(z_tanh, 1)
                        k_z += 1
                    elif kind == "ga":
                        eng.wait_ge(gemm_done, DONE[c, u])
                        eng.wait_ge(z_out, k_z)
                        if i:
                            eng.wait_ge(ao_out, 2 * (i - 1) + u + 1)
                        A.activation(cth[:, u, :], PS[:, u, :], ACT.Tanh, scale=0.5,
                                     bias=bgh[:, 2 * i + u:2 * i + u + 1]).then_inc(g_tanh, 1)
                    elif kind == "gs":
                        eng.wait_ge(gemm_done, DONE[c, u])
                        eng.wait_ge(z_out, k_z)
                        if i:
                            eng.wait_ge(gs_sp[u], 16 * i)
                        A.activation(cth[:, u, :], PS[:, u, :], ACT.Tanh, scale=0.5,
                                     bias=bgh[:, 8 + 2 * i + u:8 + 2 * i + u + 1]).then_inc(gs_tanh, 1)
                    elif kind == "so" and i[1] == 1:
                        f = 2 * i[0] + u
                        eng.wait_ge(so_a, f + 1)
                        A.activation(mix_hi[:, f, :], cacc[:, u, :], ACT.Copy, scale=0.5).then_inc(so_hi, 1)
                    elif kind == "up":
                        k = 2 * i + u
                        t = (i % 2) * FT + 2 * (i // 2) + u
                        b = 2 * (i % 2) + u
                        it = i // 2
                        dst = cacc[:, u, :] if i % 2 == 0 else ga2[:, u, :]
                        eng.wait_ge(gemm_done, DONE[c, u])
                        if it:
                            eng.wait_ge(u_lo if i % 2 else u_mul, 2 * (it - 1) + u + 1)
                        A.activation(dst, PS[:, b, :], ACT.Identity, bias=FW(3, t), scale=FW(2, t)).then_inc(u_acc, 1)
                        if i % 2:
                            eng.wait_ge(u_tap, 2 * k + 2)
                            A.activation(cth[:, u, :], ga2[:, u, :], ACT.Tanh).then_inc(u_tanh, 1)
                            f = 2 * it + u
                            eng.wait_ge(u_mul, f + 1)
                            A.activation(act_hi[:, f, :], ga2[:, u, :], ACT.Copy).then_inc(u_hi, 1)
                    if kind == "vd" and i == 1 and u == 1:
                        eng.wait_ge(spc, 1)
                        A.activation(sp[0][:, :], sp[0][:, :], ACT.Exp, scale=-1.0).then_inc(spa, 1)
                    for what, n in RIDES.get((c, u), []):
                        if what == "acs":
                            if n == 0:
                                eng.wait_ge(acs_mm, 1)
                                A.activation(acsT[:, :], PS[0:NH, 2, :], ACT.Copy).then_inc(acs_ev, 1)
                        elif what == "att":
                            if n < N_ATT:
                                eng.wait_ge(a_sc, n + 1)
                                if n:
                                    eng.wait_ge(a_exp, GQ * n)
                                sv = PS[:, 2 + 2 * (n % 2):4 + 2 * (n % 2), :].rearrange("p b (j s) -> p (b j) s", j=2)
                                A.activation(S[:, :, :], sv[:, :, P:2 * P], ACT.Copy).then_inc(a_cur, 1)
                            if 1 <= n <= N_ATT:
                                k = n - 1
                                eng.wait_ge(a_tp, k + 1)
                                if k:
                                    eng.wait_ge(a_ptc, k)
                                    eng.wait_ge(a_ptp, k)
                                A.activation(pt[:, :, :], PS[:, 6, :].rearrange("p (j q) -> p j q", j=GQ),
                                             ACT.Copy).then_inc(a_pt, 1)
                            if n >= 2:
                                k = n - 2
                                g, b = k % HKV, k // HKV
                                o = (g % 2) * HD
                                eng.wait_ge(a_pv, k + 1)
                                A.activation(a_hi[o:o + HD, (g // 2) * GQ:(g // 2) * GQ + GQ, b * P:(b + 1) * P],
                                             PS[o:o + HD, 7, :].rearrange("p (j q) -> p j q", j=GQ),
                                             ACT.Copy).then_inc(a_oh, 1)
                            if n < N_ATT:
                                eng.wait_ge(a_nm, n + 1)
                                if n:
                                    eng.wait_ge(a_tp, n)
                                for j in range(GQ):
                                    A.activation(Pr[:, j, :], S[:, j, :], ACT.Exp, bias=nm[:, j:j + 1],
                                                 accum_out=rsum[:, j:j + 1]).then_inc(a_exp, 1)
                                eng.wait_ge(a_df, n + 1)
                                A.activation(es, es, ACT.Exp).then_inc(a_es, 1)
                        elif what == "load":
                            g, cc = n // NT, n % NT
                            if n == 0:
                                eng.wait_ge(acs_out, 16)
                                eng.wait_ge(a_ol, N_ATT)
                            if n == 8:
                                eng.wait_ge(gemm_done, DONE[AT[("ao", 3)]])
                            if n >= 3:
                                eng.wait_ge(d_mm, n - 2)
                            rows_ = acs_d[HG * g:HG * g + HG, cc * P:(cc + 1) * P]
                            eng.dma_start(ag_of[n // 8][:, n % 3, :, :],
                                          rows_.unsqueeze(0).broadcast_to([P, HG, P])).then_inc(d_ab[n % 3], 16)
                        elif what == "dec":
                            a_ = ag_of[n // 8][:, n % 3, :, :]
                            eng.wait_ge(d_ab[n % 3], 16 * (n // 3 + 1))
                            if n >= 2:
                                eng.wait_ge(d_y, n - 1)
                            A.activation(cdec[:, n % 2, :], a_[:, :, P - 1], ACT.Exp).then_inc(d_cd, 1)
                            eng.wait_ge(d_dd, n + 1)
                            A.activation(dd8, dd8, ACT.Exp).then_inc(d_de, 1)
                            eng.wait_ge(d_seg, n + 1)
                            A.activation(a_, a_, ACT.Exp).then_inc(d_exp, 1)
                        elif what == "s1":
                            g, cc = n // NT, n % NT
                            if n:
                                eng.wait_ge(d_y, n)
                            for hh in range(2):
                                src = acs_d[HG * g:HG * g + HG, cc * P:(cc + 1) * P].rearrange("(i two) l -> two i l", two=2)[hh]
                                eng.dma_start(e2[hh * HD:(hh + 1) * HD, :, :],
                                              src.unsqueeze(0).broadcast_to([HD, TG, P])).then_inc(d_e2, 16)
                            eng.wait_ge(d_bc, n + 1)
                            if n:
                                eng.wait_ge(d_cbm, n)
                                eng.wait_ge(d_mm, n)
                            A.activation(bncb[:, :], PS[:, 3, 0:2 * P], ACT.Copy).then_inc(d_bcs, 1)
                        elif what == "s2":
                            g, cc = n // NT, n % NT
                            eng.wait_ge(d_e2, 32 * (n + 1))
                            A.activation(e2[:, :, :], e2[:, :, :], ACT.Exp).then_inc(d_e2x, 1)
                            eng.wait_ge(d_y, n + 1)
                            A.activation(yo[:, :].rearrange("p (i l) -> p i l", i=TG),
                                         sz[:, TG * g:TG * g + TG, cc * P:(cc + 1) * P], ACT.Square).then_inc(d_sq, 1)
                        elif what == "gend":
                            eng.wait_ge(d_sum, NT * (n + 1))
                            if n:
                                eng.wait_ge(g_w, TG * n)
                            A.activation(gsd[:, :], PS[:, 7, :], ACT.Sqrt, bias=epsc, scale=1.0 / (TG * P)).then_inc(g_sd, 1)
                            for t in range(TG):
                                eng.wait_ge(g_w, TG * n + t + 1)
                                A.activation(y_hi[:, TG * n + t, :], sz[:, TG * n + t, :], ACT.Copy).then_inc(g_hi, 1)
                if kind == "out" and i == 3:
                    for t in range(NT):
                        eng.wait_ge(h_add, NT + t + 1)
                        A.activation(hjunk[:, :], h[:, t, :], ACT.Square, accum_out=hss[:, t:t + 1]).then_inc(n_sq, 1)
                        eng.wait_ge(n_sq, NT + t + 1)
                        A.activation(hsd[:, t:t + 1], hss[:, t:t + 1], ACT.Sqrt, bias=epsc, scale=1.0 / D).then_inc(n_sd, 1)
                        if t:
                            norm_hi(t - 1)
                    norm_hi(NT - 1)
            for t in range(NT):
                eng.wait_ge(dn_add, NT + t + 1)
                if t:
                    eng.wait_ge(f_sq, t)
                A.activation(fjunk[:, :], h[:, t, :], ACT.Square, accum_out=fss[:, t:t + 1]).then_inc(f_sq, 1)
                eng.wait_ge(f_sq, t + 1)
                A.activation(fsd[:, t:t + 1], fss[:, t:t + 1], ACT.Sqrt, bias=epsc, scale=1.0 / D).then_inc(f_sd, 1)

        @block.vector
        def _(eng):
            V = nc.vector

            def bcast(cols, n, width):
                return cols.unsqueeze(2).broadcast_to([P, n, width])

            def split(c):
                eng.wait_ge(w_rounded, c + 1)
                n = chunk_len(c)
                V.tensor_tensor(wlo[:, c % 2, 0:n], raw[:, c % 2, 0:n], f32(whi[:, c % 2, 0:n]),
                                ALU.subtract).then_inc(w_split, 1)

            def norm_scale(t, k, src, root, inv, dst):
                eng.wait_ge(n_sd, k + 1)
                V.reciprocal(inv[:, t:t + 1], root[:, t:t + 1]).then_inc(n_rs, 1)
                eng.wait_ge(n_rs, k + 1)
                if k:
                    eng.wait_ge(n_tp, k)
                V.tensor_scalar(dst, src, inv[:, t:t + 1], None, ALU.mult).then_inc(n_sc, 1)

            def norm_weight(t, k, dst, w):
                eng.wait_ge(n_tp, k + 1)
                if k:
                    eng.wait_ge(n_lo, k)
                b = 4 + 2 * (t % 2)
                V.tensor_tensor(dst.rearrange("p (k l) -> p k l", k=KT),
                                PS[:, b:b + 2, :].rearrange("p b (k l) -> p (b k) l", l=P),
                                bcast(w, KT, P), ALU.mult).then_inc(n_tw, 1)

            def norm_lo(t, k, src, hi, lo):
                eng.wait_ge(n_hi, k + 1)
                V.tensor_tensor(lo[:, :, t * P:(t + 1) * P], src.rearrange("p (k l) -> p k l", k=KT),
                                f32(hi[:, :, t * P:(t + 1) * P]), ALU.subtract).then_inc(n_lo, 1)

            eng.wait_ge(pcols_t, 3)
            for i, n in enumerate((P, P, 88)):
                V.tensor_copy(pcol[:, i, 0:n], PS[:, i, 0:n]).then_inc(pcols, 1)
            eng.wait_ge(pcols, 3)
            V.tensor_scalar(cwh[:, 0:5 * NX], pcol[:, 0, 0:5 * NX], 0.5, None, ALU.mult).then_inc(pcols, 1)
            V.tensor_scalar(bgh[:, :], pcol[:, 1, bg0:bg0 + 16], 0.5, None, ALU.mult).then_inc(pcols, 1)
            for k in range(4):
                o = (k % 2) * 2 * FT + FT
                V.tensor_scalar(fwh[:, k, :], pcol[:, 1 + k // 2, o:o + FT], 0.5, None, ALU.mult).then_inc(pcols, 1)
            for hh in range(2):
                V.tensor_copy(dsk[hh * HD:(hh + 1) * HD, :], dskb[hh * HD:(hh + 1) * HD, hh:NH:2]).then_inc(pcols, 1)
            for t in range(NT):
                norm_scale(t, t, xnat[:, t, :], sd, rs, xsc[:, :])
                if t:
                    norm_weight(t - 1, t - 1, xt[:, :], n1w)
                    norm_lo(t - 1, t - 1, xt[:, :], xn_hi, xn_lo)
            norm_weight(NT - 1, NT - 1, xt[:, :], n1w)
            norm_lo(NT - 1, NT - 1, xt[:, :], xn_hi, xn_lo)
            split(0)
            k_conv = k_z = n_sp = n_yo = n_yx = n_stm = 0
            for c, (kind, i) in enumerate(CHUNKS):
                if c + 1 < len(CHUNKS):
                    split(c + 1)
                if kind == "vd" and i == 1:
                    for t in range(NT):
                        eng.wait_ge(gemm_done, DONE[c, t])
                        V.tensor_copy(v[:, t, :], PS[:, 4 + t, 0:HKV * HD]).then_inc(v_ready, 1)
                        if t == 0:
                            eng.wait_ge(params_in, 16 * 13)
                        V.tensor_tensor(dtr[:, t, :], PS[:, 4 + t, HKV * HD:VW], dtb[:, :],
                                        ALU.add).then_inc(v_ready, 1)
                    X = dtr[:, :, :].rearrange("p t h -> p (t h)")
                    e, z, w, pl, r, q_ = (s_[:, :] for s_ in sp)
                    eng.wait_ge(v_ready, 2 * NT)
                    V.tensor_scalar(q_, X, -1.0, None, ALU.mult).then_inc(spd, 1)
                    eng.wait_ge(spd, 1)
                    V.tensor_tensor(e, X, q_, ALU.max).then_inc(spc, 1)
                    eng.wait_ge(spa, 2)

                    def chained(ins):
                        nonlocal n_sp
                        n_sp += 1
                        ins.then_inc(spd, 1)
                        eng.wait_ge(spd, n_sp + 1)

                    chained(V.tensor_scalar(r, e, 2.0, None, ALU.add))
                    chained(V.reciprocal(r, r))
                    chained(V.tensor_tensor(z, e, r, ALU.mult))
                    chained(V.tensor_tensor(w, z, z, ALU.mult))
                    chained(V.tensor_scalar(pl, w, 1.0 / 17, 1.0 / 15, ALU.mult, ALU.add))
                    for k in (13, 11, 9, 7, 5, 3, 1):
                        chained(V.tensor_tensor(pl, pl, w, ALU.mult))
                        chained(V.tensor_scalar(pl, pl, 1.0 / k, None, ALU.add))
                    chained(V.scalar_tensor_tensor(out=pl, in0=z, scalar=2.0, in1=pl, op0=ALU.mult, op1=ALU.mult))
                    chained(V.tensor_scalar(r, X, 0.0, None, ALU.max))
                    chained(V.tensor_tensor(dt[:, :, :].rearrange("p t h -> p (t h)"), r, pl, ALU.add))
                    V.scalar_tensor_tensor(out=q_.rearrange("p (t h) -> p t h", t=NT), in0=dt[:, :, :], scalar=-1.0,
                                           in1=nA[:, :].unsqueeze(1).broadcast_to([P, NT, NH]),
                                           op0=ALU.mult, op1=ALU.mult).then_inc(da_ready, 1)
                if kind in FORM_B and kind != "vd":
                    add, nh, last = (h_add, i // 2, i % 2 == 1) if kind == "out" else (dn_add, i // 6, i % 6 == 5)
                    if last:
                        for t in range(NT):
                            eng.wait_ge(gemm_done, DONE[c, t])
                            if kind == "out" and nh == 0 and t == 0:
                                eng.wait_ge(h_in, 16)
                            hv = h[:, t, nh * 512:nh * 512 + 512]
                            V.tensor_tensor(hv, hv, PS[:, (4, 0)[nh] + t, :], ALU.add).then_inc(add, 1)
                            if kind == "out" and nh == 1:
                                if t:
                                    norm_scale(t - 1, NT + t - 1, h[:, t - 1, :], hsd, hrs, hsc[:, :])
                                if t > 1:
                                    norm_weight(t - 2, NT + t - 2, ht[:, :], n2w)
                                    norm_lo(t - 2, NT + t - 2, ht[:, :], hn_hi, hn_lo)
                        if kind == "out" and nh == 1:
                            norm_scale(NT - 1, 2 * NT - 1, h[:, NT - 1, :], hsd, hrs, hsc[:, :])
                            for t in (NT - 2, NT - 1):
                                norm_weight(t, NT + t, ht[:, :], n2w)
                                norm_lo(t, NT + t, ht[:, :], hn_hi, hn_lo)
                    continue
                for u in range(2):
                    b = PS[:, u, :]
                    if kind in ("bc", "xs"):
                        t = 2 * i + u + (16 if kind == "bc" else 0)
                        acc = cacc[:, u, :]
                        eng.wait_ge(c_acc, k_conv + 1)
                        for back in (1, 2, 3):
                            if back > 1:
                                eng.wait_ge(c_tap, 3 * k_conv + back - 1)
                            V.scalar_tensor_tensor(out=acc[:, back:SEQ], in0=b[:, 0:SEQ - back], scalar=CW(3 - back, t),
                                                   in1=acc[:, back:SEQ], op0=ALU.mult, op1=ALU.add).then_inc(c_tap, 1)
                        eng.wait_ge(c_tanh, k_conv + 1)
                        dst = bc[:, t - 16, :] if kind == "bc" else xs[:, t, :]
                        V.scalar_tensor_tensor(out=dst, in0=cth[:, u, :], scalar=1.0, in1=acc,
                                               op0=ALU.add, op1=ALU.mult).then_inc(c_out, 1)
                        k_conv += 1
                    elif kind == "z":
                        eng.wait_ge(z_tanh, k_z + 1)
                        if k_z == 0:
                            eng.wait_ge(acs_out, 16)
                        V.scalar_tensor_tensor(out=sz[:, 2 * i + u, :], in0=cth[:, u, :], scalar=1.0, in1=b,
                                               op0=ALU.add, op1=ALU.mult).then_inc(z_out, 1)
                        k_z += 1
                    elif kind == "ao":
                        eng.wait_ge(gemm_done, DONE[c, u])
                        eng.wait_ge(g_tanh, 2 * i + u + 1)
                        if i:
                            eng.wait_ge(ao_sp[u], 16 * i)
                        V.scalar_tensor_tensor(out=cacc[:, u, :], in0=cth[:, u, :], scalar=1.0, in1=b,
                                               op0=ALU.add, op1=ALU.mult).then_inc(ao_out, 1)
                    elif kind == "so" and i[1] == 1:
                        f = 2 * i[0] + u
                        eng.wait_ge(gemm_done, DONE[c, u])
                        eng.wait_ge(so_in[u], 32 * (i[0] + 1))
                        V.scalar_tensor_tensor(out=cth[:, u, :], in0=cth[:, u, :], scalar=1.0,
                                               in1=PS[:, 2 * (i[0] % 2) + u, :], op0=ALU.add, op1=ALU.mult).then_inc(so_g, 1)
                        eng.wait_ge(so_g, f + 1)
                        V.tensor_tensor(cacc[:, u, :], cacc[:, u, :], cth[:, u, :], ALU.add).then_inc(so_a, 1)
                        eng.wait_ge(so_hi, f + 1)
                        V.scalar_tensor_tensor(out=mix_lo[:, f, :], in0=cacc[:, u, :], scalar=0.5, in1=f32(mix_hi[:, f, :]),
                                               op0=ALU.mult, op1=ALU.subtract).then_inc(so_lo, 1)
                    elif kind == "up":
                        k, it = 2 * i + u, i // 2
                        t = (i % 2) * FT + 2 * it + u
                        acc = ga2[:, u, :] if i % 2 else cacc[:, u, :]
                        eng.wait_ge(u_acc, k + 1)
                        for back in (1, 2):
                            if back > 1:
                                eng.wait_ge(u_tap, 2 * k + 1)
                            V.scalar_tensor_tensor(out=acc[:, back:SEQ], in0=PS[:, 2 * (i % 2) + u, 0:SEQ - back],
                                                   scalar=FW(2 - back, t), in1=acc[:, back:SEQ],
                                                   op0=ALU.mult, op1=ALU.add).then_inc(u_tap, 1)
                        if i % 2:
                            f = 2 * it + u
                            eng.wait_ge(u_tanh, f + 1)
                            V.scalar_tensor_tensor(out=acc, in0=cth[:, u, :], scalar=1.0, in1=acc,
                                                   op0=ALU.add, op1=ALU.mult).then_inc(u_silu, 1)
                            eng.wait_ge(u_silu, f + 1)
                            V.tensor_tensor(acc, acc, cacc[:, u, :], ALU.mult).then_inc(u_mul, 1)
                            eng.wait_ge(u_hi, f + 1)
                            V.tensor_tensor(act_lo[:, f, :], acc, f32(act_hi[:, f, :]), ALU.subtract).then_inc(u_lo, 1)
                    for what, n in RIDES.get((c, u), []):
                        if what == "acs" and n == 1:
                            eng.wait_ge(acs_tp, 1)
                            V.tensor_scalar(nacs[:, :, :].rearrange("p t h -> p (t h)"), PS[:, 3, 0:NT * NH],
                                            -1.0, None, ALU.mult).then_inc(acs_nat, 1)
                        if what == "att":
                            g, b_ = n % HKV, n // HKV
                            if n < N_ATT:
                                eng.wait_ge(a_cur, n + 1)
                                if b_:
                                    prev = PS[:, 2 + 2 * (n % 2):4 + 2 * (n % 2), :].rearrange(
                                        "p b (j s) -> p (b j) s", j=2)[:, :, 0:P]
                                else:
                                    prev = negt[:, :].unsqueeze(1).broadcast_to([P, GQ, P])
                                V.copy_predicated(S[:, :, :], mprev[:, :].unsqueeze(1).broadcast_to([P, GQ, P]),
                                                  prev).then_inc(a_sel, 1)
                                eng.wait_ge(a_sel, n + 1)
                                V.tensor_reduce(mx, S[:, :, :], AX.X, ALU.max).then_inc(a_max, 1)
                                eng.wait_ge(a_max, n + 1)
                                V.tensor_tensor(m_, mx, snk[:, GQ * g:GQ * g + GQ], ALU.max).then_inc(a_m, 1)
                                eng.wait_ge(a_m, n + 1)
                                V.tensor_scalar(nm, m_, -1.0, None, ALU.mult).then_inc(a_nm, 1)
                                V.tensor_tensor(es, snk[:, GQ * g:GQ * g + GQ], m_, ALU.subtract).then_inc(a_df, 1)
                            if 1 <= n <= N_ATT:
                                k = n - 1
                                eng.wait_ge(a_pt, k + 1)
                                if k:
                                    eng.wait_ge(a_pv, k)
                                V.tensor_tensor(ptc[:, :, :], pt[:, :, :], tri[:, :].unsqueeze(1).broadcast_to([P, GQ, P]),
                                                ALU.mult).then_inc(a_ptc, 1)
                            if n >= 2:
                                k = n - 2
                                g2, b2 = k % HKV, k // HKV
                                o = (g2 % 2) * HD
                                tl = slice((g2 // 2) * GQ, (g2 // 2) * GQ + GQ)
                                eng.wait_ge(a_oh, k + 1)
                                V.tensor_tensor(a_lo[o:o + HD, tl, b2 * P:(b2 + 1) * P],
                                                PS[o:o + HD, 7, :].rearrange("p (j q) -> p j q", j=GQ),
                                                f32(a_hi[o:o + HD, tl, b2 * P:(b2 + 1) * P]), ALU.subtract).then_inc(a_ol, 1)
                            if n < N_ATT:
                                eng.wait_ge(a_exp, GQ * (n + 1))
                                eng.wait_ge(a_es, n + 1)
                                V.tensor_tensor(den, rsum, es, ALU.add).then_inc(a_den, 1)
                                eng.wait_ge(a_den, n + 1)
                                V.reciprocal(rden, den).then_inc(a_rd, 1)
                                eng.wait_ge(a_rd, n + 1)
                                V.tensor_tensor(Pr[:, :, :], Pr[:, :, :], bcast(rden, GQ, P), ALU.mult).then_inc(a_pr, 1)
                        g, cc = n // NT, n % NT
                        hs = slice(HG * g, HG * g + HG)
                        if what == "dec":
                            a_ = ag_of[n // 8][:, n % 3, :, :]
                            eng.wait_ge(d_ab[n % 3], 16 * (n // 3 + 1))
                            if n:
                                eng.wait_ge(d_ddt, n)
                            V.tensor_tensor(dd8, a_[:, :, P - 1], nacs[:, cc, hs], ALU.add).then_inc(d_dd, 1)
                            eng.wait_ge(d_cd, n + 1)
                            eng.wait_ge(d_dd, n + 1)
                            for hd in range(HG):
                                ins = V.tensor_scalar(a_[:, hd, :], a_[:, hd, :], nacs[:, cc, HG * g + hd:HG * g + hd + 1],
                                                      0.0, ALU.add, ALU.min)
                            ins.then_inc(d_seg, 1)
                            eng.wait_ge(d_de, n + 1)
                            if n >= 2:
                                eng.wait_ge(d_xcd, n - 1)
                            V.tensor_tensor(ddt[:, n % 2, :], dd8, dt[:, cc, hs], ALU.mult).then_inc(d_ddt, 1)
                        if what == "s1":
                            a_, xc, xcd = ag_of[n // 8][:, n % 3, :, :], xc_of[n // 8], xcd_of[n // 8]
                            eng.wait_ge(d_x, n + 1)
                            if n:
                                eng.wait_ge(d_mm, n)
                            xv = PS[:, 2, :].rearrange("p (h q) -> p h q", h=HG)
                            V.tensor_tensor(xc[:, :].rearrange("p (h q) -> p h q", h=HG), xv,
                                            bcast(dt[:, cc, hs], HG, HD), ALU.mult).then_inc(d_xc, 1)
                            eng.wait_ge(d_ddt, n + 1)
                            V.tensor_tensor(xcd[:, :].rearrange("p (h q) -> p h q", h=HG), xv,
                                            bcast(ddt[:, n % 2, :], HG, HD), ALU.mult).then_inc(d_xcd, 1)
                            eng.wait_ge(d_bcs, n + 1)
                            if n:
                                eng.wait_ge(d_m, n)
                            V.tensor_tensor(cbm[:, :], bncb[:, P:2 * P], tri[:, :], ALU.mult).then_inc(d_cbm, 1)
                            eng.wait_ge(d_cbm, n + 1)
                            eng.wait_ge(d_exp, n + 1)
                            V.tensor_tensor(a_, a_, cbm[:, :].unsqueeze(1).broadcast_to([P, HG, P]),
                                            ALU.mult).then_inc(d_m, 1)
                        if what == "s2":
                            eng.wait_ge(d_mm, n + 1)
                            sv = st[:, :].rearrange("p (h q) -> p h q", h=HG)
                            if cc == 0:
                                V.tensor_copy(st[:, :], PS[:, 6, :]).then_inc(d_stp, 1)
                            elif cc < NT - 1:
                                V.tensor_tensor(sv, sv, bcast(cdec[:, n % 2, :], HG, HD), ALU.mult).then_inc(d_stm, 1)
                                n_stm += 1
                                eng.wait_ge(d_stm, n_stm)
                                V.tensor_tensor(st[:, :], st[:, :], PS[:, 6, :], ALU.add).then_inc(d_stp, 1)
                            yv = yo[:, :].rearrange("p (i l) -> p i l", i=TG)
                            dg = PS[:, 5, :].rearrange("p (i l) -> p i l", i=TG)
                            xsv = xs[:, TG * g:TG * g + TG, cc * P:(cc + 1) * P]
                            szv = sz[:, TG * g:TG * g + TG, cc * P:(cc + 1) * P]
                            eng.wait_ge(d_dxs, n + 1)
                            if n:
                                eng.wait_ge(d_s1, n)
                            if cc:
                                eng.wait_ge(d_e2x, n + 1)
                                V.tensor_tensor(yv, PS[:, 4, :].rearrange("p (i l) -> p i l", i=TG),
                                                e2[:, :, :], ALU.mult).then_inc(d_yo, 1)
                                n_yo += 1
                                eng.wait_ge(d_yo, n_yo)
                                V.tensor_tensor(yv, yv, xsv, ALU.add).then_inc(d_yx, 1)
                                n_yx += 1
                                eng.wait_ge(d_yx, n_yx)
                                V.tensor_tensor(yv, yv, dg, ALU.add).then_inc(d_yd, 1)
                            else:
                                eng.wait_ge(d_e2x, n + 1)
                                V.tensor_tensor(yv, xsv, dg, ALU.add).then_inc(d_yd, 1)
                            eng.wait_ge(d_yd, n + 1)
                            V.scalar_tensor_tensor(out=szv, in0=yv, scalar=0.5, in1=szv,
                                                   op0=ALU.mult, op1=ALU.mult).then_inc(d_y, 1)
                        if what == "gend":
                            eng.wait_ge(g_sd, n + 1)
                            V.reciprocal(gsd[:, :], gsd[:, :]).then_inc(g_rs, 1)
                            eng.wait_ge(g_rs, n + 1)
                            for t in range(TG):
                                f = TG * n + t
                                V.scalar_tensor_tensor(out=sz[:, f, :], in0=sz[:, f, :], scalar=snw[:, f:f + 1],
                                                       in1=gsd[:, :], op0=ALU.mult, op1=ALU.mult).then_inc(g_w, 1)
                            for t in range(TG):
                                f = TG * n + t
                                eng.wait_ge(g_hi, f + 1)
                                V.tensor_tensor(y_lo[:, f, :], sz[:, f, :], f32(y_hi[:, f, :]),
                                                ALU.subtract).then_inc(g_lo, 1)
            eng.wait_ge(fnw_in, 16)
            for t in range(NT):
                eng.wait_ge(f_sd, t + 1)
                V.reciprocal(frs[:, t:t + 1], fsd[:, t:t + 1]).then_inc(f_rs, 1)
                eng.wait_ge(f_rs, t + 1)
                if t >= 2:
                    eng.wait_ge(f_st[t % 2], 16)
                V.scalar_tensor_tensor(out=fo[:, t % 2, :], in0=h[:, t, :], scalar=frs[:, t:t + 1], in1=fnw[:, :],
                                       op0=ALU.mult, op1=ALU.mult).then_inc(f_out, 1)

        @block.tensor
        def _(eng):
            T = nc.tensor
            freed_by = {}

            def take(b, sem_, value):
                if b in freed_by:
                    eng.wait_ge(*freed_by[b])
                freed_by[b] = (sem_, value)

            def three(out_, w, m, first, last):
                T.matmul(out_, w[0], m[0], start=first, stop=False)
                T.matmul(out_, w[0], m[1], start=False, stop=False)
                return T.matmul(out_, w[1], m[0], start=False, stop=last)

            eng.wait_ge(consts, 11)
            eng.wait_ge(params_in, 16 * 13)
            for i, n in enumerate((P, P, 88)):
                take(i, pcols, 3)
                T.transpose(PS[:, i, 0:n], stage[0:n, i, :], ident[0:n, 0:n]).then_inc(pcols_t, 1)

            def norm_transposes(t, k, src):
                b = 4 + 2 * (t % 2)
                eng.wait_ge(n_sc, k + 1)
                take(b, n_tw, k + 1)
                take(b + 1, n_tw, k + 1)
                for kt in range(KT):
                    ins = T.transpose(PS[:, b + kt // 4, (kt % 4) * P:(kt % 4 + 1) * P], src[:, kt * P:(kt + 1) * P], ident[:, :])
                ins.then_inc(n_tp, 1)

            for t in range(NT):
                norm_transposes(t, t, xsc)
            k_conv = k_z = 0
            for c, (kind, i) in enumerate(CHUNKS):
                s_ = c % 2
                wh, wl = whi[:, s_, :], wlo[:, s_, :]
                eng.wait_ge(w_split, c + 1)
                if kind in FORM_B:
                    if kind == "vd":
                        nk, width, k0, first, last = 4, VW, 4 * i, i == 0, i == 1
                        mh, ml, b0 = xn_hi, xn_lo, 4
                    elif kind == "out":
                        nk, width, k0, first, last = 4, 512, 4 * (i % 2), i % 2 == 0, i % 2 == 1
                        mh, ml, b0 = mix_hi, mix_lo, (4, 0)[i // 2]
                        eng.wait_ge(so_lo, k0 + 4)
                    else:
                        k0, nk = down_tiles(i)
                        width, first, last = 512, i % 6 == 0, i % 6 == 5
                        mh, ml, b0 = act_hi, act_lo, (4, 0)[i // 6]
                        eng.wait_ge(u_lo, k0 + nk)
                    for t in range(NT):
                        if kind == "vd" and first:
                            eng.wait_ge(n_lo, t + 1)
                        if first:
                            if kind == "vd":
                                take(b0 + t, v_ready, 2 * t + 2)
                            else:
                                take(b0 + t, h_add if kind == "out" else dn_add, NT * (i // (2 if kind == "out" else 6)) + t + 1)
                        for kt in range(nk):
                            tok = slice(t * P, (t + 1) * P)
                            cols_ = slice(kt * width, (kt + 1) * width)
                            ins = three(PS[:, b0 + t, 0:width], (mh[:, k0 + kt, tok], ml[:, k0 + kt, tok]),
                                        (wh[:, cols_], wl[:, cols_]), first and kt == 0, last and kt == nk - 1)
                        ins.then_inc(gemm_done, 1)
                    if kind == "out" and i == 3:
                        for t in range(NT):
                            norm_transposes(t, NT + t, hsc)
                        eng.wait_ge(n_lo, 2 * NT)
                    continue
                for u in range(2):
                    b, k0, first, last = u, 0, True, True
                    mh, ml = xn_hi, xn_lo
                    if kind == "k":
                        take(b, qk_ready, u + 1)
                    elif kind == "q":
                        take(b, qk_ready, 2 + 2 * i + u + 1)
                    elif kind in ("bc", "xs"):
                        k_conv += 1
                        take(b, c_tap, 3 * k_conv)
                    elif kind == "z":
                        k_z += 1
                        take(b, z_out, k_z)
                    elif kind == "ga":
                        take(b, g_tanh, 2 * i + u + 1)
                    elif kind == "ao":
                        take(b, ao_out, 2 * i + u + 1)
                        mh, ml = a_hi, a_lo
                        if i == 0 and u == 0:
                            eng.wait_ge(a_ol, N_ATT)
                    elif kind == "gs":
                        take(b, gs_tanh, 2 * i + u + 1)
                    elif kind == "so":
                        b = 2 * (i[0] % 2) + u
                        mh, ml, k0 = y_hi, y_lo, KT * i[1]
                        first, last = i[1] == 0, i[1] == 1
                        if first:
                            take(b, so_g, 2 * i[0] + u + 1)
                    elif kind == "up":
                        b = 2 * (i % 2) + u
                        take(b, u_tap, 2 * (2 * i + u) + 2)
                        mh, ml = hn_hi, hn_lo
                    for kt in range(KT):
                        if kind == "so" and (k0 + kt) % TG == 0:
                            eng.wait_ge(g_lo, k0 + kt + TG)
                        w_ = slice(kt * 256 + u * P, kt * 256 + (u + 1) * P)
                        ins = three(PS[:, b, :], (wh[:, w_], wl[:, w_]), (mh[:, k0 + kt, :], ml[:, k0 + kt, :]),
                                    first and kt == 0, last and kt == KT - 1)
                    ins.then_inc(gemm_done, 1)
                    for what, n in RIDES.get((c, u), []):
                        if what == "acs" and n == 0:
                            eng.wait_ge(da_ready, 1)
                            take(2, acs_ev, 1)
                            for t in range(NT):
                                ins = T.matmul(PS[0:NH, 2, t * P:(t + 1) * P], sp[5][:, t * NH:(t + 1) * NH], tri[:, :],
                                               start=True, stop=True)
                            ins.then_inc(acs_mm, 1)
                        if what == "acs" and n == 1:
                            eng.wait_ge(acs_ev, 1)
                            take(3, acs_nat, 1)
                            for t in range(NT):
                                ins = T.transpose(PS[:, 3, t * NH:(t + 1) * NH], acsT[:, t * P:(t + 1) * P],
                                                  ident[0:NH, 0:NH])
                            ins.then_inc(acs_tp, 1)
                        if what == "att":
                            if n < N_ATT:
                                g, b_ = n % HKV, n // HKV
                                o = (g % 2) * HD
                                if n == 0:
                                    eng.wait_ge(qk_ready, 10)
                                for q_ in range(2):
                                    take(2 + 2 * (n % 2) + q_, a_sel, n + 1)
                                for j in range(GQ):
                                    bank = PS[:, 2 + 2 * (n % 2) + j // 2, :]
                                    c0 = (j % 2) * 2 * P + (0 if b_ else P)
                                    k0_ = max(b_ - 1, 0) * P
                                    ins = T.matmul(bank[:, c0:(j % 2 + 1) * 2 * P],
                                                   qT[o:o + HD, (g // 2) * GQ + j, b_ * P:(b_ + 1) * P],
                                                   kT[o:o + HD, g // 2, k0_:(b_ + 1) * P], start=True, stop=True)
                                ins.then_inc(a_sc, 1)
                            if 1 <= n <= N_ATT:
                                k = n - 1
                                eng.wait_ge(a_pr, k + 1)
                                take(6, a_pt, k + 1)
                                for j in range(GQ):
                                    ins = T.transpose(PS[:, 6, j * P:(j + 1) * P], Pr[:, j, :], ident[:, :])
                                ins.then_inc(a_tp, 1)
                            if n >= 2:
                                k = n - 2
                                g, b_ = k % HKV, k // HKV
                                o = (g % 2) * HD
                                eng.wait_ge(a_ptc, k + 1)
                                eng.wait_ge(a_ptp, k + 1)
                                take(7, a_ol, k + 1)
                                if b_:
                                    T.matmul(PS[o:o + HD, 7, :], v[:, b_ - 1, g * HD:(g + 1) * HD],
                                             ptp[:, :, :].rearrange("p j q -> p (j q)"), start=True, stop=False)
                                T.matmul(PS[o:o + HD, 7, :], v[:, b_, g * HD:(g + 1) * HD],
                                         ptc[:, :, :].rearrange("p j q -> p (j q)"), start=b_ == 0, stop=True).then_inc(a_pv, 1)
                        g, cc = n // NT, n % NT
                        tok = slice(cc * P, (cc + 1) * P)
                        if what == "s1":
                            if True:
                                eng.wait_ge(c_out, 8 + 4 * (g + 1))
                                take(2, d_xcd, n + 1)
                                for t in range(TG):
                                    ins = T.transpose(PS[:, 2, t * P:(t + 1) * P], xs[:, TG * g + t, tok], ident[:, :])
                                ins.then_inc(d_x, 1)
                                take(3, d_bcs, n + 1)
                                T.transpose(PS[:, 3, 0:P], bc[:, g, tok], ident[:, :])
                                T.matmul(PS[:, 3, P:2 * P], bc[:, g, tok], bc[:, NG + g, tok], start=True,
                                         stop=True).then_inc(d_bc, 1)
                        if what == "s2":
                            if True:
                                k = n
                                ag, xc, xcd = ag_of[n // 8], xc_of[n // 8], xcd_of[n // 8]
                                if cc < NT - 1:
                                    eng.wait_ge(d_xcd, k + 1)
                                    eng.wait_ge(d_bcs, k + 1)
                                    take(6, d_stp, (NT - 1) * g + cc + 1)
                                    T.matmul(PS[:, 6, :], bncb[:, 0:P], xcd[:, :], start=True, stop=True)
                                if cc:
                                    eng.wait_ge(d_stp, (NT - 1) * g + cc)
                                    take(4, d_yd, k + 1)
                                    for t in range(TG):
                                        T.matmul(PS[:, 4, t * P:(t + 1) * P], st[:, t * P:(t + 1) * P],
                                                 bc[:, NG + g, tok], start=True, stop=True)
                                eng.wait_ge(d_m, k + 1)
                                eng.wait_ge(d_xc, k + 1)
                                take(5, d_yd, k + 1)
                                for hd in range(HG):
                                    o = (hd % 2) * HD
                                    ins = T.matmul(PS[o:o + HD, 5, (hd // 2) * P:(hd // 2 + 1) * P],
                                                   xc[:, hd * HD:(hd + 1) * HD], ag[:, k % 3, hd, :],
                                                   start=True, stop=True)
                                ins.then_inc(d_mm, 1)
                        if what == "sum":
                            if True:
                                k = n
                                eng.wait_ge(d_s2, k + 1)
                                if cc == 0:
                                    take(7, g_sd, g + 1)
                                T.matmul(PS[:, 7, cc * P:(cc + 1) * P], ones[:, :], sq2[:, :], start=True,
                                         stop=True).then_inc(d_sum, 1)


_INS = ["x", "norm1_w", "w_in", "b_gate", "attn_sinks", "w_attn_o", "ssd_conv_w", "ssd_conv_b", "dt_bias",
        "a_log", "d_skip", "ssd_norm_w", "w_ssd_o", "w_out", "norm2_w", "w_up", "ffn_conv_w", "ffn_conv_b",
        "w_down", "final_norm_w"]


def kernel(**inputs):
    import numpy as _np
    import concourse.bacc as _bacc
    from concourse import mybir as _mybir
    from concourse.bass_utils import run_bass_kernel_spmd as _run

    nc = _bacc.Bacc("TRN2", target_bir_lowering=False, num_devices=1)
    arrays, args = {}, []
    for name in _INS:
        a = _np.ascontiguousarray(inputs[name])
        arrays[f"in_{name}"] = a
        args.append(nc.dram_tensor(f"in_{name}", a.shape, _mybir.dt.from_np(a.dtype), kind="ExternalInput").ap())
    out = nc.dram_tensor("out_0", (1, SEQ, D), F32, kind="ExternalOutput").ap()
    hybrid_layer(nc, *args, out)
    r = _run(nc, [arrays], core_ids=[0])
    return r.results[0]["out_0"]
```

```python
import concourse.bass as bass
from concourse import mybir
from contextlib import ExitStack

F32 = mybir.dt.float32
F32R = mybir.dt.float32r
I32 = mybir.dt.int32
ALU = mybir.AluOpType
ACT = mybir.ActivationFunctionType
AX = mybir.AxisListType

P = 128
SEQ, D = 512, 1024
NT = SEQ // P
KT = D // P
HQ, HKV, HD = 16, 4, 64
GQ = HQ // HKV
DI = 2 * D
NH, NG, NS = 32, 4, 128
HG = NH // NG
TG = DI // NG // P
XBC = DI + 2 * NG * NS
FF = 2816
FT = FF // P
EPS = 1e-5
NEG = -1e30
Q0 = 0
K0 = Q0 + HQ * HD
V0 = K0 + HKV * HD
Z0 = V0 + HKV * HD
X0 = Z0 + DI
B0 = X0 + DI
DT0 = X0 + XBC
GA0 = DT0 + NH
GS0 = GA0 + D
CH = 2048
VW = HKV * HD + NH

CHUNKS = [("vd", 0), ("vd", 1), ("k", 0)] + [("q", i) for i in range(4)]
CHUNKS += [("bc", i) for i in range(4)]
CHUNKS += [("xs", 0), ("xs", 1), ("z", 0), ("z", 1), ("xs", 2), ("xs", 3), ("z", 2), ("z", 3)]
for _i in range(4):
    CHUNKS += [("ga", _i), ("ao", _i)]
CHUNKS += [("xs", 4), ("xs", 5), ("z", 4), ("z", 5), ("xs", 6), ("xs", 7), ("z", 6), ("z", 7)]
CHUNKS += [("gs", i) for i in range(4)]
for _i in range(2):
    CHUNKS += [("so", (2 * _i, 0)), ("so", (2 * _i + 1, 0)), ("so", (2 * _i, 1)), ("so", (2 * _i + 1, 1))]
CHUNKS += [("out", i) for i in range(4)]
CHUNKS += [("up", i) for i in range(22)]
CHUNKS += [("down", i) for i in range(12)]
AT = {ch: n for n, ch in enumerate(CHUNKS)}

FORM_B = ("vd", "out", "down")
DONE = {}
_n = 0
for _c, (_kind, _i) in enumerate(CHUNKS):
    for _p in range(4 if _kind in FORM_B else 2):
        _n += 1
        DONE[_c, _p] = _n
    DONE[_c] = _n
_c2, _c3 = AT[("out", 2)], AT[("out", 3)]
for _p in range(4):
    DONE[_c2, _p], DONE[_c3, _p] = DONE[_c2 - 1] + 2 * _p + 1, DONE[_c2 - 1] + 2 * _p + 2
DONE[_c2] = DONE[_c2, 3]

N_ATT = NT * HKV
N_SSD = NG * NT
SLOTS = {"PE": 2, "ACT": 3, "DVE": 3, "POOL": 1}
ATT_STAGES = (
    ("PE", "scores", 1), ("PE", "probs_t", 5), ("PE", "values", 7), ("ACT", "cur", 1), ("ACT", "exp", 2),
    ("ACT", "pt", 7), ("ACT", "oh", 10), ("DVE", "sel", 1), ("DVE", "pr", 4), ("DVE", "ptc", 7),
    ("DVE", "ol", 10), ("POOL", "ptp", 2))
SSD_STAGES = (
    ("PE", "s1", 1), ("PE", "s2", 4), ("PE", "sum", 6), ("ACT", "load", -6), ("ACT", "dec", -4),
    ("ACT", "e2load", 1), ("ACT", "bcs", 2), ("ACT", "e2x", 5), ("ACT", "sq", 5), ("ACT", "dexp", 1),
    ("DVE", "dec", -4), ("DVE", "xdt", 2), ("DVE", "m", 2), ("DVE", "state", 5), ("DVE", "y", 5),
    ("POOL", "dxs", 0), ("POOL", "ysq", 1), ("POOL", "seg", -2))
RIDES = {}


def ride(engine, slot, what, n):
    RIDES.setdefault((engine, slot), []).append((n, what))


def first_unit(n):
    if n < N_SSD // 2:
        return 2 * AT[("ga", 0)] + 1 + 2.0 * n
    return 2 * AT[("xs", 6)] + 0 + 1.9375 * (n - N_SSD // 2)


for _n in range(N_ATT):
    for _e, _w, _v in ATT_STAGES:
        ride(_e, int((2 * AT[("bc", 0)] + -4.5 + 1.5625 * _n) * SLOTS[_e]) + _v, _w, _n)
for _n in range(N_SSD):
    for _e, _w, _v in SSD_STAGES:
        ride(_e, int(first_unit(_n) * SLOTS[_e]) + _v, _w, _n)
for _g in range(NG):
    for _k in range(TG + 1):
        for _e in ("ACT", "DVE"):
            ride(_e, 3 * (int(first_unit(_g * NT + NT - 1)) + 3 + (_k if _g < NG - 1 else 0)) + 2, "gnorm", (_g, _k))
_u = 2 * AT[("q", 1)] + 1
ride("PE", 2 * _u + 1, "acs", -2)
ride("PE", 2 * _u + 5, "acs", -1)
ride("ACT", 3 * _u + 2, "acs", -2)
ride("DVE", 3 * _u + 8, "acs", -1)


def rides_at(engine, c, u, slot=0):
    return sorted(RIDES.get((engine, SLOTS[engine] * (2 * c + u) + slot), []),
                  key=lambda r: r[0] if isinstance(r[0], int) else r[0][0] * NT + NT - 1.5)


def att_step(n):
    return 2 * (n // 8) + n % 2, (n % 8) // 2


def hybrid_layer(nc, x, norm1_w, w_in, b_gate, attn_sinks, w_attn_o, ssd_conv_w, ssd_conv_b, dt_bias,
                 a_log, d_skip, ssd_norm_w, w_ssd_o, w_out, norm2_w, w_up, ffn_conv_w, ffn_conv_b,
                 w_down, final_norm_w, out):
    ctx = ExitStack()
    with ctx:
        base = 16512

        def sb(name, shape, kb, dt=F32):
            return nc.alloc_sbuf_tensor_at(name, shape, dt, offset=base + int(kb * 1024))

        xn_hi = sb("xn_hi", [P, KT, SEQ], 0, F32R)
        xn_lo = sb("xn_lo", [P, KT, SEQ], 16, F32R)
        raw = sb("w_raw", [P, 2, CH], 32)
        whi = sb("w_hi", [P, 2, CH], 48, F32R)
        wlo = sb("w_lo", [P, 2, CH], 64, F32R)
        xs = sb("xs", [P, 16, SEQ], 80)
        y_hi = sb("y_hi", [P, 16, SEQ], 80, F32R)
        sz = sb("sz", [P, 16, SEQ], 112)
        y_lo = sb("y_lo", [P, 16, SEQ], 112, F32R)
        bc = sb("bc", [P, 2 * NG, SEQ], 144)
        qT = sb("qT", [P, 8, SEQ], 160)
        a_hi = sb("a_hi", [P, 8, SEQ], 160, F32R)
        a_lo = sb("a_lo", [P, 8, SEQ], 96, F32R)
        kT = sb("kT", [P, 2, SEQ], 176)
        v = sb("v", [P, NT, HKV * HD], 180)
        cacc = sb("conv_acc", [P, 2, SEQ], 184)
        cth = sb("conv_tanh", [P, 2, SEQ], 188)
        xnat = sb("x_nat", [P, NT, D], 112)
        xsc = sb("x_scaled", [P, 2, D], 128)
        junk = sb("junk", [P, D], 136)
        stage = sb("param_rows", [P, 3, P], 140)
        dskb = sb("d_skip_rows", [P, NH], 141.5)
        n1row = sb("norm1_row", [P, D], 144)
        sp = [sb(f"softplus{i}", [P, NT * NH], 112 + 0.5 * i) for i in range(6)]
        acsT = sb("acs_t", [NH, SEQ], 116)
        S = sb("scores", [P, 2, GQ, P], 128)
        Pr = sb("probs", [P, 2, GQ, P], 132)
        pt = sb("probs_t", [P, GQ, P], 136)
        ptc = sb("probs_t_cur", [P, GQ, P], 138)
        ptp = sb("probs_t_prev", [P, GQ, P], 140)
        ag_of = [sb(f"decay{i}", [P, 3, HG, P], o) for i, o in enumerate((128, 160))]
        xc_of = [sb(f"xdt{i}", [P, SEQ], o) for i, o in enumerate((140, 172))]
        xcd_of = [sb(f"xdt_decayed{i}", [P, SEQ], o) for i, o in enumerate((142, 174))]
        e2 = sb("decay_off", [P, TG, P], 176)
        st = sb("state", [P, SEQ], 178)
        yo = sb("y_off", [P, SEQ], 180)
        bncb = sb("b_nat_cb", [P, 2 * P], 182)
        cbm = sb("cb_masked", [P, P], 183)
        gsd = sb("group_rms", [P, SEQ], 203.5)
        sq1 = sb("y_sq_pair", [P, 2 * P], 205.5)
        sq2 = sb("y_sq_sum", [P, P], 206.5)
        mix_hi = sb("mix_hi", [P, KT, SEQ], 144, F32R)
        mix_lo = sb("mix_lo", [P, KT, SEQ], 160, F32R)
        h = sb("h", [P, NT, D], 0)
        hn_hi = sb("hn_hi", [P, KT, SEQ], 16, F32R)
        hn_lo = sb("hn_lo", [P, KT, SEQ], 80, F32R)
        hsc = sb("h_scaled", [P, 2, D], 100)
        n2row = sb("norm2_row", [P, D], 108)
        hjunk = sb("h_junk", [P, D], 96)
        act_hi = sb("act_hi", [P, FT, SEQ], 96, F32R)
        act_lo = sb("act_lo", [P, FT, SEQ], 140, F32R)
        ga2 = sb("gated", [P, 2, SEQ], 203.5)
        fnw = sb("final_norm_row", [P, D], 16)
        fo = sb("final_out", [P, NT, D], 80)
        fjunk = sb("f_junk", [P, 512], 28)
        ident = sb("ident", [P, P], 192)
        ones = sb("ones", [P, P], 192.5)
        tri = sb("tri", [P, P], 193)
        mprevT = sb("mask_prev_t", [P, P], 194)
        mprev = sb("mask_prev", [P, P], 194.5, I32)
        negt = sb("neg_tile", [P, P], 195)
        pcol = sb("param_cols", [P, 3, P], 195.5)
        small = sb("small", [P, 512], 197)
        dt = sb("dt", [P, NT, NH], 199)
        nacs = sb("neg_acs", [P, NT, NH], 199.5)
        ddt = sb("dt_decay", [P, 2, HG], 200)
        cdec = sb("chunk_decay", [P, 2, HG], 200.125)
        dsk = sb("d_cols", [P, 16], 200.25)
        dtr = sb("dt_raw", [P, NT, NH], 200.5)
        nA = sb("neg_a", [P, NH], 201)
        dtb = sb("dt_bias", [P, NH], 201.25)
        cwh = sb("half_conv", [P, P], 201.5)
        fwh = sb("half_ffn", [P, 4, FT], 202)
        bgh = sb("half_gate_bias", [P, 16], 202.5)
        PS = ctx.enter_context(nc.psum_tensor("banks", [P, 8, 512], F32))

        NX = XBC // P
        PARAM_SIZES = (5 * NX, P, 4 * FT)
        CW = lambda k, t: cwh[:, k * NX + t:k * NX + t + 1]
        CB = lambda t: cwh[:, 4 * NX + t:4 * NX + t + 1]
        bg0 = 4 * FT + KT
        snw = pcol[:, 1, bg0 + 16:bg0 + 32]

        def FW(k, t):
            if t >= FT:
                return fwh[:, k, t - FT:t - FT + 1]
            if k < 2:
                return pcol[:, 1, k * 2 * FT + t:k * 2 * FT + t + 1]
            o = (k - 2) * 2 * FT + t
            return pcol[:, 2, o:o + 1]

        ss, sd, rs = small[:, 0:8], small[:, 8:16], small[:, 16:24]
        mx, m_, nm, rsum, es, den, rden = [small[:, 104 + 8 * k:112 + 8 * k].rearrange("p (b j) -> p b j", b=2)
                                           for k in range(7)]
        snk = small[:, 52:68]
        epsc = small[:, 68:69]
        dd8 = small[:, 72:80]
        fss, fsd, frs = small[:, 80:84], small[:, 84:88], small[:, 88:92]
        fhs, fhb = small[:, 160:164], small[:, 164:168]
        hss, hsd, hrs = small[:, 92:96], small[:, 96:100], small[:, 100:104]

        acs_d = nc.dram_tensor("acs_scratch", [NH, SEQ], F32, kind="Internal").ap()
        mixa_d = nc.dram_tensor("mixa_scratch", [KT, P, SEQ], F32, kind="Internal").ap()
        gs_d = nc.dram_tensor("gs_scratch", [KT, P, SEQ], F32, kind="Internal").ap()

        PARAM_ROWS = [
            (stage[0:96, 0, :], ssd_conv_w[0].rearrange("k (t p) -> (k t) p", p=P)),
            (stage[96:120, 0, :], ssd_conv_b[0].rearrange("(t p) -> t p", p=P)),
            (stage[0:88, 1, :], ffn_conv_w[0, 0:2].rearrange("k (t p) -> (k t) p", p=P)),
            (stage[88:96, 1, :], norm2_w[0].rearrange("(t p) -> t p", p=P)),
            (stage[96:112, 1, :], b_gate[0].rearrange("(t p) -> t p", p=P)),
            (stage[112:128, 1, :], ssd_norm_w[0].rearrange("(t p) -> t p", p=P)),
            (stage[0:44, 2, :], ffn_conv_w[0, 2].rearrange("(t p) -> t p", p=P)),
            (stage[44:88, 2, :], ffn_conv_b[0].rearrange("(t p) -> t p", p=P)),
            (dtb[:, :], dt_bias[0].unsqueeze(0).broadcast_to([P, NH])),
            (nA[:, :], a_log[0].unsqueeze(0).broadcast_to([P, NH])),
            (dskb[:, :], d_skip[0].unsqueeze(0).broadcast_to([P, NH])),
            (snk, attn_sinks[0].unsqueeze(0).broadcast_to([P, HQ])),
        ]

        def sem(name):
            return ctx.enter_context(nc.semaphore(name))

        n1_in, n2_in = sem("norm1_in"), sem("norm2_in")
        x_in = [sem(f"x_in{t}") for t in range(NT)]
        params_in = sem("params_in")
        w_in_slot = [sem(f"w_loaded{i}") for i in range(2)]
        w_rounded, w_split = sem("w_rounded"), sem("w_split")
        consts = sem("consts")
        pcols_t, pcols = sem("param_transposed"), sem("params_ready")
        gemm_done = sem("gemm_done")
        n_sq, n_sd, n_rs, n_sc, n_tp, n_tw, n_hi, n_lo = [sem("n_" + s) for s in (
            "squared", "root", "rstd", "scaled", "transposed", "weighted", "hi", "lo")]
        n_tab = sem("root_table")
        qk_ready = sem("qk_ready")
        vd_done, v_ready = sem("vd_done"), sem("v_ready")
        spc, spa, spd, da_ready = sem("softplus_abs"), sem("softplus_exp"), sem("softplus_steps"), sem("da_ready")
        acs_mm, acs_ev, acs_out, acs_tp, acs_nat = [sem("acs_" + s) for s in ("mm", "copied", "stored", "t", "nat")]
        c_acc, c_tap, c_tanh, c_out = [sem("conv_" + s) for s in ("bias", "tap", "tanh", "out")]
        z_tanh, z_out = sem("z_tanh"), sem("z_out")
        g_tanh, ao_out, gs_tanh = sem("ga_tanh"), sem("ao_gated"), sem("gs_tanh")
        ao_sp = [sem(f"ao_spilled{j}") for j in range(2)]
        gs_sp = [sem(f"gs_spilled{j}") for j in range(2)]
        a_sc, a_cur, a_sel, a_max, a_m, a_nm, a_exp, a_es, a_den, a_rd, a_pr = [sem("att_" + s) for s in (
            "scores", "cur", "selected", "max", "m", "negm", "exp", "sink", "den", "rden", "probs")]
        a_df = sem("att_sinkdiff")
        a_tp, a_pt, a_ptc, a_ptp, a_pv, a_oh, a_ol = [sem("att_" + s) for s in (
            "transposed", "pt", "ptc", "ptp", "pv", "hi", "lo")]
        d_ab = [sem(f"ssd_acs_in{i}") for i in range(3)]
        d_e2 = sem("ssd_acs2_in")
        (d_x, d_bc, d_bcs, d_seg, d_cbm, d_exp, d_m, d_e2x, d_dd, d_de, d_cd, d_ddt, d_xc, d_xcd, d_dxs, d_stt, d_stm,
         d_mm, d_yo, d_yd, d_yx, d_y, d_sq, d_s1, d_s2, d_sum, d_stp) = [sem("ssd_" + s) for s in (
             "xs_t", "b_cb", "b_cb_copied", "seg", "cb_masked", "exp", "m", "e2", "dd", "dexp", "cdec", "ddt", "xc", "xcd",
             "dxs", "st_mm", "st_scaled", "diag", "yoff", "yadd", "yskip", "y", "sq", "sq1", "sq2", "sum", "state")]
        g_sd, g_rs, g_w, g_hi, g_lo = [sem("gnorm_" + s) for s in ("root", "rstd", "weighted", "hi", "lo")]
        so_in = [sem(f"so_in{j}") for j in range(2)]
        so_g, so_a, so_hi, so_lo = [sem("so_" + s) for s in ("gated", "added", "hi", "lo")]
        h_in = sem("h_x_in")
        out_done, h_add = sem("out_done"), sem("h_added")
        u_acc, u_tap, u_tanh, u_silu, u_mul, u_hi, u_lo = [sem("up_" + s) for s in (
            "bias", "tap", "tanh", "silu", "mul", "hi", "lo")]
        dn_done, dn_add = sem("down_done"), sem("down_added")
        f_sq, f_sd, f_rs, f_out, fnw_in = [sem("final_" + s) for s in ("squared", "root", "rstd", "weighted", "row_in")]
        f_st, f_bias = sem("final_stored"), sem("final_first_half")

        win = w_in[0]

        def down_tiles(i):
            sizes = (3, 3, 4, 4, 4, 4)
            kc = i % 6
            return sum(sizes[:kc]), sizes[kc]

        def chunk_dmas(c):
            kind, i = CHUNKS[c]
            slot = raw[:, c % 2, :]

            def cols(w, k0, nk, c0, nc_):
                return w[k0 * P:(k0 + nk) * P, c0:c0 + nc_].rearrange("(t p) n -> p t n", p=P)

            a = slot.rearrange("p (t n) -> p t n", t=KT)
            b = slot.rearrange("p (t n) -> p t n", t=4)
            if kind == "k":
                return [(a, cols(win, 0, KT, K0, 256))]
            if kind == "q":
                res = []
                for u in range(2):
                    t = 2 * i + u
                    G, j = t // GQ, t % GQ
                    for hh in range(2):
                        c0 = Q0 + ((2 * G + hh) * GQ + j) * HD
                        res.append((a[:, :, u * P + hh * HD:u * P + (hh + 1) * HD], cols(win, 0, KT, c0, HD)))
                return res
            if kind == "vd":
                s = slot[:, 0:4 * VW].rearrange("p (t n) -> p t n", t=4)
                return [(s[:, :, 0:HKV * HD], cols(win, 4 * i, 4, V0, HKV * HD)),
                        (s[:, :, HKV * HD:VW], cols(win, 4 * i, 4, DT0, NH))]
            c0 = {"bc": B0, "xs": X0, "z": Z0, "ga": GA0, "gs": GS0}.get(kind)
            if c0 is not None:
                return [(a, cols(win, 0, KT, c0 + 256 * i, 256))]
            if kind == "ao":
                res = []
                for G in range(2):
                    for hh in range(2):
                        r0 = (2 * G + hh) * GQ * HD
                        src = w_attn_o[0][r0:r0 + GQ * HD, 256 * i:256 * i + 256].rearrange("(j d) n -> d j n", d=HD)
                        res.append((a[hh * HD:(hh + 1) * HD, G * GQ:(G + 1) * GQ, :], src))
                return res
            if kind == "so":
                f, kh = i
                return [(a, cols(w_ssd_o[0], KT * kh, KT, 256 * f, 256))]
            if kind == "out":
                return [(b, cols(w_out[0], 4 * (i % 2), 4, 512 * (i // 2), 512))]
            if kind == "up":
                return [(a, cols(w_up[0], 0, KT, (i % 2) * FF + 256 * (i // 2), 256))]
            if kind == "down":
                nh, (k0, nk) = i // 6, down_tiles(i)
                return [(b[:, 0:nk, :], cols(w_down[0], k0, nk, 512 * nh, 512))]

        def tiles_in(c):
            kind, i = CHUNKS[c]
            if kind == "vd":
                return 4, VW
            if kind == "down":
                return down_tiles(i)[1], 512
            return (4, 512) if kind == "out" else (KT, 256)

        def halves(c):
            n, w = tiles_in(c)
            return (0, (n // 2) * w), ((n // 2) * w, n * w)

        loads_before = []
        _cnt = [0, 0]
        for c in range(len(CHUNKS)):
            _cnt[c % 2] += 16 * len(chunk_dmas(c))
            loads_before.append(_cnt[c % 2])

        f32 = lambda t: t.bitcast(F32)
        block = ctx.enter_context(nc.Block())

        @block.sync
        def _(eng):
            for c in range(len(CHUNKS)):
                for t in ((0, 1), (2, 3))[c] if c < 2 else ():
                    eng.dma_start(xnat[:, t, :], x[0, t * P:(t + 1) * P, :]).then_inc(x_in[t], 16)
                    if t == 0:
                        eng.dma_start(n1row[:, :], norm1_w[0].unsqueeze(0).broadcast_to([P, D])).then_inc(n1_in, 16)
                if c >= 2:
                    eng.wait_ge(w_split, 2 * (c - 1))
                for dst, src in chunk_dmas(c):
                    eng.dma_start(dst, src).then_inc(w_in_slot[c % 2], 16)
                if c == AT[("so", (2, 1))]:
                    eng.wait_ge(gemm_done, DONE[AT[("gs", 3)]])
                    eng.dma_start(h[:, :, :], x[0].rearrange("(t p) n -> p t n", p=P)).then_inc(h_in, 16)
                if c == AT[("out", 3)]:
                    eng.wait_ge(gemm_done, DONE[AT[("so", (3, 1))]])
                    eng.dma_start(n2row[:, :], norm2_w[0].unsqueeze(0).broadcast_to([P, D])).then_inc(n2_in, 16)
                if c == AT[("down", 3)]:
                    eng.wait_ge(gemm_done, DONE[AT[("up", 21)]])
                    eng.dma_start(fnw[:, :], final_norm_w.unsqueeze(0).broadcast_to([P, D])).then_inc(fnw_in, 16)
            for t in range(NT):
                for nh in range(2) if t == NT - 1 else (slice(0, 2),):
                    eng.wait_ge(f_out, 2 * t + (1 if nh == 0 else 2))
                    cols = slice(0, D) if t < NT - 1 else slice(nh * 512, nh * 512 + 512)
                    eng.dma_start(out[0, t * P:(t + 1) * P, cols], fo[:, t, cols]).then_inc(f_st, 16)
            eng.wait_ge(f_st, 16 * (NT + 1))

        @block.gpsimd
        def _(eng):
            n = [0]

            def made(ins):
                n[0] += 1
                ins.then_inc(consts, 1)

            made(eng.memset(epsc, EPS))
            for t_, val in ((ident, 0.0), (ones, 1.0), (tri, 1.0), (mprevT, 1.0), (negt, NEG)):
                made(eng.memset(t_[:, :], val))
            made(eng.memset(f32(mprev[:, :]), 1.0))
            eng.wait_ge(consts, 7)
            made(eng.affine_select(out=ident[:, :], in_=ident[:, :], compare_op=ALU.not_equal, fill=1.0, base=0,
                                   pattern=[[-1, P]], channel_multiplier=1))
            made(eng.affine_select(out=tri[:, :], in_=tri[:, :], compare_op=ALU.is_ge, fill=0.0, base=0,
                                   pattern=[[1, P]], channel_multiplier=-1))
            made(eng.affine_select(out=mprevT[:, :], in_=mprevT[:, :], compare_op=ALU.is_gt, fill=0.0, base=0,
                                   pattern=[[-1, P]], channel_multiplier=1))
            made(eng.affine_select(out=f32(mprev[:, :]), in_=f32(mprev[:, :]), compare_op=ALU.is_gt, fill=0.0,
                                   base=0, pattern=[[1, P]], channel_multiplier=-1))

            for dst, src in PARAM_ROWS:
                eng.dma_start(dst, src).then_inc(params_in, 16)

            eng.wait_ge(acs_ev, 1)
            eng.dma_start(acs_d, acsT[:, :]).then_inc(acs_out, 16)

            for c, (kind, i) in enumerate(CHUNKS):
                if kind == "so" and i[1] == 1:
                    if i[0] == 0:
                        eng.wait_ge(c_out, 24)
                    for j in range(2):
                        f = 2 * i[0] + j
                        if i[0] == 0:
                            eng.wait_ge(ao_sp[j], 16 * 4)
                            eng.wait_ge(gs_sp[j], 16 * 4)
                        else:
                            eng.wait_ge(so_lo, 2 * (i[0] - 1) + j + 1)
                        eng.dma_start(cacc[:, j, :], mixa_d[f]).then_inc(so_in[j], 16)
                        eng.dma_start(cth[:, j, :], gs_d[f]).then_inc(so_in[j], 16)
                for u in range(2):
                    if kind == "ao":
                        eng.wait_ge(ao_out, 2 * i + u + 1)
                        eng.dma_start(mixa_d[2 * i + u], cacc[:, u, :]).then_inc(ao_sp[u], 16)
                    if kind == "gs":
                        eng.wait_ge(gs_tanh, 2 * i + u + 1)
                        eng.dma_start(gs_d[2 * i + u], cth[:, u, :]).then_inc(gs_sp[u], 16)
                    for n, what in rides_at("POOL", c, u):
                        if what == "ptp":
                            if True:
                                k = n
                                eng.wait_ge(a_pt, k + 1)
                                if k:
                                    eng.wait_ge(a_pv, k)
                                eng.tensor_tensor(ptp[:, :, :], pt[:, :, :],
                                                  mprevT[:, :].unsqueeze(1).broadcast_to([P, GQ, P]),
                                                  ALU.mult).then_inc(a_ptp, 1)
                        elif what == "seg":
                            g, cc = n // NT, n % NT
                            ag = ag_of[n // 8][:, n % 3, :, :]
                            eng.wait_ge(d_cd, n + 1)
                            eng.wait_ge(d_dd, n + 1)
                            for hd in range(HG):
                                ins = eng.tensor_scalar(ag[:, hd, :], ag[:, hd, :], nacs[:, cc, HG * g + hd:HG * g + hd + 1],
                                                        0.0, ALU.add, ALU.min)
                            ins.then_inc(d_seg, 1)
                        elif what == "dxs":
                            g, cc = n // NT, n % NT
                            eng.wait_ge(d_x, n + 1)
                            eng.wait_ge(pcols, 11)
                            v_ = xs[:, TG * g:TG * g + TG, cc * P:(cc + 1) * P]
                            eng.tensor_tensor(v_, v_, dsk[:, TG * g:TG * g + TG].unsqueeze(2)
                                              .broadcast_to([P, TG, P]), ALU.mult).then_inc(d_dxs, 1)
                        elif what == "ysq":
                            eng.wait_ge(d_sq, n + 1)
                            if n:
                                eng.wait_ge(d_s2, n)
                            eng.tensor_tensor(sq1[:, :], yo[:, 0:2 * P], yo[:, 2 * P:4 * P], ALU.add).then_inc(d_s1, 1)
                            eng.wait_ge(d_s1, n + 1)
                            if n:
                                eng.wait_ge(d_sum, n)
                            eng.tensor_tensor(sq2[:, :], sq1[:, 0:P], sq1[:, P:2 * P], ALU.add).then_inc(d_s2, 1)

        @block.scalar
        def _(eng):
            A = nc.scalar
            def split(c):
                eng.wait_ge(w_in_slot[c % 2], loads_before[c])
                if c >= 2:
                    eng.wait_ge(gemm_done, DONE[c - 2])
                for lo_, hi_ in halves(c):
                    A.activation(whi[:, c % 2, lo_:hi_], raw[:, c % 2, lo_:hi_], ACT.Copy).then_inc(w_rounded, 1)

            def norm_square(t, k, src, scratch, total, root):
                if k:
                    eng.wait_ge(n_sq, k)
                A.activation(scratch, src[:, t, :], ACT.Square, accum_out=total[:, t:t + 1]).then_inc(n_sq, 1)
                eng.wait_ge(n_sq, k + 1)
                A.activation(root[:, t:t + 1], total[:, t:t + 1], ACT.Sqrt, bias=epsc, scale=1.0 / D).then_inc(n_sd, 1)

            def norm_round(t, k, hi):
                for hf in range(2):
                    eng.wait_ge(n_tp, 2 * k + hf + 1)
                    A.activation(hi[:, hf * KT // 2:(hf + 1) * KT // 2, t * P:(t + 1) * P],
                                 PS[:, 4 + 2 * (t % 2) + hf, :].rearrange("p (k l) -> p k l", l=P),
                                 ACT.Copy).then_inc(n_hi, 1)

            def rides(c, u, slot):
                for n, what in rides_at("ACT", c, u, slot):
                    if what == "acs":
                        eng.wait_ge(acs_mm, 1)
                        A.activation(acsT[:, :], PS[0:NH, 2, :], ACT.Copy).then_inc(acs_ev, 1)
                    elif what == "cur":
                        eng.wait_ge(a_sc, n + 1)
                        if n >= 2:
                            eng.wait_ge(a_exp, GQ * (n - 1))
                        sv = PS[:, 2 + 2 * (n % 2):4 + 2 * (n % 2), :].rearrange("p b (j s) -> p (b j) s", j=2)
                        A.activation(S[:, n % 2, :, :], sv[:, :, P:2 * P], ACT.Copy).then_inc(a_cur, 1)
                    elif what == "exp":
                        eng.wait_ge(a_nm, n + 1)
                        if n >= 2:
                            eng.wait_ge(a_tp, n - 1)
                        for j in range(GQ):
                            A.activation(Pr[:, n % 2, j, :], S[:, n % 2, j, :], ACT.Exp, bias=nm[:, n % 2, j:j + 1],
                                         accum_out=rsum[:, n % 2, j:j + 1]).then_inc(a_exp, 1)
                        eng.wait_ge(a_df, n + 1)
                        A.activation(es[:, n % 2, :], es[:, n % 2, :], ACT.Exp).then_inc(a_es, 1)
                    elif what == "pt":
                        eng.wait_ge(a_tp, n + 1)
                        if n:
                            eng.wait_ge(a_ptc, n)
                            eng.wait_ge(a_ptp, n)
                        A.activation(pt[:, :, :], PS[:, 6, :].rearrange("p (j q) -> p j q", j=GQ),
                                     ACT.Copy).then_inc(a_pt, 1)
                    elif what == "oh":
                        g, b = att_step(n)
                        o = (g % 2) * HD
                        eng.wait_ge(a_pv, n + 1)
                        A.activation(a_hi[o:o + HD, (g // 2) * GQ:(g // 2) * GQ + GQ, b * P:(b + 1) * P],
                                     PS[o:o + HD, 7, :].rearrange("p (j q) -> p j q", j=GQ),
                                     ACT.Copy).then_inc(a_oh, 1)
                    elif what == "load":
                        g, cc = n // NT, n % NT
                        if n == 0:
                            eng.wait_ge(acs_out, 16)
                            eng.wait_ge(a_ol, N_ATT)
                        if n == 8:
                            eng.wait_ge(gemm_done, DONE[AT[("ao", 3)]])
                        if n >= 3:
                            eng.wait_ge(d_mm, n - 2)
                        rows_ = acs_d[HG * g:HG * g + HG, cc * P:(cc + 1) * P]
                        eng.dma_start(ag_of[n // 8][:, n % 3, :, :],
                                      rows_.unsqueeze(0).broadcast_to([P, HG, P])).then_inc(d_ab[n % 3], 16)
                    elif what == "dec":
                        a_ = ag_of[n // 8][:, n % 3, :, :]
                        eng.wait_ge(d_ab[n % 3], 16 * (n // 3 + 1))
                        if n >= 2:
                            eng.wait_ge(d_y, n - 1)
                        A.activation(cdec[:, n % 2, :], a_[:, :, P - 1], ACT.Exp).then_inc(d_cd, 1)
                        eng.wait_ge(d_dd, n + 1)
                        A.activation(dd8, dd8, ACT.Exp).then_inc(d_de, 1)
                    elif what == "dexp":
                        a_ = ag_of[n // 8][:, n % 3, :, :]
                        eng.wait_ge(d_seg, n + 1)
                        A.activation(a_, a_, ACT.Exp).then_inc(d_exp, 1)
                    elif what == "e2load":
                        g, cc = n // NT, n % NT
                        if n:
                            eng.wait_ge(d_y, n)
                        for hh in range(2):
                            src = acs_d[HG * g:HG * g + HG, cc * P:(cc + 1) * P].rearrange("(i two) l -> two i l", two=2)[hh]
                            eng.dma_start(e2[hh * HD:(hh + 1) * HD, :, :],
                                          src.unsqueeze(0).broadcast_to([HD, TG, P])).then_inc(d_e2, 16)
                    elif what == "bcs":
                        eng.wait_ge(d_bc, n + 1)
                        if n:
                            eng.wait_ge(d_cbm, n)
                            eng.wait_ge(d_mm, n)
                        A.activation(bncb[:, :], PS[:, 3, 0:2 * P], ACT.Copy).then_inc(d_bcs, 1)
                    elif what == "e2x":
                        eng.wait_ge(d_e2, 32 * (n + 1))
                        A.activation(e2[:, :, :], e2[:, :, :], ACT.Exp).then_inc(d_e2x, 1)
                    elif what == "sq":
                        g, cc = n // NT, n % NT
                        eng.wait_ge(d_y, n + 1)
                        A.activation(yo[:, :].rearrange("p (i l) -> p i l", i=TG),
                                     sz[:, TG * g:TG * g + TG, cc * P:(cc + 1) * P], ACT.Square).then_inc(d_sq, 1)
                    elif what == "gnorm":
                        gg, part = n
                        f = TG * gg + part - 1
                        if part == 0:
                            eng.wait_ge(d_sum, NT * (gg + 1))
                            if gg:
                                eng.wait_ge(g_w, TG * gg)
                            A.activation(gsd[:, :], PS[:, 7, :], ACT.Sqrt, bias=epsc, scale=1.0 / (TG * P)).then_inc(g_sd, 1)
                        else:
                            eng.wait_ge(g_w, f + 1)
                            A.activation(y_hi[:, f, :], sz[:, f, :], ACT.Copy).then_inc(g_hi, 1)

            eng.wait_ge(consts, 1)
            A.activation(small[:, 168:169], epsc, ACT.Sqrt).then_inc(n_tab, 1)
            for t in range(NT):
                eng.wait_ge(x_in[t], 16)
                norm_square(t, t, xnat, junk[:, :], ss, sd)
                if t == 1:
                    split(0)
                if t:
                    norm_round(t - 1, t - 1, xn_hi)
            split(1)
            norm_round(NT - 1, NT - 1, xn_hi)
            k_conv = k_z = k_gs = 0
            for c, (kind, i) in enumerate(CHUNKS):
                if 1 < c + 1 < len(CHUNKS) and c not in (AT[("out", 3)], AT[("up", 0)]):
                    split(c + 1)
                for u in range(2):
                    rides(c, u, 0)
                    if kind in ("k", "q"):
                        eng.wait_ge(gemm_done, DONE[c, u])
                        if kind == "k":
                            A.activation(kT[:, u, :], PS[:, u, :], ACT.Copy).then_inc(qk_ready, 1)
                        else:
                            A.activation(qT[:, 2 * i + u, :], PS[:, u, :], ACT.Copy,
                                         scale=HD ** -0.5).then_inc(qk_ready, 1)
                    elif kind in ("bc", "xs"):
                        t = 2 * i + u + (16 if kind == "bc" else 0)
                        eng.wait_ge(gemm_done, DONE[c, u])
                        if k_conv == 0:
                            eng.wait_ge(pcols, 11)
                        if kind == "xs" and i == 4:
                            eng.wait_ge(ao_sp[u], 16 * 4)
                        if k_conv >= 2:
                            eng.wait_ge(c_out, k_conv - 1)
                        A.activation(cacc[:, u, :], PS[:, u, :], ACT.Identity, bias=CB(t),
                                     scale=CW(3, t)).then_inc(c_acc, 1)
                        rides(c, u, 1)
                        eng.wait_ge(c_tap, 3 * k_conv + 3)
                        A.activation(cth[:, u, :], cacc[:, u, :], ACT.Tanh).then_inc(c_tanh, 1)
                        k_conv += 1
                    elif kind == "z":
                        eng.wait_ge(gemm_done, DONE[c, u])
                        eng.wait_ge(c_out, k_conv)
                        if k_z >= 2:
                            eng.wait_ge(z_out, k_z - 1)
                        A.activation(cth[:, u, :], PS[:, u, :], ACT.Tanh, scale=0.5).then_inc(z_tanh, 1)
                        k_z += 1
                    elif kind == "ga":
                        eng.wait_ge(gemm_done, DONE[c, u])
                        eng.wait_ge(z_out, k_z)
                        if i:
                            eng.wait_ge(ao_out, 2 * (i - 1) + u + 1)
                        A.activation(cth[:, u, :], PS[:, u, :], ACT.Tanh, scale=0.5,
                                     bias=bgh[:, 2 * i + u:2 * i + u + 1]).then_inc(g_tanh, 1)
                    elif kind == "gs":
                        eng.wait_ge(gemm_done, DONE[c, u])
                        eng.wait_ge(z_out, k_z)
                        if i:
                            eng.wait_ge(gs_sp[u], 16 * i)
                        A.activation(cth[:, u, :], PS[:, u, :], ACT.Tanh, scale=0.5,
                                     bias=bgh[:, 8 + 2 * i + u:8 + 2 * i + u + 1]).then_inc(gs_tanh, 1)
                    elif kind == "so" and i[1] == 1:
                        f = 2 * i[0] + u
                        eng.wait_ge(so_a, f + 1)
                        A.activation(mix_hi[:, f, :], cacc[:, u, :], ACT.Copy, scale=0.5).then_inc(so_hi, 1)
                    elif kind == "up":
                        k = 2 * i + u
                        t = (i % 2) * FT + 2 * (i // 2) + u
                        b = 2 * (i % 2) + u
                        it = i // 2
                        dst = cacc[:, u, :] if i % 2 == 0 else ga2[:, u, :]
                        eng.wait_ge(gemm_done, DONE[c, u])
                        if it:
                            eng.wait_ge(u_lo if i % 2 else u_mul, 2 * (it - 1) + u + 1)
                        A.activation(dst, PS[:, b, :], ACT.Identity, bias=FW(3, t), scale=FW(2, t)).then_inc(u_acc, 1)
                        if i % 2:
                            eng.wait_ge(u_tap, 2 * k + 2)
                            A.activation(cth[:, u, :], ga2[:, u, :], ACT.Tanh).then_inc(u_tanh, 1)
                            f = 2 * it + u
                            eng.wait_ge(u_mul, f + 1)
                            A.activation(act_hi[:, f, :], ga2[:, u, :], ACT.Copy).then_inc(u_hi, 1)
                    if kind not in ("bc", "xs"):
                        rides(c, u, 1)
                    if kind == "vd" and i == 1 and u == 1:
                        eng.wait_ge(params_in, 16 * len(PARAM_ROWS))
                        A.activation(nA[:, :], nA[:, :], ACT.Exp).then_inc(spa, 1)
                        eng.wait_ge(spc, 1)
                        A.activation(sp[0][:, :], sp[0][:, :], ACT.Exp, scale=-1.0).then_inc(spa, 1)
                    rides(c, u, 2)
                if kind == "out" and i == 3:
                    for t in range(NT):
                        eng.wait_ge(h_add, NT + t + 1)
                        norm_square(t, NT + t, h, hjunk[:, :], hss, hsd)
                        if t == NT - 1:
                            split(c + 2)
                        if t:
                            norm_round(t - 1, NT + t - 1, hn_hi)
                        if t == NT - 2:
                            split(c + 1)
                    norm_round(NT - 1, 2 * NT - 1, hn_hi)
                if kind == "down" and i == 8:
                    for t in range(NT):
                        eng.wait_ge(dn_add, t + 1)
                        if t:
                            eng.wait_ge(f_sq, t)
                        A.activation(fjunk[:, :], h[:, t, 0:512], ACT.Square, accum_out=fhs[:, t:t + 1]).then_inc(f_sq, 1)
            for t in range(NT):
                eng.wait_ge(dn_add, NT + t + 1)
                if t == 0:
                    eng.wait_ge(f_bias, 1)
                eng.wait_ge(f_sq, NT + t)
                A.activation(fjunk[:, :], h[:, t, 512:D], ACT.Square, accum_out=fss[:, t:t + 1]).then_inc(f_sq, 1)
                eng.wait_ge(f_sq, NT + t + 1)
                A.activation(fsd[:, t:t + 1], fss[:, t:t + 1], ACT.Sqrt, bias=fhb[:, t:t + 1], scale=1.0 / D).then_inc(f_sd, 1)

        @block.vector
        def _(eng):
            V = nc.vector

            def bcast(cols, n, width):
                return cols.unsqueeze(2).broadcast_to([P, n, width])

            def split(c):
                for k, (lo_, hi_) in enumerate(halves(c)):
                    eng.wait_ge(w_rounded, 2 * c + k + 1)
                    V.tensor_tensor(wlo[:, c % 2, lo_:hi_], raw[:, c % 2, lo_:hi_], f32(whi[:, c % 2, lo_:hi_]),
                                    ALU.subtract).then_inc(w_split, 1)

            def norm_scale(t, k, src, root, inv, dst, row):
                eng.wait_ge(n_sd, k + 1)
                V.reciprocal(inv[:, t:t + 1], root[:, t:t + 1]).then_inc(n_rs, 1)
                eng.wait_ge(n_rs, k + 1)
                if t == 0:
                    eng.wait_ge(n2_in if k else n1_in, 16)
                if k >= 2:
                    eng.wait_ge(n_tp, 2 * (k - 1))
                V.scalar_tensor_tensor(out=dst[:, t % 2, :], in0=src[:, t, :], scalar=inv[:, t:t + 1], in1=row[:, :],
                                       op0=ALU.mult, op1=ALU.mult).then_inc(n_sc, 1)

            def norm_lo(t, k, hi, lo):
                for hf in range(2):
                    eng.wait_ge(n_hi, 2 * k + hf + 1)
                    part = (slice(0, P), slice(hf * KT // 2, (hf + 1) * KT // 2), slice(t * P, (t + 1) * P))
                    V.tensor_tensor(lo[part], PS[:, 4 + 2 * (t % 2) + hf, :].rearrange("p (k l) -> p k l", l=P),
                                    f32(hi[part]), ALU.subtract).then_inc(n_lo, 1)

            def final_tile(t):
                if t == 0:
                    eng.wait_ge(fnw_in, 16)
                eng.wait_ge(f_sd, t + 1)
                V.reciprocal(frs[:, t:t + 1], fsd[:, t:t + 1]).then_inc(f_rs, 1)
                eng.wait_ge(f_rs, t + 1)
                for nh in range(2):
                    half_ = slice(nh * 512, nh * 512 + 512)
                    V.scalar_tensor_tensor(out=fo[:, t, half_], in0=h[:, t, half_], scalar=frs[:, t:t + 1],
                                           in1=fnw[:, half_], op0=ALU.mult, op1=ALU.mult).then_inc(f_out, 1)

            n_yo = n_yx = n_stm = 0

            def rides(c, u, slot):
                nonlocal n_yo, n_yx, n_stm
                for n, what in rides_at("DVE", c, u, slot):
                    if what == "gnorm":
                        gg, part = n
                        f = TG * gg + part - 1
                        if part == 0:
                            eng.wait_ge(g_sd, gg + 1)
                            V.reciprocal(gsd[:, :], gsd[:, :]).then_inc(g_rs, 1)
                        else:
                            eng.wait_ge(g_rs, gg + 1)
                            V.scalar_tensor_tensor(out=sz[:, f, :], in0=sz[:, f, :], scalar=snw[:, f:f + 1],
                                                   in1=gsd[:, :], op0=ALU.mult, op1=ALU.mult).then_inc(g_w, 1)
                            eng.wait_ge(g_hi, f + 1)
                            V.tensor_tensor(y_lo[:, f, :], sz[:, f, :], f32(y_hi[:, f, :]),
                                            ALU.subtract).then_inc(g_lo, 1)
                        continue
                    g, cc = n // NT, n % NT
                    hs = slice(HG * g, HG * g + HG)
                    ag, xc, xcd = ag_of[n // 8][:, n % 3, :, :], xc_of[n // 8], xcd_of[n // 8]
                    if what == "acs":
                        eng.wait_ge(acs_tp, 1)
                        V.tensor_scalar(nacs[:, :, :].rearrange("p t h -> p (t h)"), PS[:, 3, 0:NT * NH],
                                        -1.0, None, ALU.mult).then_inc(acs_nat, 1)
                    elif what == "sel":
                        g, b_ = att_step(n)
                        k = n % 2
                        snk_ = snk[:, GQ * g:GQ * g + GQ]
                        eng.wait_ge(a_cur, n + 1)
                        if b_:
                            prev = PS[:, 2 + 2 * k:4 + 2 * k, :].rearrange("p b (j s) -> p (b j) s", j=2)[:, :, 0:P]
                        else:
                            prev = negt[:, :].unsqueeze(1).broadcast_to([P, GQ, P])
                        V.copy_predicated(S[:, k, :, :], mprev[:, :].unsqueeze(1).broadcast_to([P, GQ, P]),
                                          prev).then_inc(a_sel, 1)
                        eng.wait_ge(a_sel, n + 1)
                        V.tensor_reduce(mx[:, k, :], S[:, k, :, :], AX.X, ALU.max).then_inc(a_max, 1)
                        eng.wait_ge(a_max, n + 1)
                        V.tensor_tensor(m_[:, k, :], mx[:, k, :], snk_, ALU.max).then_inc(a_m, 1)
                        eng.wait_ge(a_m, n + 1)
                        V.tensor_scalar(nm[:, k, :], m_[:, k, :], -1.0, None, ALU.mult).then_inc(a_nm, 1)
                        V.tensor_tensor(es[:, k, :], snk_, m_[:, k, :], ALU.subtract).then_inc(a_df, 1)
                    elif what == "pr":
                        k = n % 2
                        eng.wait_ge(a_exp, GQ * (n + 1))
                        eng.wait_ge(a_es, n + 1)
                        V.tensor_tensor(den[:, k, :], rsum[:, k, :], es[:, k, :], ALU.add).then_inc(a_den, 1)
                        eng.wait_ge(a_den, n + 1)
                        V.reciprocal(rden[:, k, :], den[:, k, :]).then_inc(a_rd, 1)
                        eng.wait_ge(a_rd, n + 1)
                        V.tensor_tensor(Pr[:, k, :, :], Pr[:, k, :, :], bcast(rden[:, k, :], GQ, P),
                                        ALU.mult).then_inc(a_pr, 1)
                    elif what == "ptc":
                        eng.wait_ge(a_pt, n + 1)
                        if n:
                            eng.wait_ge(a_pv, n)
                        V.tensor_tensor(ptc[:, :, :], pt[:, :, :], tri[:, :].unsqueeze(1).broadcast_to([P, GQ, P]),
                                        ALU.mult).then_inc(a_ptc, 1)
                    elif what == "ol":
                        g, b_ = att_step(n)
                        o = (g % 2) * HD
                        tl = slice((g // 2) * GQ, (g // 2) * GQ + GQ)
                        tok = slice(b_ * P, (b_ + 1) * P)
                        eng.wait_ge(a_oh, n + 1)
                        V.tensor_tensor(a_lo[o:o + HD, tl, tok], PS[o:o + HD, 7, :].rearrange("p (j q) -> p j q", j=GQ),
                                        f32(a_hi[o:o + HD, tl, tok]), ALU.subtract).then_inc(a_ol, 1)
                    elif what == "dec":
                        eng.wait_ge(d_ab[n % 3], 16 * (n // 3 + 1))
                        if n:
                            eng.wait_ge(d_ddt, n)
                        V.tensor_tensor(dd8, ag[:, :, P - 1], nacs[:, cc, hs], ALU.add).then_inc(d_dd, 1)
                        eng.wait_ge(d_de, n + 1)
                        if n >= 2:
                            eng.wait_ge(d_xcd, n - 1)
                        V.tensor_tensor(ddt[:, n % 2, :], dd8, dt[:, cc, hs], ALU.mult).then_inc(d_ddt, 1)
                    elif what == "xdt":
                        eng.wait_ge(d_x, n + 1)
                        if n:
                            eng.wait_ge(d_mm, n)
                        xv = PS[:, 2, :].rearrange("p (h q) -> p h q", h=HG)
                        V.tensor_tensor(xc[:, :].rearrange("p (h q) -> p h q", h=HG), xv,
                                        bcast(dt[:, cc, hs], HG, HD), ALU.mult).then_inc(d_xc, 1)
                        eng.wait_ge(d_ddt, n + 1)
                        V.tensor_tensor(xcd[:, :].rearrange("p (h q) -> p h q", h=HG), xv,
                                        bcast(ddt[:, n % 2, :], HG, HD), ALU.mult).then_inc(d_xcd, 1)
                    elif what == "m":
                        eng.wait_ge(d_bcs, n + 1)
                        if n:
                            eng.wait_ge(d_m, n)
                        V.tensor_tensor(cbm[:, :], bncb[:, P:2 * P], tri[:, :], ALU.mult).then_inc(d_cbm, 1)
                        eng.wait_ge(d_cbm, n + 1)
                        eng.wait_ge(d_exp, n + 1)
                        V.tensor_tensor(ag, ag, cbm[:, :].unsqueeze(1).broadcast_to([P, HG, P]), ALU.mult).then_inc(d_m, 1)
                    elif what == "state":
                        eng.wait_ge(d_mm, n + 1)
                        sv = st[:, :].rearrange("p (h q) -> p h q", h=HG)
                        if cc == 0:
                            V.tensor_copy(st[:, :], PS[:, 6, :]).then_inc(d_stp, 1)
                        elif cc < NT - 1:
                            V.tensor_tensor(sv, sv, bcast(cdec[:, n % 2, :], HG, HD), ALU.mult).then_inc(d_stm, 1)
                            n_stm += 1
                            eng.wait_ge(d_stm, n_stm)
                            V.tensor_tensor(st[:, :], st[:, :], PS[:, 6, :], ALU.add).then_inc(d_stp, 1)
                    elif what == "y":
                        yv = yo[:, :].rearrange("p (i l) -> p i l", i=TG)
                        dg = PS[:, 5, :].rearrange("p (i l) -> p i l", i=TG)
                        xsv = xs[:, TG * g:TG * g + TG, cc * P:(cc + 1) * P]
                        szv = sz[:, TG * g:TG * g + TG, cc * P:(cc + 1) * P]
                        eng.wait_ge(d_dxs, n + 1)
                        if n:
                            eng.wait_ge(d_s1, n)
                        if cc:
                            eng.wait_ge(d_e2x, n + 1)
                            V.tensor_tensor(yv, PS[:, 4, :].rearrange("p (i l) -> p i l", i=TG),
                                            e2[:, :, :], ALU.mult).then_inc(d_yo, 1)
                            n_yo += 1
                            eng.wait_ge(d_yo, n_yo)
                            V.tensor_tensor(yv, yv, xsv, ALU.add).then_inc(d_yx, 1)
                            n_yx += 1
                            eng.wait_ge(d_yx, n_yx)
                            V.tensor_tensor(yv, yv, dg, ALU.add).then_inc(d_yd, 1)
                        else:
                            eng.wait_ge(d_e2x, n + 1)
                            V.tensor_tensor(yv, xsv, dg, ALU.add).then_inc(d_yd, 1)
                        eng.wait_ge(d_yd, n + 1)
                        V.scalar_tensor_tensor(out=szv, in0=yv, scalar=0.5, in1=szv,
                                               op0=ALU.mult, op1=ALU.mult).then_inc(d_y, 1)

            norm_scale(0, 0, xnat, sd, rs, xsc, n1row)
            for t in range(NT):
                if t + 1 < NT:
                    norm_scale(t + 1, t + 1, xnat, sd, rs, xsc, n1row)
                if t == 0:
                    split(0)
                if t == NT - 1:
                    split(1)
                norm_lo(t, t, xn_hi, xn_lo)
            k_conv = k_z = n_sp = 0
            for c, (kind, i) in enumerate(CHUNKS):
                if 1 < c + 1 < len(CHUNKS) and c not in (AT[("out", 3)], AT[("up", 0)]):
                    split(c + 1)
                if kind == "vd" and i == 1:
                    for t in range(NT):
                        eng.wait_ge(gemm_done, DONE[c, t])
                        V.tensor_copy(v[:, t, :], PS[:, t, 0:HKV * HD]).then_inc(v_ready, 1)
                        if t == 0:
                            eng.wait_ge(params_in, 16 * len(PARAM_ROWS))
                        V.tensor_tensor(dtr[:, t, :], PS[:, t, HKV * HD:VW], dtb[:, :],
                                        ALU.add).then_inc(v_ready, 1)
                    eng.wait_ge(pcols_t, 3)
                    for k, n in enumerate(PARAM_SIZES):
                        V.tensor_copy(pcol[:, k, 0:n], PS[:, 4 + k, 0:n]).then_inc(pcols, 1)
                    eng.wait_ge(pcols, 3)
                    V.tensor_scalar(cwh[:, 0:5 * NX], pcol[:, 0, 0:5 * NX], 0.5, None, ALU.mult).then_inc(pcols, 1)
                    V.tensor_scalar(bgh[:, :], pcol[:, 1, bg0:bg0 + 16], 0.5, None, ALU.mult).then_inc(pcols, 1)
                    for k in range(4):
                        o = (k % 2) * 2 * FT + FT
                        V.tensor_scalar(fwh[:, k, :], pcol[:, 1 + k // 2, o:o + FT], 0.5, None, ALU.mult).then_inc(pcols, 1)
                    for hh in range(2):
                        V.tensor_copy(dsk[hh * HD:(hh + 1) * HD, :], dskb[hh * HD:(hh + 1) * HD, hh:NH:2]).then_inc(pcols, 1)
                    X = dtr[:, :, :].rearrange("p t h -> p (t h)")
                    e, z, w, pl, r, q_ = (s_[:, :] for s_ in sp)
                    eng.wait_ge(v_ready, 2 * NT)
                    V.tensor_scalar(q_, X, -1.0, None, ALU.mult).then_inc(spd, 1)
                    eng.wait_ge(spd, 1)
                    V.tensor_tensor(e, X, q_, ALU.max).then_inc(spc, 1)
                    eng.wait_ge(spa, 2)

                    def chained(ins):
                        nonlocal n_sp
                        n_sp += 1
                        ins.then_inc(spd, 1)
                        eng.wait_ge(spd, n_sp + 1)

                    chained(V.tensor_scalar(r, e, 2.0, None, ALU.add))
                    chained(V.reciprocal(r, r))
                    chained(V.tensor_tensor(z, e, r, ALU.mult))
                    chained(V.tensor_tensor(w, z, z, ALU.mult))
                    chained(V.tensor_scalar(pl, w, 1.0 / 17, 1.0 / 15, ALU.mult, ALU.add))
                    for k in (13, 11, 9, 7, 5, 3, 1):
                        chained(V.tensor_tensor(pl, pl, w, ALU.mult))
                        chained(V.tensor_scalar(pl, pl, 1.0 / k, None, ALU.add))
                    chained(V.scalar_tensor_tensor(out=pl, in0=z, scalar=2.0, in1=pl, op0=ALU.mult, op1=ALU.mult))
                    chained(V.tensor_scalar(r, X, 0.0, None, ALU.max))
                    chained(V.tensor_tensor(dt[:, :, :].rearrange("p t h -> p (t h)"), r, pl, ALU.add))
                    V.scalar_tensor_tensor(out=q_.rearrange("p (t h) -> p t h", t=NT), in0=dt[:, :, :], scalar=-1.0,
                                           in1=nA[:, :].unsqueeze(1).broadcast_to([P, NT, NH]),
                                           op0=ALU.mult, op1=ALU.mult).then_inc(da_ready, 1)
                if kind == "down" and i == 9:
                    eng.wait_ge(f_sq, NT)
                    V.tensor_scalar(fhb, fhs, 1.0 / D, EPS, ALU.mult, ALU.add).then_inc(f_bias, 1)
                if kind in FORM_B and kind != "vd":
                    add, nh, last = (h_add, i // 2, i % 2 == 1) if kind == "out" else (dn_add, i // 6, i % 6 == 5)
                    if last:
                        for t in range(NT):
                            eng.wait_ge(gemm_done, DONE[c, t])
                            if kind == "out" and nh == 0 and t == 0:
                                eng.wait_ge(h_in, 16)
                            hv = h[:, t, nh * 512:nh * 512 + 512]
                            V.tensor_tensor(hv, hv, PS[:, (4, 0)[nh] + t, :], ALU.add).then_inc(add, 1)
                            if kind == "out" and nh == 1:
                                if t == NT - 1:
                                    norm_scale(t, NT + t, h, hsd, hrs, hsc, n2row)
                                    split(c + 2)
                                if t:
                                    norm_lo(t - 1, NT + t - 1, hn_hi, hn_lo)
                                if t < NT - 1:
                                    norm_scale(t, NT + t, h, hsd, hrs, hsc, n2row)
                                if t == NT - 2:
                                    split(c + 1)
                            if kind == "down" and nh == 1 and t:
                                final_tile(t - 1)
                        if kind == "out" and nh == 1:
                            norm_lo(NT - 1, 2 * NT - 1, hn_hi, hn_lo)
                    continue
                for u in range(2):
                    rides(c, u, 0)
                    if kind not in ("bc", "xs"):
                        rides(c, u, 1)
                    b = PS[:, u, :]
                    if kind in ("bc", "xs"):
                        t = 2 * i + u + (16 if kind == "bc" else 0)
                        acc = cacc[:, u, :]
                        eng.wait_ge(c_acc, k_conv + 1)
                        for back in (1, 2, 3):
                            if back > 1:
                                eng.wait_ge(c_tap, 3 * k_conv + back - 1)
                            V.scalar_tensor_tensor(out=acc[:, back:SEQ], in0=b[:, 0:SEQ - back], scalar=CW(3 - back, t),
                                                   in1=acc[:, back:SEQ], op0=ALU.mult, op1=ALU.add).then_inc(c_tap, 1)
                        rides(c, u, 1)
                        eng.wait_ge(c_tanh, k_conv + 1)
                        dst = bc[:, t - 16, :] if kind == "bc" else xs[:, t, :]
                        V.scalar_tensor_tensor(out=dst, in0=cth[:, u, :], scalar=1.0, in1=acc,
                                               op0=ALU.add, op1=ALU.mult).then_inc(c_out, 1)
                        k_conv += 1
                    elif kind == "z":
                        eng.wait_ge(z_tanh, k_z + 1)
                        if k_z == 0:
                            eng.wait_ge(acs_out, 16)
                        V.scalar_tensor_tensor(out=sz[:, 2 * i + u, :], in0=cth[:, u, :], scalar=1.0, in1=b,
                                               op0=ALU.add, op1=ALU.mult).then_inc(z_out, 1)
                        k_z += 1
                    elif kind == "ao":
                        eng.wait_ge(gemm_done, DONE[c, u])
                        eng.wait_ge(g_tanh, 2 * i + u + 1)
                        if i:
                            eng.wait_ge(ao_sp[u], 16 * i)
                        V.scalar_tensor_tensor(out=cacc[:, u, :], in0=cth[:, u, :], scalar=1.0, in1=b,
                                               op0=ALU.add, op1=ALU.mult).then_inc(ao_out, 1)
                    elif kind == "so" and i[1] == 1:
                        f = 2 * i[0] + u
                        eng.wait_ge(gemm_done, DONE[c, u])
                        eng.wait_ge(so_in[u], 32 * (i[0] + 1))
                        V.scalar_tensor_tensor(out=cth[:, u, :], in0=cth[:, u, :], scalar=1.0,
                                               in1=PS[:, 2 * (i[0] % 2) + u, :], op0=ALU.add, op1=ALU.mult).then_inc(so_g, 1)
                        eng.wait_ge(so_g, f + 1)
                        V.tensor_tensor(cacc[:, u, :], cacc[:, u, :], cth[:, u, :], ALU.add).then_inc(so_a, 1)
                        eng.wait_ge(so_hi, f + 1)
                        V.scalar_tensor_tensor(out=mix_lo[:, f, :], in0=cacc[:, u, :], scalar=0.5, in1=f32(mix_hi[:, f, :]),
                                               op0=ALU.mult, op1=ALU.subtract).then_inc(so_lo, 1)
                    elif kind == "up":
                        k, it = 2 * i + u, i // 2
                        t = (i % 2) * FT + 2 * it + u
                        acc = ga2[:, u, :] if i % 2 else cacc[:, u, :]
                        eng.wait_ge(u_acc, k + 1)
                        for back in (1, 2):
                            if back > 1:
                                eng.wait_ge(u_tap, 2 * k + 1)
                            V.scalar_tensor_tensor(out=acc[:, back:SEQ], in0=PS[:, 2 * (i % 2) + u, 0:SEQ - back],
                                                   scalar=FW(2 - back, t), in1=acc[:, back:SEQ],
                                                   op0=ALU.mult, op1=ALU.add).then_inc(u_tap, 1)
                        if i % 2:
                            f = 2 * it + u
                            eng.wait_ge(u_tanh, f + 1)
                            V.scalar_tensor_tensor(out=acc, in0=cth[:, u, :], scalar=1.0, in1=acc,
                                                   op0=ALU.add, op1=ALU.mult).then_inc(u_silu, 1)
                            eng.wait_ge(u_silu, f + 1)
                            V.tensor_tensor(acc, acc, cacc[:, u, :], ALU.mult).then_inc(u_mul, 1)
                            eng.wait_ge(u_hi, f + 1)
                            V.tensor_tensor(act_lo[:, f, :], acc, f32(act_hi[:, f, :]), ALU.subtract).then_inc(u_lo, 1)
                    rides(c, u, 2)
            final_tile(NT - 1)

        @block.tensor
        def _(eng):
            T = nc.tensor
            freed_by = {}

            def take(b, sem_, value):
                if b in freed_by:
                    eng.wait_ge(*freed_by[b])
                freed_by[b] = (sem_, value)

            def three(out_, w, m, first, last):
                T.matmul(out_, w[0], m[0], start=first, stop=False)
                T.matmul(out_, w[0], m[1], start=False, stop=False)
                return T.matmul(out_, w[1], m[0], start=False, stop=last)

            def norm_transposes(t, k, src):
                b = 4 + 2 * (t % 2)
                if k == 0:
                    eng.wait_ge(consts, 11)
                eng.wait_ge(n_sc, k + 1)
                for hf in range(2):
                    take(b + hf, n_lo, 2 * k + hf + 1)
                    for j in range(4):
                        kt = 4 * hf + j
                        ins = T.transpose(PS[:, b + hf, j * P:(j + 1) * P], src[:, t % 2, kt * P:(kt + 1) * P], ident[:, :])
                    ins.then_inc(n_tp, 1)

            def rides(c, u, slot):
                for n, what in rides_at("PE", c, u, slot):
                    if what == "acs" and n == -2:
                        eng.wait_ge(da_ready, 1)
                        take(2, acs_ev, 1)
                        for t in range(NT):
                            ins = T.matmul(PS[0:NH, 2, t * P:(t + 1) * P], sp[5][:, t * NH:(t + 1) * NH], tri[:, :],
                                           start=True, stop=True)
                        ins.then_inc(acs_mm, 1)
                    if what == "acs" and n == -1:
                        eng.wait_ge(acs_ev, 1)
                        take(3, acs_nat, 1)
                        for t in range(NT):
                            ins = T.transpose(PS[:, 3, t * NH:(t + 1) * NH], acsT[:, t * P:(t + 1) * P],
                                              ident[0:NH, 0:NH])
                        ins.then_inc(acs_tp, 1)
                    if what == "scores":
                        g, b_ = att_step(n)
                        o = (g % 2) * HD
                        if n % 8 == 0:
                            eng.wait_ge(qk_ready, 6 + n // 2)
                        for q_ in range(2):
                            take(2 + 2 * (n % 2) + q_, a_sel, n + 1)
                        for j in range(GQ):
                            bank = PS[:, 2 + 2 * (n % 2) + j // 2, :]
                            c0 = (j % 2) * 2 * P + (0 if b_ else P)
                            k0_ = max(b_ - 1, 0) * P
                            ins = T.matmul(bank[:, c0:(j % 2 + 1) * 2 * P],
                                           qT[o:o + HD, (g // 2) * GQ + j, b_ * P:(b_ + 1) * P],
                                           kT[o:o + HD, g // 2, k0_:(b_ + 1) * P], start=True, stop=True)
                        ins.then_inc(a_sc, 1)
                    if what == "probs_t":
                        k = n
                        eng.wait_ge(a_pr, k + 1)
                        take(6, a_pt, k + 1)
                        for j in range(GQ):
                            ins = T.transpose(PS[:, 6, j * P:(j + 1) * P], Pr[:, k % 2, j, :], ident[:, :])
                        ins.then_inc(a_tp, 1)
                    if what == "values":
                        k = n
                        g, b_ = att_step(k)
                        o = (g % 2) * HD
                        eng.wait_ge(a_ptc, k + 1)
                        eng.wait_ge(a_ptp, k + 1)
                        take(7, a_ol, k + 1)
                        if b_:
                            T.matmul(PS[o:o + HD, 7, :], v[:, b_ - 1, g * HD:(g + 1) * HD],
                                     ptp[:, :, :].rearrange("p j q -> p (j q)"), start=True, stop=False)
                        T.matmul(PS[o:o + HD, 7, :], v[:, b_, g * HD:(g + 1) * HD],
                                 ptc[:, :, :].rearrange("p j q -> p (j q)"), start=b_ == 0, stop=True).then_inc(a_pv, 1)
                    if what == "acs":
                        continue
                    g, cc = n // NT, n % NT
                    tok = slice(cc * P, (cc + 1) * P)
                    if what == "s1":
                        eng.wait_ge(c_out, 8 + 4 * (g + 1))
                        take(2, d_xcd, n + 1)
                        for t in range(TG):
                            ins = T.transpose(PS[:, 2, t * P:(t + 1) * P], xs[:, TG * g + t, tok], ident[:, :])
                        ins.then_inc(d_x, 1)
                        take(3, d_bcs, n + 1)
                        T.transpose(PS[:, 3, 0:P], bc[:, g, tok], ident[:, :])
                        T.matmul(PS[:, 3, P:2 * P], bc[:, g, tok], bc[:, NG + g, tok], start=True,
                                 stop=True).then_inc(d_bc, 1)
                    if what == "s2":
                        k = n
                        ag, xc, xcd = ag_of[n // 8], xc_of[n // 8], xcd_of[n // 8]
                        if cc < NT - 1:
                            eng.wait_ge(d_xcd, k + 1)
                            eng.wait_ge(d_bcs, k + 1)
                            take(6, d_stp, (NT - 1) * g + cc + 1)
                            T.matmul(PS[:, 6, :], bncb[:, 0:P], xcd[:, :], start=True, stop=True)
                        if cc:
                            eng.wait_ge(d_stp, (NT - 1) * g + cc)
                            take(4, d_yd, k + 1)
                            for t in range(TG):
                                T.matmul(PS[:, 4, t * P:(t + 1) * P], st[:, t * P:(t + 1) * P],
                                         bc[:, NG + g, tok], start=True, stop=True)
                        eng.wait_ge(d_m, k + 1)
                        eng.wait_ge(d_xc, k + 1)
                        take(5, d_yd, k + 1)
                        for hd in range(HG):
                            o = (hd % 2) * HD
                            ins = T.matmul(PS[o:o + HD, 5, (hd // 2) * P:(hd // 2 + 1) * P],
                                           xc[:, hd * HD:(hd + 1) * HD], ag[:, k % 3, hd, :],
                                           start=True, stop=True)
                        ins.then_inc(d_mm, 1)
                    if what == "sum":
                        k = n
                        eng.wait_ge(d_s2, k + 1)
                        if cc == 0:
                            take(7, g_sd, g + 1)
                        T.matmul(PS[:, 7, cc * P:(cc + 1) * P], ones[:, :], sq2[:, :], start=True,
                                 stop=True).then_inc(d_sum, 1)

            def unit(c, u, b, k0, mh, ml, first, last, tok):
                kind = CHUNKS[c][0]
                for kt in range(KT):
                    if kt == KT // 2:
                        rides(c, u, 0)
                    if u == 0 and tok.start == 0 and kt in (0, KT // 2):
                        eng.wait_ge(w_split, 2 * c + 1 + (kt > 0))
                    if kind == "so" and (k0 + kt) % TG == 0:
                        eng.wait_ge(g_lo, k0 + kt + TG)
                    w_ = slice(kt * 256 + u * P, kt * 256 + (u + 1) * P)
                    ins = three(PS[:, b, tok], (whi[:, c % 2, w_], wlo[:, c % 2, w_]),
                                (mh[:, k0 + kt, tok], ml[:, k0 + kt, tok]), first and kt == 0, last and kt == KT - 1)
                return ins

            norm_transposes(0, 0, xsc)
            norm_transposes(1, 1, xsc)
            k_conv = k_z = 0
            for c, (kind, i) in enumerate(CHUNKS):
                half = tiles_in(c)[0] // 2
                if (kind, i) == ("out", 2):
                    continue
                if kind in FORM_B:
                    if kind == "vd":
                        nk, width, k0, first, last = 4, VW, 4 * i, i == 0, i == 1
                        mh, ml, b0 = xn_hi, xn_lo, 0
                        took, per = v_ready, 2
                    elif kind == "out":
                        nk, width, k0, first, last = 4, 512, 4 * (i % 2), i != 1, i % 2 == 1
                        mh, ml, b0 = mix_hi, mix_lo, (4, 0)[i // 2]
                        took, per = h_add, 1
                        if i < 2:
                            eng.wait_ge(so_lo, k0 + 4)
                    else:
                        k0, nk = down_tiles(i)
                        width, first, last = 512, i % 6 == 0, i % 6 == 5
                        mh, ml, b0 = act_hi, act_lo, (4, 0)[i // 6]
                        took, per = dn_add, 1
                        eng.wait_ge(u_lo, k0 + nk)
                    nth = {"vd": 0, "out": i // 2, "down": i // 6}[kind]
                    cs = (c - 1, c) if (kind, i) == ("out", 3) else (c,)
                    for t in range(NT):
                        if kind == "vd" and first:
                            if 0 < t < NT - 1:
                                norm_transposes(t + 1, t + 1, xsc)
                            eng.wait_ge(n_lo, 2 * t + 2)
                        if first:
                            take(b0 + t, took, per * (NT * nth + t + 1))
                        for ck in cs:
                            kb = k0 - 4 * (c - ck)
                            tok = slice(t * P, (t + 1) * P)
                            for kt in range(nk):
                                if t == 0 and kt in (0, half):
                                    eng.wait_ge(w_split, 2 * ck + 1 + (kt > 0))
                                cols_ = slice(kt * width, (kt + 1) * width)
                                ins = three(PS[:, b0 + t, 0:width], (mh[:, kb + kt, tok], ml[:, kb + kt, tok]),
                                            (whi[:, ck % 2, cols_], wlo[:, ck % 2, cols_]),
                                            first and ck == cs[0] and kt == 0, last and ck == c and kt == nk - 1)
                            ins.then_inc(gemm_done, 1)
                        if len(cs) == 2 and t:
                            norm_transposes(t - 1, NT + t - 1, hsc)
                    if kind == "vd" and last:
                        eng.wait_ge(params_in, 16 * len(PARAM_ROWS))
                        for k, n in enumerate(PARAM_SIZES):
                            take(4 + k, pcols, 3)
                            T.transpose(PS[:, 4 + k, 0:n], stage[0:n, k, :], ident[0:n, 0:n]).then_inc(pcols_t, 1)
                    continue
                for u in range(2):
                    b, k0, first, last = u, 0, True, True
                    mh, ml = xn_hi, xn_lo
                    if kind == "k":
                        take(b, qk_ready, u + 1)
                    elif kind == "q":
                        take(b, qk_ready, 2 + 2 * i + u + 1)
                    elif kind in ("bc", "xs"):
                        k_conv += 1
                        take(b, c_tap, 3 * k_conv)
                    elif kind == "z":
                        k_z += 1
                        take(b, z_out, k_z)
                    elif kind == "ga":
                        take(b, g_tanh, 2 * i + u + 1)
                    elif kind == "ao":
                        take(b, ao_out, 2 * i + u + 1)
                        mh, ml = a_hi, a_lo
                        if i == 0 and u == 0:
                            eng.wait_ge(a_ol, N_ATT)
                    elif kind == "gs":
                        take(b, gs_tanh, 2 * i + u + 1)
                    elif kind == "so":
                        b = 2 * (i[0] % 2) + u
                        mh, ml, k0 = y_hi, y_lo, KT * i[1]
                        first, last = i[1] == 0, i[1] == 1
                        if first:
                            take(b, so_g, 2 * i[0] + u + 1)
                    elif kind == "up":
                        b = 2 * (i % 2) + u
                        if i >= 2 or i == u == 0:
                            take(b, u_tap, 2 * (2 * i + u) + 2)
                        mh, ml = hn_hi, hn_lo
                    if kind == "up" and i < 2:
                        if i == 0 and u == 0:
                            for cu in range(4):
                                if cu == 0:
                                    eng.wait_ge(n_lo, 2 * (NT + 2))
                                if cu == 1:
                                    norm_transposes(NT - 1, 2 * NT - 1, hsc)
                                if cu >= 1:
                                    take(cu, u_tap, 2 * cu + 2)
                                ins = unit(c + cu // 2, cu % 2, cu, 0, mh, ml, True, True, slice(0, SEQ // 2))
                            eng.wait_ge(n_lo, 4 * NT)
                        unit(c, u, b, 0, mh, ml, True, True, slice(SEQ // 2, SEQ)).then_inc(gemm_done, 1)
                        continue
                    unit(c, u, b, k0, mh, ml, first, last, slice(0, SEQ)).then_inc(gemm_done, 1)
                    rides(c, u, 1)


_INS = ["x", "norm1_w", "w_in", "b_gate", "attn_sinks", "w_attn_o", "ssd_conv_w", "ssd_conv_b", "dt_bias",
        "a_log", "d_skip", "ssd_norm_w", "w_ssd_o", "w_out", "norm2_w", "w_up", "ffn_conv_w", "ffn_conv_b",
        "w_down", "final_norm_w"]


def kernel(**inputs):
    import numpy as _np
    import concourse.bacc as _bacc
    from concourse import mybir as _mybir
    from concourse.bass_utils import run_bass_kernel_spmd as _run

    nc = _bacc.Bacc("TRN2", target_bir_lowering=False, num_devices=1)
    arrays, args = {}, []
    for name in _INS:
        a = _np.ascontiguousarray(inputs[name])
        arrays[f"in_{name}"] = a
        args.append(nc.dram_tensor(f"in_{name}", a.shape, _mybir.dt.from_np(a.dtype), kind="ExternalInput").ap())
    out = nc.dram_tensor("out_0", (1, SEQ, D), F32, kind="ExternalOutput").ap()
    hybrid_layer(nc, *args, out)
    r = _run(nc, [arrays], core_ids=[0])
    return r.results[0]["out_0"]
```
